# Optimizing a Trainium2 kernel written in Bass

```python
import jax
import jax.numpy as jnp
from jax import lax
import numpy as np
import math
import jax, jax.numpy as jnp

D_MODEL = 1024
BATCH = 1
SEQ = 512
DEPTH = 1

GRID_W = 64
N_MEM = 256
HEAD_DIM = 64
NA_HEADS = 6
NA_WIDTH = NA_HEADS * HEAD_DIM
NA_WIN_ROWS = 8
NA_WIN_COLS = 16
RW_HEADS = 6
RW_WIDTH = RW_HEADS * HEAD_DIM
DECAY_LORA = 64
AAA_LORA = 64
GATE_LORA = 128
MEM_HEADS = 4
MEM_WIDTH = MEM_HEADS * HEAD_DIM
N_BRANCH = 3
N_EXPERTS = 16
EC_CAPACITY = 2
EXPERT_FF = 2 * D_MODEL
RMS_EPS = 1e-6
GN_EPS = 64e-5
IN_WIDTHS = (NA_WIDTH, NA_WIDTH, NA_WIDTH, RW_WIDTH, RW_WIDTH, RW_WIDTH, DECAY_LORA, AAA_LORA, GATE_LORA, MEM_WIDTH, D_MODEL, D_MODEL, D_MODEL)
D_IN = sum(IN_WIDTHS)


def rms_norm(x, g):
    xf = x.astype(jnp.float32)
    y = xf * lax.rsqrt(jnp.mean(xf * xf, axis=-1, keepdims=True) + RMS_EPS)
    return (y * g.astype(jnp.float32)).astype(x.dtype)

def split_columns(p):
    cuts = []
    acc = 0
    for w in IN_WIDTHS[:-1]:
        acc += w
        cuts.append(acc)
    return jnp.split(p, cuts, axis=-1)

def to_heads(t, n_heads):
    b, s, c = t.shape
    return t.reshape(b, s, n_heads, c // n_heads)

def neighborhood_attention(q, k, v, rpb):
    b, s, h, dh = q.shape
    rows = s // GRID_W
    kr = min(NA_WIN_ROWS, rows)
    kc = NA_WIN_COLS
    q = (q * (dh ** -0.5)).reshape(b, rows, GRID_W, h, dh).transpose(1, 0, 2, 3, 4)
    k = k.reshape(b, rows, GRID_W, h, dh)
    v = v.reshape(b, rows, GRID_W, h, dh)
    col = jnp.arange(GRID_W)
    col_start = jnp.clip(col - kc // 2, 0, GRID_W - kc)
    col_idx = col_start[:, None] + jnp.arange(kc)[None, :]
    col_off = col_idx - col[:, None] + (NA_WIN_COLS - 1)

    def row_block(args):
        r, q_r = args
        r_start = jnp.clip(r - kr // 2, 0, rows - kr)
        k_win = lax.dynamic_slice_in_dim(k, r_start, kr, axis=1)[:, :, col_idx]
        v_win = lax.dynamic_slice_in_dim(v, r_start, kr, axis=1)[:, :, col_idx]
        row_off = r_start + jnp.arange(kr) - r + (NA_WIN_ROWS - 1)
        bias = rpb[:, row_off[:, None, None], col_off[None, :, :]].transpose(0, 2, 1, 3)
        scores = jnp.einsum('bwhd,biwjhd->bhwij', q_r, k_win).astype(jnp.float32) + bias.astype(jnp.float32)[None]
        probs = jax.nn.softmax(scores.reshape(b, h, GRID_W, kr * kc), axis=-1).reshape(b, h, GRID_W, kr, kc)
        return jnp.einsum('bhwij,biwjhd->bwhd', probs.astype(v.dtype), v_win)

    out = lax.map(row_block, (jnp.arange(rows), q))
    return out.transpose(1, 0, 2, 3, 4).reshape(b, s, h * dh)

def token_shift(t, direction):
    if direction == 0:
        return jnp.pad(t[:, :-1], ((0, 0), (1, 0), (0, 0)))
    return jnp.pad(t[:, 1:], ((0, 0), (0, 1), (0, 0)))

def wkv7_scan(r, w, k, v, a, b, reverse):
    bsz, _, h, n = r.shape

    def step(state, inp):
        r_t, w_t, k_t, v_t, a_t, b_t = inp
        sa = jnp.einsum('bhvk,bhk->bhv', state, a_t)
        state = state * w_t[:, :, None, :] + sa[..., None] * b_t[:, :, None, :] + v_t[..., None] * k_t[:, :, None, :]
        return state, jnp.einsum('bhvk,bhk->bhv', state, r_t)

    xs = tuple(t.transpose(1, 0, 2, 3) for t in (r, w, k, v, a, b))
    _, y = lax.scan(step, jnp.zeros((bsz, h, n, n), jnp.float32), xs, reverse=reverse)
    return y.transpose(1, 0, 2, 3)

def rwkv7_bidirectional(p_r, p_k, p_v, lat_w, lat_a, lat_g, mu_rkv, mu_w, mu_a, w0, w2, a0, a2, k_k, k_a, r_k, g2, ln_g, ln_b):
    out_dtype = p_r.dtype
    f32 = lambda t: t.astype(jnp.float32)
    p_r, p_k, p_v, lat_w, lat_a, lat_g = (f32(t) for t in (p_r, p_k, p_v, lat_w, lat_a, lat_g))
    mu_rkv, mu_w, mu_a, w0, w2, a0, a2 = (f32(t) for t in (mu_rkv, mu_w, mu_a, w0, w2, a0, a2))
    k_k, k_a, r_k, g2, ln_g, ln_b = (f32(t) for t in (k_k, k_a, r_k, g2, ln_g, ln_b))
    bsz, s, c = p_r.shape
    y_sum = jnp.zeros((bsz, s, RW_HEADS, HEAD_DIM), jnp.float32)
    bonus_sum = jnp.zeros((bsz, s, RW_HEADS, HEAD_DIM), jnp.float32)
    for d in range(2):
        def mix(t, mu):
            return t + (token_shift(t, d) - t) * mu
        r = mix(p_r, mu_rkv[d, 0])
        k = mix(p_k, mu_rkv[d, 1])
        v = mix(p_v, mu_rkv[d, 2])
        w_log = -jax.nn.softplus(-(w0[d] + jnp.tanh(mix(lat_w, mu_w[d])) @ w2[d])) - 0.5
        decay = jnp.exp(-jnp.exp(w_log))
        a = jax.nn.sigmoid(a0[d] + mix(lat_a, mu_a[d]) @ a2[d])
        kk = to_heads(k * k_k, RW_HEADS)
        kk = kk / jnp.maximum(jnp.sqrt(jnp.sum(kk * kk, axis=-1, keepdims=True)), 1e-12)
        k = k * (1.0 + (a - 1.0) * k_a)
        rh, kh, vh, ah = (to_heads(t, RW_HEADS) for t in (r, k, v, a))
        y_sum = y_sum + wkv7_scan(rh, to_heads(decay, RW_HEADS), kh, vh, -kk, kk * ah, reverse=(d == 1))
        bonus_sum = bonus_sum + jnp.sum(rh * kh * r_k, axis=-1, keepdims=True) * vh
    mean = jnp.mean(y_sum, axis=-1, keepdims=True)
    var = jnp.mean(jnp.square(y_sum - mean), axis=-1, keepdims=True)
    y = ((y_sum - mean) * lax.rsqrt(var + GN_EPS)).reshape(bsz, s, c) * ln_g + ln_b
    y = y + bonus_sum.reshape(bsz, s, c)
    g = jax.nn.sigmoid(lat_g) @ g2
    return (y * g).astype(out_dtype)

def memory_attention(q, mem_h, w_mem_kv):
    b, s, _ = q.shape
    mk, mv = jnp.split(mem_h @ w_mem_kv, 2, axis=-1)
    qh = to_heads(q, MEM_HEADS) * (HEAD_DIM ** -0.5)
    kh = to_heads(mk, MEM_HEADS)
    vh = to_heads(mv, MEM_HEADS)
    scores = jnp.einsum('bshd,bmhd->bhsm', qh, kh).astype(jnp.float32)
    probs = jax.nn.softmax(scores, axis=-1)
    return jnp.einsum('bhsm,bmhd->bshd', probs.astype(vh.dtype), vh).reshape(b, s, MEM_WIDTH)

def expert_choice_ffn(h, w_router, w_gate, w_up, w_down):
    b, s, d = h.shape
    cap = EC_CAPACITY * s // N_EXPERTS
    affinity = jax.nn.softmax((h @ w_router).astype(jnp.float32), axis=-1)
    top_val, top_idx = lax.top_k(affinity.transpose(0, 2, 1), cap)
    xe = jax.vmap(lambda hb, ib: hb[ib])(h, top_idx)
    act = jax.nn.silu(jnp.einsum('becd,edf->becf', xe, w_gate)) * jnp.einsum('becd,edf->becf', xe, w_up)
    ye = jnp.einsum('becf,efd->becd', act, w_down) * top_val[..., None].astype(h.dtype)
    return jax.vmap(lambda yb, ib: jnp.zeros((s, d), yb.dtype).at[ib.reshape(-1)].add(yb.reshape(-1, d)))(ye, top_idx)

def first_inputs(seed: int = 0) -> dict:
    key = jax.random.key(seed)
    ks = iter(jax.random.split(key, 40))
    L = DEPTH

    def nrm(shape, scale):
        return scale * jax.random.normal(next(ks), shape, jnp.float32)

    def uni(shape):
        return jax.random.uniform(next(ks), shape, jnp.float32, 0.0, 1.0)

    decay_ramp = jnp.linspace(-6.5, -1.5, RW_WIDTH, dtype=jnp.float32)
    return {
        'x': nrm((BATCH, SEQ, D_MODEL), 1.0),
        'mem': nrm((BATCH, N_MEM, D_MODEL), 1.0),
        'norm_mix_g': 1.0 + nrm((L, D_MODEL), 0.02),
        'norm_mem_g': 1.0 + nrm((L, D_MODEL), 0.02),
        'w_in': nrm((L, D_MODEL, D_IN), D_MODEL ** -0.5),
        'na_rpb': nrm((L, NA_HEADS, 2 * NA_WIN_ROWS - 1, 2 * NA_WIN_COLS - 1), 0.05),
        'rw_mu_rkv': uni((L, 2, 3, RW_WIDTH)),
        'rw_mu_w': uni((L, 2, DECAY_LORA)),
        'rw_mu_a': uni((L, 2, AAA_LORA)),
        'rw_w0': decay_ramp + nrm((L, 2, RW_WIDTH), 0.1),
        'rw_w2': nrm((L, 2, DECAY_LORA, RW_WIDTH), 0.1),
        'rw_a0': nrm((L, 2, RW_WIDTH), 0.1),
        'rw_a2': nrm((L, 2, AAA_LORA, RW_WIDTH), 0.1),
        'rw_k_k': 0.85 + nrm((L, RW_WIDTH), 0.02),
        'rw_k_a': 1.0 + nrm((L, RW_WIDTH), 0.02),
        'rw_r_k': nrm((L, RW_HEADS, HEAD_DIM), 0.1),
        'rw_g2': nrm((L, GATE_LORA, RW_WIDTH), GATE_LORA ** -0.5),
        'rw_ln_g': 1.0 + nrm((L, RW_WIDTH), 0.02),
        'rw_ln_b': nrm((L, RW_WIDTH), 0.02),
        'w_mem_kv': nrm((L, D_MODEL, 2 * MEM_WIDTH), D_MODEL ** -0.5),
        'w_branch_na': nrm((L, NA_WIDTH, D_MODEL), NA_WIDTH ** -0.5),
        'w_branch_rw': nrm((L, RW_WIDTH, D_MODEL), RW_WIDTH ** -0.5),
        'w_branch_mem': nrm((L, MEM_WIDTH, D_MODEL), MEM_WIDTH ** -0.5),
        'w_out': nrm((L, D_MODEL, D_MODEL), D_MODEL ** -0.5),
        'norm_ffn_g': 1.0 + nrm((L, D_MODEL), 0.02),
        'w_router': nrm((L, D_MODEL, N_EXPERTS), D_MODEL ** -0.5),
        'w_exp_gate': nrm((L, N_EXPERTS, D_MODEL, EXPERT_FF), D_MODEL ** -0.5),
        'w_exp_up': nrm((L, N_EXPERTS, D_MODEL, EXPERT_FF), D_MODEL ** -0.5),
        'w_exp_down': nrm((L, N_EXPERTS, EXPERT_FF, D_MODEL), EXPERT_FF ** -0.5),
        'norm_final_g': 1.0 + nrm((D_MODEL,), 0.02),
    }

def first_block(x, mem, norm_mix_g, norm_mem_g, w_in, na_rpb, rw_mu_rkv, rw_mu_w, rw_mu_a, rw_w0, rw_w2, rw_a0, rw_a2, rw_k_k, rw_k_a, rw_r_k, rw_g2, rw_ln_g, rw_ln_b, w_mem_kv, w_branch_na, w_branch_rw, w_branch_mem, w_out, norm_ffn_g, w_router, w_exp_gate, w_exp_up, w_exp_down, norm_final_g):
    for l in range(DEPTH):
        h = rms_norm(x, norm_mix_g[l])
        (na_q, na_k, na_v, p_r, p_k, p_v, lat_w, lat_a, lat_g, mem_q,
         gate_na, gate_rw, gate_mem) = split_columns(h @ w_in[l])
        y_na = neighborhood_attention(to_heads(na_q, NA_HEADS), to_heads(na_k, NA_HEADS), to_heads(na_v, NA_HEADS), na_rpb[l])
        y_rw = rwkv7_bidirectional(p_r, p_k, p_v, lat_w, lat_a, lat_g, rw_mu_rkv[l], rw_mu_w[l], rw_mu_a[l], rw_w0[l], rw_w2[l], rw_a0[l], rw_a2[l], rw_k_k[l], rw_k_a[l], rw_r_k[l], rw_g2[l], rw_ln_g[l], rw_ln_b[l])
        y_mem = memory_attention(mem_q, rms_norm(mem, norm_mem_g[l]), w_mem_kv[l])
        merged = (jax.nn.sigmoid(gate_na) * (y_na @ w_branch_na[l])
                  + jax.nn.sigmoid(gate_rw) * (y_rw @ w_branch_rw[l])
                  + jax.nn.sigmoid(gate_mem) * (y_mem @ w_branch_mem[l]))
        x = x + merged @ w_out[l]
        x = x + expert_choice_ffn(rms_norm(x, norm_ffn_g[l]), w_router[l], w_exp_gate[l], w_exp_up[l], w_exp_down[l])
    return rms_norm(x, norm_final_g)


CHUNK = 64
MIX_A_WIDTH = D_MODEL // 2
MIX_B_WIDTH = D_MODEL - MIX_A_WIDTH
A_GROUPS = 8
A_GROUP_DIM = MIX_A_WIDTH // A_GROUPS
A_BLOCK = 128
B_HEADS = 8
B_HEAD_DIM = MIX_B_WIDTH // B_HEADS
B_LEFT_CHUNKS = 8
B_BAND = (B_LEFT_CHUNKS + 1) * CHUNK
REL_CLIP = 128
PEER_HEADS = 8
PEER_NKEYS = 128
PEER_EXPERTS = PEER_NKEYS * PEER_NKEYS
PEER_QDIM = 256
PEER_HALF = PEER_QDIM // 2
PEER_TOPK = 16
PEER_TOKEN_BLOCK = 128
IN_COLS = 2 * MIX_A_WIDTH + 3 * MIX_B_WIDTH
EPS = 1e-6
NEG_INF = -1e30


def rms_norm_2(x, g):
    xf = x.astype(jnp.float32)
    y = xf * lax.rsqrt(jnp.mean(xf * xf, axis=-1, keepdims=True) + EPS)
    return (y * g.astype(jnp.float32)).astype(x.dtype)

def gmlp_spatial_gating(u, v, norm_g, w_s, b_s):
    bsz, s, _ = u.shape
    u = jax.nn.gelu(u)
    v = rms_norm_2(jax.nn.gelu(v), norm_g)
    nblk = s // A_BLOCK
    v = v.reshape(bsz, nblk, A_BLOCK, A_GROUPS, A_GROUP_DIM)
    pos = jnp.arange(A_BLOCK)
    mask = (pos[None, :] // CHUNK) <= (pos[:, None] // CHUNK)
    w = jnp.where(mask[None], w_s, jnp.zeros_like(w_s)).astype(v.dtype)
    sp = jnp.einsum('gij,bnjgc->bnigc', w, v) + b_s.T.astype(v.dtype)[None, None, :, :, None]
    return u * sp.reshape(bsz, s, MIX_A_WIDTH)

def banded_chunk_attention(q, k, v, q_g, k_g, rel_bias):
    bsz, s, _ = q.shape
    nc = s // CHUNK
    pad = B_LEFT_CHUNKS * CHUNK
    q = rms_norm_2(q.reshape(bsz, nc, CHUNK, B_HEADS, B_HEAD_DIM), q_g)
    k = rms_norm_2(k.reshape(bsz, s, B_HEADS, B_HEAD_DIM), k_g)
    v = v.reshape(bsz, s, B_HEADS, B_HEAD_DIM)
    padw = ((0, 0), (pad, 0), (0, 0), (0, 0))
    kp = jnp.pad(k, padw).reshape(bsz, nc + B_LEFT_CHUNKS, CHUNK, B_HEADS, B_HEAD_DIM)
    vp = jnp.pad(v, padw).reshape(bsz, nc + B_LEFT_CHUNKS, CHUNK, B_HEADS, B_HEAD_DIM)
    band_idx = jnp.arange(nc)[:, None] + jnp.arange(B_LEFT_CHUNKS + 1)[None, :]
    kb = kp[:, band_idx].reshape(bsz, nc, B_BAND, B_HEADS, B_HEAD_DIM)
    vb = vp[:, band_idx].reshape(bsz, nc, B_BAND, B_HEADS, B_HEAD_DIM)
    scores = jnp.einsum('bcihd,bcjhd->bhcij', q, kb).astype(jnp.float32) * (B_HEAD_DIM ** -0.5)
    qi = jnp.arange(CHUNK)[:, None] + pad
    kj = jnp.arange(B_BAND)[None, :]
    rel_idx = jnp.clip(qi - kj, -REL_CLIP, REL_CLIP) + REL_CLIP
    bias = rel_bias.astype(jnp.float32)[:, rel_idx]
    valid = kj >= (pad - jnp.arange(nc)[:, None] * CHUNK)
    scores = scores + bias[None, :, None]
    scores = jnp.where(valid[None, None, :, None, :], scores, NEG_INF)
    p = jax.nn.softmax(scores, axis=-1).astype(v.dtype)
    out = jnp.einsum('bhcij,bcjhd->bcihd', p, vb)
    return out.reshape(bsz, s, MIX_B_WIDTH)

def peer_ffn(x, w_query, sub_keys, expert_u, expert_v):
    bsz, s, d = x.shape
    tokens = x.reshape(-1, PEER_TOKEN_BLOCK, d)

    def block(xb):
        q = (xb @ w_query).reshape(PEER_TOKEN_BLOCK, PEER_HEADS, 2, PEER_HALF)
        sc = jnp.einsum('thpd,hpkd->thpk', q, sub_keys).astype(jnp.float32)
        s_top, i_top = lax.top_k(sc, PEER_TOPK)
        cand = s_top[:, :, 0, :, None] + s_top[:, :, 1, None, :]
        cand_idx = i_top[:, :, 0, :, None] * PEER_NKEYS + i_top[:, :, 1, None, :]
        cand = cand.reshape(PEER_TOKEN_BLOCK, PEER_HEADS, PEER_TOPK * PEER_TOPK)
        cand_idx = cand_idx.reshape(PEER_TOKEN_BLOCK, PEER_HEADS, PEER_TOPK * PEER_TOPK)
        best, pos = lax.top_k(cand, PEER_TOPK)
        eidx = jnp.take_along_axis(cand_idx, pos, axis=-1)
        g = jax.nn.softmax(best, axis=-1)
        u = jnp.take(expert_u, eidx, axis=0)
        h = jax.nn.gelu(jnp.einsum('thkd,td->thk', u, xb))
        vv = jnp.take(expert_v, eidx, axis=0)
        return jnp.einsum('thk,thkd->td', (g * h.astype(jnp.float32)).astype(xb.dtype), vv)

    return lax.map(block, tokens).reshape(bsz, s, d)

def second_inputs(seed: int = 0) -> dict:
    key = jax.random.key(seed)
    ks = jax.random.split(key, 16)
    f32 = jnp.float32
    nrm = lambda k, shape, sc: jax.random.normal(k, shape, f32) * sc
    return {
        "x": nrm(ks[0], (BATCH, SEQ, D_MODEL), 1.0),
        "ln_mix_g": 1.0 + nrm(ks[1], (DEPTH, D_MODEL), 0.02),
        "w_in": nrm(ks[2], (DEPTH, D_MODEL, IN_COLS), D_MODEL ** -0.5),
        "gmlp_norm_g": 1.0 + nrm(ks[3], (DEPTH, MIX_A_WIDTH), 0.02),
        "gmlp_w_s": nrm(ks[4], (DEPTH, A_GROUPS, A_BLOCK, A_BLOCK), A_BLOCK ** -0.5),
        "gmlp_b_s": 1.0 + nrm(ks[5], (DEPTH, A_GROUPS, A_BLOCK), 0.1),
        "q_norm_g": 1.0 + nrm(ks[6], (DEPTH, B_HEAD_DIM), 0.02),
        "k_norm_g": 1.0 + nrm(ks[7], (DEPTH, B_HEAD_DIM), 0.02),
        "rel_bias": nrm(ks[8], (DEPTH, B_HEADS, 2 * REL_CLIP + 1), 0.1),
        "w_out": nrm(ks[9], (DEPTH, D_MODEL, D_MODEL), D_MODEL ** -0.5),
        "ln_ffn_g": 1.0 + nrm(ks[10], (DEPTH, D_MODEL), 0.02),
        "peer_w_query": nrm(ks[11], (DEPTH, D_MODEL, PEER_HEADS * PEER_QDIM), D_MODEL ** -0.5),
        "peer_sub_keys": nrm(ks[12], (DEPTH, PEER_HEADS, 2, PEER_NKEYS, PEER_HALF), PEER_HALF ** -0.5),
        "peer_u": nrm(ks[13], (DEPTH, PEER_EXPERTS, D_MODEL), D_MODEL ** -0.5),
        "peer_v": nrm(ks[14], (DEPTH, PEER_EXPERTS, D_MODEL), 0.1),
    }

def second_block(x, ln_mix_g, w_in, gmlp_norm_g, gmlp_w_s, gmlp_b_s, q_norm_g, k_norm_g, rel_bias,
              w_out, ln_ffn_g, peer_w_query, peer_sub_keys, peer_u, peer_v):
    a0, a1 = MIX_A_WIDTH, 2 * MIX_A_WIDTH
    q0, k0, v0 = a1, a1 + MIX_B_WIDTH, a1 + 2 * MIX_B_WIDTH
    for l in range(DEPTH):
        xn = rms_norm_2(x, ln_mix_g[l])
        proj = xn @ w_in[l]
        a_out = gmlp_spatial_gating(proj[..., :a0], proj[..., a0:a1],
                                    gmlp_norm_g[l], gmlp_w_s[l], gmlp_b_s[l])
        b_out = banded_chunk_attention(proj[..., q0:k0], proj[..., k0:v0], proj[..., v0:],
                                       q_norm_g[l], k_norm_g[l], rel_bias[l])
        x = x + jnp.concatenate([a_out, b_out], axis=-1) @ w_out[l]
        x = x + peer_ffn(rms_norm_2(x, ln_ffn_g[l]), peer_w_query[l], peer_sub_keys[l],
                         peer_u[l], peer_v[l])
    return x


def setup_inputs(seed=0):
    out = dict(first_inputs(seed))
    for name, value in second_inputs(seed + 1).items():
        if name != "x":
            out[name + "_2"] = value
    return out


def reference(
    x, mem, norm_mix_g, norm_mem_g, w_in, na_rpb, rw_mu_rkv, rw_mu_w, rw_mu_a, rw_w0, rw_w2,
    rw_a0, rw_a2, rw_k_k, rw_k_a, rw_r_k, rw_g2, rw_ln_g, rw_ln_b, w_mem_kv, w_branch_na,
    w_branch_rw, w_branch_mem, w_out, norm_ffn_g, w_router, w_exp_gate, w_exp_up, w_exp_down,
    norm_final_g, ln_mix_g_2, w_in_2, gmlp_norm_g_2, gmlp_w_s_2, gmlp_b_s_2, q_norm_g_2,
    k_norm_g_2, rel_bias_2, w_out_2, ln_ffn_g_2, peer_w_query_2, peer_sub_keys_2, peer_u_2,
    peer_v_2,
):
    x = first_block(
        x, mem, norm_mix_g, norm_mem_g, w_in, na_rpb, rw_mu_rkv, rw_mu_w, rw_mu_a, rw_w0, rw_w2,
        rw_a0, rw_a2, rw_k_k, rw_k_a, rw_r_k, rw_g2, rw_ln_g, rw_ln_b, w_mem_kv, w_branch_na,
        w_branch_rw, w_branch_mem, w_out, norm_ffn_g, w_router, w_exp_gate, w_exp_up,
        w_exp_down, norm_final_g,
    )
    return second_block(
        x, ln_mix_g_2, w_in_2, gmlp_norm_g_2, gmlp_w_s_2, gmlp_b_s_2, q_norm_g_2, k_norm_g_2,
        rel_bias_2, w_out_2, ln_ffn_g_2, peer_w_query_2, peer_sub_keys_2, peer_u_2, peer_v_2,
    )


_drawn_inputs = setup_inputs


def setup_inputs(seed=0):
    import zlib

    import numpy as np

    out = dict(_drawn_inputs(seed))
    spreads = {}
    factors = {'norm_mix_g': 3.11,
     'norm_mem_g': 8.0,
     'na_rpb': 5.493,
     'rw_mu_w': 7.635,
     'rw_w2': 2.843,
     'rw_a0': 3.193,
     'rw_k_k': 27.675,
     'rw_k_a': 4.714,
     'rw_ln_g': 23.326,
     'rw_ln_b': 18.137,
     'norm_ffn_g': 3.375,
     'ln_mix_g_2': 3.97,
     'gmlp_norm_g_2': 20.282,
     'q_norm_g_2': 8.0,
     'k_norm_g_2': 8.0,
     'rel_bias_2': 24.149,
     'ln_ffn_g_2': 64.0,
     'gmlp_b_s_2': 3.545}
    for name, (base, spread) in spreads.items():
        noise = np.random.default_rng([zlib.crc32(name.encode()), seed]).standard_normal(out[name].shape)
        drawn = base * np.exp(spread * noise) if base else spread * noise
        out[name] = jnp.asarray(drawn.astype(out[name].dtype))
    for name, factor in factors.items():
        out[name] = (out[name] * factor).astype(out[name].dtype)
    return out
```

```python
import math
from contextlib import ExitStack

import numpy as np

import concourse.bass as bass
from concourse import mybir

NS = 6
TILES_A = 33
TILES_B = 22

C_IDENT, C_ONES, C_M4, C_LVL, C_SCAN, C_BD, C_IOTA, C_WM, C_EM, C_ES, C_END = (
    0, 128, 256, 768, 1536, 2048, 2176, 2688, 2816, 2944, 2952)
(K_MIX, K_MEM, K_FFN, K_MIX2, K_FFN2, K_MU, K_MUWA, K_W0, K_A0, K_KK, K_KA, K_RK, K_LNG, K_LNB, K_QN, K_KN, K_END) = (
    0, 8, 16, 24, 32, 40, 58, 60, 66, 72, 75, 78, 81, 84, 87, 88, 89)


class Queue:

    def __init__(self, sem):
        self.sem, self.n, self.items = sem, 0, []

    def add(self, fns, deps, chain):
        waits = flat(deps)
        if chain and self.n:
            waits.append((self.sem, self.n))
        self.n += 1
        self.items.append((fns, waits, (self.sem, 1)))
        return (self.sem, self.n)

    def emit(self, eng):
        seen = {}
        for fns, waits, (sem, k) in self.items:
            for s, v in waits:
                if seen.get(id(s), 0) < v:
                    eng.wait_ge(s, v)
                    seen[id(s)] = v
            last = None
            for f in fns:
                last = f(eng)
            if last is not None:
                last.then_inc(sem, k)


def flat(deps):
    out = []
    for d in deps:
        if d is None:
            continue
        if len(d) == 2 and isinstance(d[1], int):
            out.append(d)
        else:
            out += flat(d)
    return out


def block_program(nc, I, O, stop=None, dbg=None):
    f32, i32, u32 = mybir.dt.float32, mybir.dt.int32, mybir.dt.uint32
    ACT, ALU, AX = mybir.ActivationFunctionType, mybir.AluOpType, mybir.AxisListType
    ADD, SUB, MUL, MAX = ALU.add, ALU.subtract, ALU.mult, ALU.max
    ctx = ExitStack()
    with ctx:
        def sem(n):
            return ctx.enter_context(nc.semaphore(n))

        TOTAL = 52600
        AR_ = ctx.enter_context(nc.sbuf_tensor("arena", [128, TOTAL], f32))
        PS = [ctx.enter_context(nc.psum_tensor(f"ps{i}", [128, 512], f32)) for i in range(8)]
        h_dram = nc.dram_tensor("h_scratch", (512, 1024), f32, kind="Internal").ap()

        PE, V, S, G, SP = (Queue(sem(f"q_{n}")) for n in ("pe", "dve", "act", "pool", "sp"))

        def v(fn, *deps):
            return V.add([fn], deps, True)

        def s(fn, *deps):
            return S.add([fn], deps, True)

        def g(fn, *deps):
            return G.add([fn], deps, True)

        def pe(fns, *deps):
            return PE.add(fns, deps, False)

        nsem = [0]
        sems = {}

        def dma(q, out, in_, *deps, on=None):
            if on is None:
                nsem[0] += 1
                on = f"d{nsem[0]}"
            if on not in sems:
                sems[on] = [sem(on), 0]
            r = sems[on]
            r[1] += 16
            q.items.append(([lambda e: e.dma_start(out, in_)], flat(deps), (r[0], 16)))
            return (r[0], r[1])

        def gather(out, table, idx, *deps, on):
            if on not in sems:
                sems[on] = [sem(on), 0]
            r = sems[on]
            r[1] += 16
            G.items.append(([lambda e: e.indirect_dma_start(out, None, table, bass.IndirectOffsetOnAxis(ap=idx, axis=0))],
                            flat(deps), (r[0], 16)))
            return (r[0], r[1])

        def tok(q):
            return (q.sem, q.n) if q.n else None

        def fence():
            return [tok(PE), tok(V), tok(S), tok(G)]

        def mm(out, l, r, st=True, sp=True):
            return lambda e: e.matmul(out, l, r, start=st, stop=sp, skip_group_check=True)

        def tr(out, in_):
            n = in_.shape[0]
            return lambda e: e.transpose(out, in_, ident[0:n, 0:n])

        def tt(o, a, b, op):
            return lambda e: e.tensor_tensor(o, a, b, op)

        def ts(o, a, s1, op, s2=None, op2=None):
            if op2 is None:
                return lambda e: e.tensor_scalar(o, a, s1, None, op)
            return lambda e: e.tensor_scalar(o, a, s1, s2, op, op2)

        def stt(o, a, sc, b, o0, o1):
            return lambda e: e.scalar_tensor_tensor(out=o, in0=a, scalar=sc, in1=b, op0=o0, op1=o1)

        def act(o, a, f, **k):
            return lambda e: e.activation(o, a, f, **k)

        def cp(o, a):
            return lambda e: e.tensor_copy(o, a)

        def bc(ap, n):
            return ap.to_broadcast(list(ap.shape[:-1]) + [n])

        class Banks:
            def __init__(self, ids):
                self.ids, self.at, self.rel = ids, 0, {i: None for i in ids}

            def take(self):
                i = self.ids[self.at % len(self.ids)]
                self.at += 1
                return i

            def free(self, i, *t):
                self.rel[i] = list(t)

        def fl(off, *shape):
            n = int(np.prod(shape))
            assert off + n <= TOTAL, (off, shape)
            a = AR_[:, off:off + n]
            if len(shape) == 1:
                return a
            names = "abcd"[:len(shape)]
            return a.rearrange("p (" + " ".join(names) + ") -> p " + " ".join(names), **dict(zip(names, shape)))

        cons = fl(0, C_END)
        ident = cons[:, 0:128]
        ones = cons[:, C_ONES:C_ONES + 128]
        cols = fl(C_END, K_END)
        o = C_END + 96
        small = fl(o, 192)
        o += 192
        RING = o
        o += NS * 2048
        X = fl(o, 4, 1024)
        o += 4096
        D0 = o
        room = TOTAL - D0

        def at(off, *shape):
            assert off + int(np.prod(shape)) <= room, (off, shape, room)
            return fl(D0 + off, *shape)

        ring_n, ring_rel = [0], {}

        def ring_next(parts):
            n = ring_n[0]
            ring_n[0] += 1
            buf = fl(RING + (n % NS) * 2048, 2048)
            t = None
            for shape, src in parts:
                dst = buf if shape is None else buf.rearrange("p (a b) -> p a b", a=shape)
                t = dma(SP, dst, src, ring_rel.get(n - NS), on=f"ring{n % NS}")
            return n, buf, t

        def ring_free(n, *t):
            ring_rel[n] = list(t)

        wt_n = [0]

        def wtile():
            t = wt_n[0]
            wt_n[0] += 1
            n, buf, tk = ring_next([(None, I["wt"][t])])
            return n, buf.rearrange("p (k c) -> p k c", k=8), tk

        tc = dma(SP, cons, I["consts"])
        tk = dma(SP, cols, I["cols"])
        tx = dma(SP, X, I["x"].rearrange("(a p) f -> p a f", p=128))

        allb = Banks(list(range(8)))

        def dump(ap, *deps):
            n = int(np.prod(ap.shape[1:]))
            dst = dbg.rearrange("p n -> p n")[:, 0:n]
            if len(ap.shape) == 3:
                dst = dst.rearrange("p (a b) -> p a b", a=ap.shape[1])
            return dma(SP, dst, ap, fence())

        def colmul(out, in_, k0):
            return lambda e: e.tensor_scalar(out, in_, cols[:, k0:k0 + 1], None, MUL)

        def rms_rows(src, dst, nt, width, junk, sc, eps, *deps):
            t = None
            for i in range(nt):
                t = s(act(junk, src[:, i, :], ACT.Square, accum_out=sc[:, i:i + 1]), *deps)
            t = v(ts(sc[:, 0:nt], sc[:, 0:nt], 1.0 / width, MUL, eps, ADD), t)
            t = s(act(sc[:, 0:nt], sc[:, 0:nt], ACT.Sqrt), t)
            t = v(lambda e: e.reciprocal(sc[:, 0:nt], sc[:, 0:nt]), t)
            for i in range(nt):
                t = v(ts(dst[:, i, :], src[:, i, :], sc[:, i:i + 1], MUL), *deps)
            return t

        def to_feature(src, dst, nt, k0, banks, *deps):
            last = []
            for c in range(8):
                b = banks.take()
                t = pe([tr(PS[b][:, 128 * i:128 * i + 128], src[:, i, 128 * c:128 * c + 128]) for i in range(nt)],
                       deps, tc, banks.rel[b])
                if c % 2:
                    t = v(colmul(dst[:, c, :], PS[b][:, 0:128 * nt], k0 + c), t, tk)
                else:
                    t = s(act(dst[:, c, :], PS[b][:, 0:128 * nt], ACT.Copy, scale=cols[:, k0 + c:k0 + c + 1]), t, tk)
                banks.free(b, t)
                last.append(t)
            return last[-2:]

        def proj_f(w, lo, rhs, n, b, *deps):
            return pe([mm(PS[b][:, 0:n], w[:, k, lo:lo + 128], rhs[:, k, :], k == 0, k == 7) for k in range(8)],
                      deps, allb.rel[b])

        def proj_t(w, lo, nn, lhs, i, out, b, *deps):
            return pe([mm(out, lhs[:, k, 128 * i:128 * i + 128], w[:, k, lo:lo + nn], k == 0, k == 7) for k in range(8)],
                      deps, allb.rel[b])

        OFF_H = 0
        hT = at(OFF_H, 8, 512)
        XN = at(4096, 4, 1024)
        JK = at(8192, 1024)
        tr1 = rms_rows(X, XN, 4, 1024.0, JK, small[:, 0:4], 1e-6, tx)
        th = to_feature(XN, hT, 4, K_MIX, allb, tr1)

        o = 4096
        pr = at(o, 3, 514); o += 1542
        pk = at(o, 3, 514); o += 1542
        pv = at(o, 3, 514); o += 1542
        pw = at(o, 514); o += 514
        lg = at(o, 512); o += 512
        yS = at(o, 3, 512); o += 1536
        bS = at(o, 3, 512); o += 1536
        R = at(o, 3, 512); o += 1536
        K = at(o, 3, 512); o += 1536
        VV = at(o, 3, 512); o += 1536
        T1o = o
        T1 = at(o, 3, 512); o += 1536
        T3 = at(o, 3, 512); o += 1536
        T4 = at(o, 3, 512); o += 1536
        T5 = at(o, 3, 512); o += 1536
        T2 = at(o, 3, 512); o += 1536
        AR = at(o, 3, 4, 256); o += 3072
        W2 = at(o, 2, 384); o += 768
        G2 = at(o, 384); o += 384
        m_ = T1o
        M4 = at(m_, 6, 512); m_ += 3072
        Tm = at(m_, 6, 128); m_ += 768
        TT = at(m_, 6, 128); m_ += 768
        X1 = at(m_, 6, 128); m_ += 768
        BT = at(m_, 6, 128); m_ += 768
        assert m_ <= T1o + 6144
        ATok = at(o, 4, 384); o += 1536
        Ro = T1o - 4608
        At, MV, U0, U = at(Ro, 3, 128), at(Ro + 384, 384), at(Ro + 768, 384), at(Ro + 1152, 384)
        SS = [at(o, 3, 128), at(o + 384, 3, 128)]; o += 768
        PCM = at(o, 3, 128); o += 384
        PC = at(o, 3, 8); o += 24

        te = fence()
        tw2 = dma(SP, W2, I["w2a2"].rearrange("p (a b) -> p a b", a=2), te)
        tg2 = dma(SP, G2, I["g2"], te)
        te = fence()
        tz = None
        for p in (pr, pk, pv):
            tz = g(lambda e, p=p: e.memset(p[:, :, 0:514:513], 0.0), te)
        tz = g(lambda e: e.memset(pw[:, 0:514:513], 0.0), te)

        dst = [p[:, c, 1:513] for p in (pr, pk, pv) for c in range(3)] + [pw[:, 1:513], lg]
        tp = []
        for n in range(22 // 2):
            if n >= 6:
                break
            rn, w, tw = wtile()
            for a in range(2):
                if 2 * n + a >= 11:
                    break
                b = allb.take()
                t = proj_f(w, 128 * a, hT, 512, b, th, tw)
                last = t
                d = dst[2 * n + a]
                t2 = s(act(d, PS[b][:, :], ACT.Copy), t, te) if a else v(cp(d, PS[b][:, :]), t, te)
                allb.free(b, t2)
                tp.append(t2)
            if 2 * n + 1 < 11:
                ring_free(rn, last)
            else:
                keep = (rn, w, tw)
        tp = [tp[-1], tp[-2], tz]

        pb = Banks([0, 1, 2, 3, 4, 5, 6, 7])
        pb.rel.update(allb.rel)

        def head_sum(src, nch, use, *deps):
            for c in range(nch):
                b = pb.take()
                t = pe([mm(PS[b][:, :], ones, src(c))], deps, tc, pb.rel[b])
                pb.free(b, use(c, PS[b], t))

        for d in range(2):
            fe = fence()
            fw = slice(None, None, None) if d == 0 else slice(None, None, -1)
            lo = 0 if d == 0 else 2
            tm = None
            for n, (p, q) in enumerate(((pr, R), (pk, K), (pv, VV))):
                v(tt(T5[:, :, :], p[:, :, lo:lo + 512], p[:, :, 1:513], SUB), tp, fe)
                for c in range(3):
                    k0 = K_MU + (d * 3 + n) * 3 + c
                    tm = v(stt(q[:, c, fw], T5[:, c, :], cols[:, k0:k0 + 1], p[:, c, 1:513], MUL, ADD), tk)
            v(tt(T5[:, 0, :], pw[:, lo:lo + 512], pw[:, 1:513], SUB))
            tm = v(stt(T5[:, 1, fw], T5[:, 0, :], cols[:, K_MUWA + d:K_MUWA + d + 1], pw[:, 1:513], MUL, ADD))
            t = s(act(T5[0:64, 2, :], T5[0:64, 1, :], ACT.Tanh), tm, fe)
            tlw = []
            for c in range(3):
                b = pb.take()
                t1 = pe([mm(PS[b][:, :], W2[0:64, d, 128 * c:128 * c + 128], T5[0:64, 2, :])], t, tw2, pb.rel[b], fe)
                t2 = s(act(T3[:, c, :], PS[b][:, :], ACT.Sigmoid, bias=cols[:, K_W0 + 3 * d + c:K_W0 + 3 * d + c + 1]), t1)
                pb.free(b, t2)
                b = pb.take()
                t1 = pe([mm(PS[b][:, :], W2[64:128, d, 128 * c:128 * c + 128], T5[64:128, 1, :])], tm, tw2, pb.rel[b])
                t2 = s(act(T2[:, c, :], PS[b][:, :], ACT.Sigmoid, bias=cols[:, K_A0 + 3 * d + c:K_A0 + 3 * d + c + 1]), t1)
                pb.free(b, t2)
                tlw = t2
            tsc = tlw
            v(ts(T3[:, :, :], T3[:, :, :], -math.exp(-0.5), MUL), tsc)
            for c in range(3):
                v(lambda e, c=c: e.tensor_tensor_scan(T4[:, c, :], cons[:, C_SCAN:C_SCAN + 512], T3[:, c, :], 0.0, MUL, ADD), tc)
            for c in range(3):
                v(ts(T1[:, c, :], K[:, c, :], cols[:, K_KK + c:K_KK + c + 1], MUL))
            t = v(tt(T5[:, :, :], T1[:, :, :], T1[:, :, :], MUL), tok(PE))
            nr = []

            def use_norm(c, P, t):
                t = s(act(T5[:, c, :], P[:, :], ACT.Sqrt), t)
                nr.append(t)
                return t
            head_sum(lambda c: T5[:, c, :], 3, use_norm, t)
            v(ts(T5[:, :, :], T5[:, :, :], 1e-12, MAX), nr)
            v(lambda e: e.reciprocal(T5[:, :, :], T5[:, :, :]))
            v(tt(T1[:, :, :], T1[:, :, :], T5[:, :, :], MUL))
            for c in range(3):
                v(ts(T5[:, c, :], T2[:, c, :], 1.0, SUB, cols[:, K_KA + c:K_KA + c + 1], MUL))
            v(stt(K[:, :, :], T5[:, :, :], 1.0, K[:, :, :], ADD, MUL))
            v(tt(T5[:, :, :], R[:, :, :], K[:, :, :], MUL))
            for c in range(3):
                t = v(ts(T5[:, c, :], T5[:, c, :], cols[:, K_RK + c:K_RK + c + 1], MUL))

            def use_bonus(c, P, t):
                if d == 0:
                    return v(tt(bS[:, c, :], P[:, :], VV[:, c, :], MUL), t)
                v(tt(T5[:, c, :], P[:, :], VV[:, c, :], MUL), t)
                return v(tt(bS[:, c, ::-1], T5[:, c, :], bS[:, c, ::-1], ADD))
            head_sum(lambda c: T5[:, c, :], 3, use_bonus, t)
            t = v(tt(T5[:, :, :], T4[:, :, :], T3[:, :, :], SUB))
            te0 = s(act(T5[:, :, :], T5[:, :, :], ACT.Exp), t)
            te1 = s(act(T3[:, :, :], T4[:, :, :], ACT.Exp, scale=-1.0), t)
            te2 = s(act(T4[:, :, :], T4[:, :, :], ACT.Exp), t)
            v(tt(T2[:, :, :], T2[:, :, :], T1[:, :, :], MUL))
            for c in range(3):
                v(stt(AR[:, c, :, 0:128], T1[:, c, :].rearrange("p (j t) -> p j t", j=4), -1.0,
                      T5[:, c, :].rearrange("p (j t) -> p j t", j=4), MUL, MUL), te0)
            v(tt(T2[:, :, :], T2[:, :, :], T3[:, :, :], MUL), te1)
            v(tt(K[:, :, :], K[:, :, :], T3[:, :, :], MUL))
            for c in range(3):
                v(tt(AR[:, c, :, 128:256], R[:, c, :].rearrange("p (j t) -> p j t", j=4),
                     T4[:, c, :].rearrange("p (j t) -> p j t", j=4), MUL), te2)
            tel = v(cp(PC, T4[:, :, 63:512:64]))
            ts0 = g(lambda e: e.memset(SS[0], 0.0), fe)
            st = ts0
            cur = 0
            for j in range(4):
                jt = slice(128 * j, 128 * j + 128)
                fj = [tok(V), tok(PE), tok(S)]
                for n, src in enumerate((None, T2, K, VV)):
                    b = pb.take()
                    t = pe([tr(PS[b][:, 128 * c:128 * c + 128], AR[:, c, j, 0:128] if src is None else src[:, c, jt])
                            for c in range(3)], tel, pb.rel[b], tok(S) if j else None)
                    t = s(act(ATok[:, n, :], PS[b][:, 0:384], ACT.Copy), t, fj)
                    pb.free(b, t)
                ttk = t
                for h in range(6):
                    c, r = h // 2, slice(64 * (h % 2), 64 * (h % 2) + 64)
                    b = pb.take()
                    t = pe([mm(PS[b][:, 0:256], T2[r, c, jt], AR[r, c, j, :]),
                            mm(PS[b][:, 256:512], K[r, c, jt], AR[r, c, j, :])], tel, pb.rel[b])
                    t = v(tt(M4[:, h, :], PS[b][:, :], cons[:, C_M4:C_M4 + 512], MUL), t, fj)
                    pb.free(b, t)
                tm4 = t

                def lvl(n):
                    return cons[:, C_LVL + 128 * n:C_LVL + 128 * n + 128].rearrange("p (a b) -> p a b", a=1).to_broadcast([128, 6, 128])
                idb = ident.rearrange("p (a b) -> p a b", a=1).to_broadcast([128, 6, 128])
                v(tt(TT[:, :, :], M4[:, :, 0:128], lvl(0), MUL))
                tTT = v(tt(TT[:, :, :], TT[:, :, :], idb, ADD))
                tT = None
                for k in range(2):
                    b = pb.take()
                    t = pe([tr(PS[b][:, 128 * q:128 * q + 128], TT[:, 3 * k + q, :]) for q in range(3)], tTT, pb.rel[b])
                    tT = s(act(Tm[:, 3 * k:3 * k + 3, :], PS[b][:, 0:384].rearrange("p (a b) -> p a b", a=3), ACT.Copy), t)
                    pb.free(b, tT)
                for n in range(1, 6):
                    tb = g(tt(BT[:, :, :], M4[:, :, 0:128], lvl(n), MUL), tm4, tok(PE))
                    tx1 = []
                    for k in range(2):
                        b = pb.take()
                        t = pe([mm(PS[b][:, 128 * q:128 * q + 128], BT[:, 3 * k + q, :], Tm[:, 3 * k + q, :])
                                for q in range(3)], tb, tT, tTT, pb.rel[b])
                        t = s(act(X1[:, 3 * k:3 * k + 3, :], PS[b][:, 0:384].rearrange("p (a b) -> p a b", a=3), ACT.Copy), t)
                        pb.free(b, t)
                        tx1.append(t)
                    bs = []
                    for k in range(2):
                        b = pb.take()
                        b2 = pb.take() if n < 5 else None
                        fs = [mm(PS[b][:, 128 * q:128 * q + 128], X1[:, 3 * k + q, :], TT[:, 3 * k + q, :]) for q in range(3)]
                        ds = [tx1[k], pb.rel[b]]
                        if b2 is not None:
                            fs += [mm(PS[b2][:, 128 * q:128 * q + 128], TT[:, 3 * k + q, :], X1[:, 3 * k + q, :]) for q in range(3)]
                            ds.append(pb.rel[b2])
                        t = pe(fs, ds)
                        bs.append((k, b, b2, t))
                    for k, b, b2, t in bs:
                        q = slice(3 * k, 3 * k + 3)
                        tTT = v(tt(TT[:, q, :], TT[:, q, :], PS[b][:, 0:384].rearrange("p (a b) -> p a b", a=3), ADD), t)
                        pb.free(b, tTT)
                        if b2 is not None:
                            tT = v(tt(Tm[:, q, :], Tm[:, q, :], PS[b2][:, 0:384].rearrange("p (a b) -> p a b", a=3), ADD), t)
                            pb.free(b2, tT)
                b = pb.take()
                t = pe([mm(PS[b][:, 64 * h:64 * h + 64], M4[:, h, 256:384], ATok[:, 3, 64 * h:64 * h + 64]) for h in range(6)],
                       tm4, ttk, pb.rel[b])
                t = s(act(MV, PS[b][:, 0:384], ACT.Copy), t, fj)
                pb.free(b, t)
                b = pb.take()
                t = pe([mm(PS[b][:, 64 * h:64 * h + 64], TT[:, h, :], MV[:, 64 * h:64 * h + 64]) for h in range(6)],
                       t, tTT, pb.rel[b])
                tu0 = s(act(U0, PS[b][:, 0:384], ACT.Copy), t)
                pb.free(b, tu0)
                b = pb.take()
                t = pe([mm(PS[b][64 * (h % 2):64 * (h % 2) + 64, 128 * (h // 2):128 * (h // 2) + 128],
                           ATok[:, 0, 64 * h:64 * h + 64], TT[:, h, :]) for h in range(6)], pb.rel[b])
                tat = s(act(At, PS[b][:, 0:384].rearrange("p (a b) -> p a b", a=3), ACT.Copy), t)
                pb.free(b, tat)
                for q in range(2):
                    n = 2 * j + q
                    r = slice(64 * q, 64 * q + 64)
                    S0, S1 = SS[cur], SS[1 - cur]
                    b = pb.take()
                    t = pe([mm(PS[b][r, 128 * p:128 * p + 128], At[:, p, r], S0[:, p, :]) for p in range(3)],
                           tat, st, pb.rel[b])
                    tu = v(tt(U[r, :], PS[b][r, 0:384], U0[r, :], ADD), t, tu0)
                    pb.free(b, tu)
                    tpc = g(tt(PCM, cons[:, C_BD:C_BD + 128].rearrange("p (a b) -> p a b", a=1).to_broadcast([128, 3, 128]),
                               PC[:, :, n:n + 1].to_broadcast([128, 3, 128]), MUL), tel, tok(V))
                    b = pb.take()
                    fs = []
                    for p in range(3):
                        pc = slice(128 * p, 128 * p + 128)
                        fs += [mm(PS[b][:, pc], ATok[r, 1, pc], U[r, pc], True, False),
                               mm(PS[b][:, pc], ATok[r, 2, pc], ATok[r, 3, pc], False, True)]
                    t = pe(fs, tu, pb.rel[b])
                    v(tt(S1, PS[b][:, 0:384].rearrange("p (a b) -> p a b", a=3), S0, ADD), t)
                    st = v(tt(S1, S1, PCM, MUL), tpc)
                    pb.free(b, st)
                    b = pb.take()
                    fs = []
                    for p in range(3):
                        oc = slice(64 * p, 64 * p + 64)
                        fs.append(mm(PS[b][:, oc], S0[:, p, :], AR[:, p, j, 128 + 64 * q:192 + 64 * q], True, False))
                        for e2 in range(2):
                            h = 2 * p + e2
                            orow = slice(64 * e2, 64 * e2 + 64)
                            fs.append(mm(PS[b][orow, oc], U[r, 64 * h:64 * h + 64], M4[r, h, 128 + 64 * q:192 + 64 * q], False, False))
                            fs.append(mm(PS[b][orow, oc], ATok[r, 3, 64 * h:64 * h + 64], M4[r, h, 384 + 64 * q:448 + 64 * q], False, True))
                    t = pe(fs, pb.rel[b])
                    src = PS[b][:, 0:192].rearrange("p (a b) -> p a b", a=3)
                    if d == 0:
                        t = s(act(yS[:, :, 64 * n:64 * n + 64], src, ACT.Copy), t, fe)
                    else:
                        o_ = yS[:, :, 448 - 64 * n:512 - 64 * n]
                        t = v(tt(o_[:, :, ::-1], src, o_[:, :, ::-1], ADD), t)
                    pb.free(b, t)
                    cur = 1 - cur
            if cur:
                raise AssertionError

        fe = fence()
        tmean = []

        def use_mean(c, P, t):
            t = v(stt(T1[:, c, :], P[:, :], -1.0 / 64, yS[:, c, :], MUL, ADD), t, fe)
            return v(tt(T3[:, c, :], T1[:, c, :], T1[:, c, :], MUL))
        head_sum(lambda c: yS[:, c, :], 3, use_mean, fe)
        rs = []

        def use_var(c, P, t):
            t = v(ts(T4[:, c, :], P[:, :], 1.0 / 64, MUL, 64e-5, ADD), t)
            t2 = s(act(T4[:, c, :], T4[:, c, :], ACT.Sqrt), t)
            rs.append(t2)
            return t
        head_sum(lambda c: T3[:, c, :], 3, use_var, tok(V))
        v(lambda e: e.reciprocal(T4[:, :, :], T4[:, :, :]), rs)
        v(tt(T1[:, :, :], T1[:, :, :], T4[:, :, :], MUL))
        for c in range(3):
            v(ts(T1[:, c, :], T1[:, c, :], cols[:, K_LNG + c:K_LNG + c + 1], MUL, cols[:, K_LNB + c:K_LNB + c + 1], ADD))
        ty = v(tt(T1[:, :, :], T1[:, :, :], bS[:, :, :], ADD))
        tg = s(act(T5[:, 0, :], lg, ACT.Sigmoid), fe)
        for c in range(3):
            b = pb.take()
            t = pe([mm(PS[b][:, :], G2[:, 128 * c:128 * c + 128], T5[:, 0, :])], tg, tg2, pb.rel[b])
            t = v(tt(yS[:, c, :], T1[:, c, :], PS[b][:, :], MUL), t)
            pb.free(b, t)
        allb.rel.update(pb.rel)
        if stop == "rw":
            dump(yS)
            return finish(nc, ctx, PE, V, S, G, SP, sems)

        YO = room - 4096 - 1536
        yR = at(YO, 3, 512)
        yN = at(YO + 1536, 3, 512)
        yM = at(YO + 3072, 2, 512)
        fe = fence()
        tyr = g(cp(yR, yS), fe)
        fe = fence()
        o = 4096
        qT = at(o, 3, 512); o += 1536
        kT = at(o, 3, 512); o += 1536
        vt = at(o, 4, 384); o += 1536
        nb = at(o, 6, 1024); o += 6144
        Pb = [at(o + 512 * i, 512) for i in range(3)]; o += 1536
        PT = [at(o + 2048 * i, 4, 512) for i in range(2)]; o += 4096
        mq = at(o, 2, 512); o += 1024
        assert o <= YO
        tnb = dma(SP, nb, I["nab"].rearrange("p (a b) -> p a b", a=6), fe)
        tqk = []
        cc = 0
        tile = keep
        vbank = [allb.take() for _ in range(4)]
        order = [("q", 0), ("q", 1), ("q", 2), ("k", 0), ("k", 1), ("k", 2), ("v", 0), ("v", 1), ("v", 2), ("m", 0), ("m", 1)]
        half = 1
        other = Banks([i for i in range(8) if i not in vbank])
        for kind, c in order:
            if half == 2:
                tile = wtile()
                half = 0
            rn, w, tw = tile
            if kind == "v":
                for i in range(4):
                    t = proj_t(w, 128 * half, 128, hT, i, PS[vbank[i]][:, 128 * c:128 * c + 128], vbank[i], tw)
                last = t
                if c == 2:
                    for i in range(4):
                        t2 = (s(act(vt[:, i, :], PS[vbank[i]][:, 0:384], ACT.Copy), t, fe) if i % 2 else
                              v(cp(vt[:, i, :], PS[vbank[i]][:, 0:384]), t, fe))
                        allb.free(vbank[i], t2)
                        tqk.append(t2)
            else:
                b = other.take()
                last = t = proj_f(w, 128 * half, hT, 512, b, tw)
                d_ = {"q": qT, "k": kT, "m": mq}[kind][:, c, :]
                if kind == "k":
                    t2 = s(act(d_, PS[b][:, :], ACT.Copy), t, fe)
                else:
                    t2 = v(ts(d_, PS[b][:, :], 0.125, MUL), t, fe)
                allb.free(b, t2)
                tqk.append(t2)
            half += 1
            if half == 2:
                ring_free(rn, last)
        assert half == 2

        def attention(nh, ntile, q_, k_, nk, bias, v_, out, Pb, PT, sm, deps, causal=False):
            sb_ = Banks([0, 1, 2])
            tb_ = Banks([3, 4, 5])
            ob_ = Banks([6, 7])
            for x_ in (sb_, tb_, ob_):
                for i in x_.ids:
                    x_.rel[i] = allb.rel[i]
            units = [(h, i) for h in range(nh) for i in range(ntile)]
            prel = [None] * 3
            ptrel = [None] * 2
            info = {}
            ptt = {}

            def scores(u):
                h, i = units[u]
                r = slice(64 * (h % 2), 64 * (h % 2) + 64)
                b = sb_.take()
                n = nk(i)
                t = pe([mm(PS[b][:, 0:n], q_[r, h // 2, 128 * i:128 * i + 128], k_[r, h // 2, 0:n])], deps, sb_.rel[b])
                P = Pb[u % 3][:, 0:n]
                m = sm[:, u % 8:u % 8 + 1]
                l = sm[:, 8 + u % 8:9 + u % 8]
                if bias is not None:
                    t = v(lambda e: e.tensor_tensor_reduce(out=P, in0=PS[b][:, 0:n], in1=bias(h, i), scale=-1.0, scalar=3.0e38,
                                                           op0=ADD, op1=ALU.min, accum_out=m), t, prel[u % 3])
                    sb_.free(b, t)
                    t = s(act(P, P, ACT.Exp, bias=m, scale=-1.0, accum_out=l), t)
                else:
                    t = v(lambda e: e.tensor_reduce(m, PS[b][:, 0:n], AX.X, MAX, negate=True), t)
                    t = s(act(P, PS[b][:, 0:n], ACT.Exp, bias=m, accum_out=l), t, prel[u % 3])
                    sb_.free(b, t)
                v(lambda e: e.reciprocal(l, l), t)
                info[u] = v(ts(P, P, l, MUL))

            def turn(u):
                h, i = units[u]
                P = Pb[u % 3]
                n = nk(i) // 128
                b = tb_.take()
                t = pe([tr(PS[b][:, 128 * k:128 * k + 128], P[:, 128 * k:128 * k + 128]) for k in range(n)], info[u], tb_.rel[b])
                prel[u % 3] = t
                t = s(act(PT[h % 2][:, 0:n, 128 * i:128 * i + 128], PS[b][:, 0:128 * n].rearrange("p (a b) -> p a b", a=n), ACT.Copy),
                      t, ptrel[h % 2])
                tb_.free(b, t)
                if i == ntile - 1:
                    nkc = nk(ntile - 1) // 128
                    if h % 2 == 0:
                        info["o"] = ob_.take()
                    b = info["o"]
                    orow = slice(64 * (h % 2), 64 * (h % 2) + 64)
                    lo = (lambda k: 128 * k) if causal else (lambda k: 0)
                    t = pe([mm(PS[b][orow, lo(k):512], v_[:, k, 64 * h:64 * h + 64], PT[h % 2][:, k, lo(k):512], k == 0, k == nkc - 1)
                            for k in range(nkc)], t, ob_.rel[b])
                    ptrel[h % 2] = t
                    if h % 2:
                        t = v(cp(out[:, h // 2, :], PS[b][:, :]), t)
                        ob_.free(b, t)
                        info["y"] = t
            for u in range(len(units) + 2):
                if u < len(units):
                    scores(u)
                if u >= 2:
                    turn(u - 2)
            for x_ in (sb_, tb_, ob_):
                allb.rel.update(x_.rel)
            return info["y"]

        ty1 = attention(6, 4, qT, kT, lambda i: 512, lambda h, i: nb[:, h, 64 * (7 - 2 * i):64 * (7 - 2 * i) + 512] , vt, yN,
                        Pb, PT, small[:, 16:32], [tqk, tnb])
        if stop == "na":
            dump(yN)
            return finish(nc, ctx, PE, V, S, G, SP, sems)

        fe = fence()
        o = 4096
        mx = at(o, 2, 1024); o += 2048
        mT = at(o, 8, 256); o += 2048
        mj = at(o, 1024); o += 1024
        mk = at(o, 2, 256); o += 512
        mv = at(o, 2, 256); o += 512
        assert o <= 4096 + 3 * 1536 + 6144
        tmx = dma(SP, mx, I["mem"].rearrange("(a p) f -> p a f", p=128), fe)
        t = rms_rows(mx, mx, 2, 1024.0, mj, small[:, 4:8], 1e-6, tmx)
        tmt = to_feature(mx, mT, 2, K_MEM, allb, t)
        rn, w, tw = wtile()
        tkv = []
        for a in range(2):
            b = allb.take()
            last = t = proj_f(w, 128 * a, mT, 256, b, tmt, tw)
            t = v(cp(mk[:, a, :], PS[b][:, 0:256]), t, fe)
            allb.free(b, t)
            tkv.append(t)
        ring_free(rn, last)
        rn, w, tw = wtile()
        for a in range(2):
            b = allb.take()
            last = t = proj_t(w, 0, 256, mT, a, PS[b][:, 0:256], b, tmt, tw)
            t = v(cp(mv[:, a, :], PS[b][:, 0:256]), t, fe)
            allb.free(b, t)
            tkv.append(t)
        ring_free(rn, last)
        ty2 = attention(4, 4, mq, mk, lambda i: 256, None, mv, yM, Pb, PT, small[:, 16:32], [tqk, tkv])
        if stop == "mem":
            dump(yM)
            return finish(nc, ctx, PE, V, S, G, SP, sems)

        fe = fence()
        mg = at(4096, 8, 512)
        sg = [at(8192 + 512 * i, 512) for i in range(6)]
        ysrc = (yN, yR, yM)
        kc0 = (0, 3, 6)
        kcn = (3, 3, 2)
        tmg = []
        for f2 in range(4):
            sgt = {}
            for br in range(3):
                rn, w, tw = wtile()
                for a in range(2):
                    b = allb.take()
                    last = t = proj_f(w, 128 * a, hT, 512, b, tw)
                    t = s(act(sg[2 * br + a], PS[b][:, :], ACT.Sigmoid), t, fe, tok(V))
                    allb.free(b, t)
                    sgt[br, a] = t
                ring_free(rn, last)
            rn, w, tw = wtile()
            for a in range(2):
                f = 2 * f2 + a
                for br in range(3):
                    b = allb.take()
                    last = t = pe([mm(PS[b][:, :], w[:, kc0[br] + k, 128 * a:128 * a + 128], ysrc[br][:, k, :], k == 0, k == kcn[br] - 1)
                                   for k in range(kcn[br])], tw, allb.rel[b], fe)
                    if br == 0:
                        t = v(tt(mg[:, f, :], sg[a], PS[b][:, :], MUL), t, sgt[0, a], fe)
                    else:
                        t = v(tt(sg[2 * br + a], sg[2 * br + a], PS[b][:, :], MUL), t, sgt[br, a])
                    allb.free(b, t)
                v(tt(mg[:, f, :], mg[:, f, :], sg[2 + a], ADD))
                t = v(tt(mg[:, f, :], mg[:, f, :], sg[4 + a], ADD))
                tmg.append(t)
            ring_free(rn, last)

        def out_proj(src, *deps):
            t = None
            for n in range(4):
                rn, w, tw = wtile()
                for i in range(4):
                    b = allb.take()
                    last = t = pe([mm(PS[b][:, 0:256], src[:, k, 128 * i:128 * i + 128], w[:, k, :], k == 0, k == 7) for k in range(8)],
                                  tw, deps, allb.rel[b])
                    t = v(tt(X[:, i, 256 * n:256 * n + 256], X[:, i, 256 * n:256 * n + 256], PS[b][:, 0:256], ADD), t)
                    allb.free(b, t)
                ring_free(rn, last)
            return t
        tX = out_proj(mg, tmg)
        if stop == "mix1":
            dump(X)
            return finish(nc, ctx, PE, V, S, G, SP, sems)

        fe = fence()
        XN = at(0, 4, 1024)
        hT = at(4096, 8, 512)
        JK = at(8192, 1024)
        rt = at(9216, 8, 16)
        lgt = at(9344, 4, 16)
        aff = at(9408, 512)
        top = at(9920, 64)
        idxu = AR_[:, D0 + 9984:D0 + 10048].bitcast(u32)
        idxf = at(10048, 64)
        tv8 = at(10112, 8)
        ti8 = at(10120, 8)
        ii8 = AR_[:, D0 + 10128:D0 + 10136].bitcast(i32)
        two = at(10144, 2, 128)
        trt = dma(SP, rt, I["rt"].rearrange("p (a b) -> p a b", a=8), fe)
        t = rms_rows(X, XN, 4, 1024.0, JK, small[:, 0:4], 1e-6, fe)
        thd = dma(G, h_dram.rearrange("(a p) f -> p a f", p=128), XN, t)
        th = to_feature(XN, hT, 4, K_FFN, allb, t)
        b = allb.take()
        t = pe([mm(PS[b][:, 16 * i:16 * i + 16], hT[:, k, 128 * i:128 * i + 128], rt[:, k, :], k == 0, k == 7)
                for i in range(4) for k in range(8)], th, trt, allb.rel[b])
        l3 = PS[b][:, 0:64].rearrange("p (a b) -> p a b", a=4)
        mxs = small[:, 32:36]
        v(lambda e: e.tensor_reduce(mxs, l3, AX.X, MAX), t)
        t = v(tt(lgt, l3, bc(mxs.rearrange("p (a b) -> p a b", b=1), 16), SUB))
        allb.free(b, t)
        t = s(act(lgt, lgt, ACT.Exp), t)
        v(lambda e: e.tensor_reduce(mxs, lgt, AX.X, ADD), t)
        v(lambda e: e.reciprocal(mxs, mxs))
        t = v(tt(lgt, lgt, bc(mxs.rearrange("p (a b) -> p a b", b=1), 16), MUL))
        b = allb.take()
        t = pe([tr(PS[b][0:16, 128 * i:128 * i + 128], lgt[:, i, :]) for i in range(4)], t, allb.rel[b])
        t = v(cp(aff[0:16, :], PS[b][0:16, :]), t)
        allb.free(b, t)
        for n in range(8):
            q = slice(8 * n, 8 * n + 8)
            v(lambda e, q=q: e.max(top[0:16, q], aff[0:16, :]))
            v(lambda e, q=q: e.max_index(idxu[0:16, q], top[0:16, q], aff[0:16, :]))
            v(lambda e, q=q: e.match_replace(aff[0:16, :], top[0:16, q], aff[0:16, :], -1.0))
        t = v(cp(idxf[0:16, :], idxu[0:16, :]))
        b = allb.take()
        t0 = allb.rel[b]
        for n, (src, dst) in enumerate(((top, tv8), (idxf, ti8))):
            for hh in range(2):
                em = cons[0:16, C_EM + 64 * hh:C_EM + 64 * hh + 64]
                t = v(tt(two[0:16, n, 64 * hh:64 * hh + 64], src[0:16, :], em, MUL))
            t = pe([mm(PS[b][:, 8 * n:8 * n + 8], two[0:16, n, :], cons[0:16, C_ES:C_ES + 8])], t, t0)
            tr1 = tr2 = v(cp(dst, PS[b][:, 8 * n:8 * n + 8]), t)
            t0 = tr1
        allb.free(b, tr1)
        t = v(cp(ii8, ti8), tr2)
        fe = fence()
        XE = [at(10496 + 1024 * i, 1024) for i in range(2)]
        XT = [at(12544 + 1024 * i, 8, 128) for i in range(2)]
        AC = at(14592, 2048)
        AT = at(16640, 16, 128)
        YE = [at(18688 + 1024 * i, 1024) for i in range(2)]
        PM = [at(20736 + 512 * i, 512) for i in range(2)]
        gb, ub, db, xb_ = Banks([0, 1]), Banks([2, 3]), Banks([4, 5]), Banks([6, 7])
        for x_ in (gb, ub, db, xb_):
            for i in x_.ids:
                x_.rel[i] = allb.rel[i]
        gath = {}
        xerel = [fe, fe]

        def fetch(c):
            gath[c] = gather(XE[c % 2], h_dram, ii8[:, c:c + 1], t, thd, xerel[c % 2], on=f"xe{c % 2}")

        def half_w(name, e, k2, f0):
            return I[name][e, 256 * k2:256 * k2 + 256, f0:f0 + 1024].rearrange("(a p) f -> p a f", p=128)

        def etile(src):
            n, buf, tk_ = ring_next([(2, src)])
            return n, buf.rearrange("p (k c) -> p k c", k=2), tk_

        xtrel = [fe, fe]
        yerel = [fe, fe]
        acrel = atrel = fe
        xtt = {}

        def turn_x(c):
            XEc, XTc = XE[c % 2], XT[c % 2]
            ts_ = []
            for k4 in range(2):
                b = xb_.take()
                t = pe([tr(PS[b][:, 128 * q:128 * q + 128], XEc[:, 512 * k4 + 128 * q:512 * k4 + 128 * q + 128]) for q in range(4)],
                       gath[c], xb_.rel[b])
                xerel[c % 2] = [t]
                for q in range(4):
                    k = 4 * k4 + q
                    t2 = v(colmul(XTc[:, k, :], PS[b][:, 128 * q:128 * q + 128], K_FFN + k), t, xtrel[c % 2])
                xb_.free(b, t2)
                ts_.append(t2)
            xtt[c] = ts_

        fetch(0)
        turn_x(0)
        for c in range(8):
            if c + 1 < 8:
                fetch(c + 1)
            XTc = XT[c % 2]
            tpm = v(ts(PM[c % 2], cons[:, C_IOTA:C_IOTA + 512], ti8[:, c:c + 1], ALU.is_equal, tv8[:, c:c + 1], MUL),
                    tr1, tr2, yerel[c % 2])
            for fh in range(2):
                for nm, bk in (("eg", gb), ("eu", ub)):
                    for k2 in range(4):
                        for e2 in range(2):
                            rn, w, tw = etile(half_w(nm, 2 * c + e2, k2, 1024 * fh))
                            orow = slice(64 * e2, 64 * e2 + 64)
                            fs = []
                            for kk in range(2):
                                k = 2 * k2 + kk
                                for n in range(2):
                                    fs.append(mm(PS[bk.ids[n]][orow, :], XTc[:, k, orow], w[:, kk, 512 * n:512 * n + 512], k == 0, k == 7))
                            t = pe(fs, tw, xtt[c], [bk.rel[i] for i in bk.ids] if k2 == 0 else None)
                            ring_free(rn, t)
                    if nm == "eg":
                        tg_ = t
                        for n in range(2):
                            t = s(act(AC[:, 1024 * fh + 512 * n:1024 * fh + 512 * n + 512], PS[gb.ids[n]][:, :], ACT.Silu), tg_, acrel)
                            gb.free(gb.ids[n], t)
                        tsl = t
                tu_ = t_last = tok(PE)
                for n in range(2):
                    a_ = AC[:, 1024 * fh + 512 * n:1024 * fh + 512 * n + 512]
                    t = v(tt(a_, a_, PS[ub.ids[n]][:, :], MUL), tu_, tsl)
                    ub.free(ub.ids[n], t)
                tac = t
                for f4 in range(2):
                    b = xb_.take()
                    f0 = 8 * fh + 4 * f4
                    t = pe([tr(PS[b][:, 128 * q:128 * q + 128], AC[:, 128 * (f0 + q):128 * (f0 + q) + 128]) for q in range(4)],
                           tac, xb_.rel[b])
                    acrel = [t]
                    t = s(act(AT[:, f0:f0 + 4, :], PS[b][:, :].rearrange("p (a b) -> p a b", a=4), ACT.Copy), t, atrel)
                    xb_.free(b, t)
                tat = t
            xtrel[c % 2] = [tu_]
            if c + 1 < 8:
                turn_x(c + 1)
            for f2 in range(8):
                for e2 in range(2):
                    rn, w, tw = etile(I["ed"][2 * c + e2, 256 * f2:256 * f2 + 256, :].rearrange("(a p) f -> p a f", p=128))
                    orow = slice(64 * e2, 64 * e2 + 64)
                    fs = [mm(PS[db.ids[n]][orow, :], AT[:, 2 * f2 + kk, orow], w[:, kk, 512 * n:512 * n + 512],
                             f2 + kk == 0, f2 == 7 and kk == 1) for kk in range(2) for n in range(2)]
                    t = pe(fs, tw, tat, [db.rel[i] for i in db.ids] if f2 == 0 else None)
                    ring_free(rn, t)
            atrel = [t]
            for n in range(2):
                t2 = s(act(YE[c % 2][:, 512 * n:512 * n + 512], PS[db.ids[n]][:, :], ACT.Copy), t, yerel[c % 2])
                db.free(db.ids[n], t2)
            for i in range(4):
                for n in range(2):
                    b = xb_.take()
                    t = pe([mm(PS[b][:, :], PM[c % 2][:, 128 * i:128 * i + 128], YE[c % 2][:, 512 * n:512 * n + 512])],
                           t2, tpm, xb_.rel[b])
                    yerel[c % 2] = [t]
                    t3 = v(tt(X[:, i, 512 * n:512 * n + 512], X[:, i, 512 * n:512 * n + 512], PS[b][:, :], ADD), t)
                    xb_.free(b, t3)
        for x_ in (gb, ub, db, xb_):
            allb.rel.update(x_.rel)
        if stop == "moe":
            dump(X)
            return finish(nc, ctx, PE, V, S, G, SP, sems)

        fe = fence()
        XN = at(0, 4, 1024)
        hT = at(4096, 8, 512)
        JK = at(8192, 1024)
        rows = at(20480, 2560)
        trw = dma(SP, rows, I["rows"], fe)
        t = rms_rows(X, XN, 4, 1024.0, JK, small[:, 0:4], 1e-6, fe)
        for i in range(4):
            t = v(tt(X[:, i, :], XN[:, i, :], rows[:, 0:1024], MUL), trw)
        t = rms_rows(X, XN, 4, 1024.0, JK, small[:, 4:8], 1e-6, t)
        th = to_feature(XN, hT, 4, K_MIX2, allb, t)
        fe = fence()
        gu = at(8192, 4, 512)
        gv = at(10240, 4, 512)
        qT = at(12288, 4, 512)
        kT = at(14336, 4, 512)
        vt = at(16384, 4, 512)
        ws = at(18432, 8, 128)
        bs_ = at(19456, 8)
        JK2 = at(19584, 512)
        tws = dma(SP, ws, I["wsT"].rearrange("p (a b) -> p a b", a=8), fe)
        tbs = dma(SP, bs_, I["bsT"], fe)
        t = g(tt(ws, ws, cons[:, C_WM:C_WM + 128].rearrange("p (a b) -> p a b", a=1).to_broadcast([128, 8, 128]), MUL), tws)
        twm = t
        tg_, tq_ = [], []
        for n in range(10):
            rn, w, tw = wtile()
            if n < 4 or n >= 8:
                dst = {0: gu, 1: gv, 4: vt}[n // 2]
                for i in range(4):
                    b = allb.take()
                    last = t = proj_t(w, 0, 256, hT, i, PS[b][:, 0:256], b, th, tw)
                    d_ = dst[:, i, 256 * (n % 2):256 * (n % 2) + 256]
                    t = s(act(d_, PS[b][:, 0:256], ACT.Gelu_apprx_tanh if n < 4 else ACT.Copy), t, fe)
                    allb.free(b, t)
                    tg_ = t
            else:
                dst = qT if n < 6 else kT
                for a in range(2):
                    b = allb.take()
                    last = t = proj_f(w, 128 * a, hT, 512, b, th, tw)
                    t = v(cp(dst[:, 2 * (n % 2) + a, :], PS[b][:, :]), t, fe)
                    allb.free(b, t)
                    tq_.append(t)
            ring_free(rn, last)
        t = rms_rows(gv, gv, 4, 512.0, JK2, small[:, 0:4], 1e-6, tg_)
        for i in range(4):
            t = v(tt(gv[:, i, :], gv[:, i, :], rows[:, 2048:2560], MUL), trw)
        for i in range(4):
            b = allb.take()
            t = pe([mm(PS[b][:, 64 * q:64 * q + 64], ws[:, q, :], gv[:, i, 64 * q:64 * q + 64]) for q in range(8)],
                   tok(V), twm, allb.rel[b])
            t = v(tt(JK2.rearrange("p (a b) -> p a b", a=8), PS[b][:, :].rearrange("p (a b) -> p a b", a=8),
                     bc(bs_.rearrange("p (a b) -> p a b", b=1), 64), ADD), t, tbs)
            allb.free(b, t)
            tgu = v(tt(gu[:, i, :], gu[:, i, :], JK2, MUL), tg_)
        fq = fence()
        sq = at(0, 4, 512)
        for arr, kcol, scale in ((qT, K_QN, 0.125), (kT, K_KN, 1.0)):
            t = v(tt(sq, arr, arr, MUL), fq)
            ts_ = []
            t9 = []
            for c in range(4):
                b = allb.take()
                t2 = pe([mm(PS[b][:, :], ones, sq[:, c, :])], t, allb.rel[b])
                t3 = v(ts(sq[:, c, :], PS[b][:, :], 1.0 / 64, MUL, 1e-6, ADD), t2)
                allb.free(b, t3)
                t9.append(s(act(sq[:, c, :], sq[:, c, :], ACT.Sqrt), t3))
            v(lambda e: e.reciprocal(sq, sq), t9)
            v(tt(arr, arr, sq, MUL))
            tqn = v(ts(arr, arr, cols[:, kcol:kcol + 1], MUL, scale, MUL))
        fe = fence()
        aT = at(4096, 8, 512)
        for c in range(4):
            b = allb.take()
            t = pe([tr(PS[b][:, 128 * i:128 * i + 128], gu[:, i, 128 * c:128 * c + 128]) for i in range(4)], tgu, allb.rel[b])
            t = s(act(aT[:, c, :], PS[b][:, :], ACT.Copy), t, fe)
            allb.free(b, t)
        fe = fence()
        PT = [at(8192 + 2048 * i, 4, 512) for i in range(2)]
        ab = at(0, 8, 512)
        tab = dma(SP, ab, I["abias"].rearrange("p (a b) -> p a b", a=8), fe)
        Pb = [at(18432 + 512 * i, 512) for i in range(3)]
        assert 18432 + 1536 <= 20480
        ta2 = attention(8, 4, qT, kT, lambda i: 128 * (i + 1), lambda h, i: ab[:, h, 384 - 128 * i:512], vt, aT[:, 4:8, :],
                        Pb, PT, small[:, 16:32], [tab, fe], causal=True)
        tX = out_proj(aT, fence())
        if stop == "mix2":
            dump(X)
            return finish(nc, ctx, PE, V, S, G, SP, sems)

        fe = fence()
        XN = at(0, 4, 1024)
        hT = at(4096, 8, 512)
        qT = at(8192, 16, 512)
        JK = at(16384, 1024)
        t = rms_rows(X, XN, 4, 1024.0, JK, small[:, 0:4], 1e-6, fe)
        th = to_feature(XN, hT, 4, K_FFN2, allb, t)
        for i in range(4):
            txb = v(tt(XN[:, i, :], XN[:, i, :], rows[:, 1024:2048], MUL), th, tok(PE))
        tq_ = []
        for n in range(8):
            rn, w, tw = wtile()
            for a in range(2):
                b = allb.take()
                last = t = proj_f(w, 128 * a, hT, 512, b, th, tw)
                t = s(act(qT[:, 2 * n + a, :], PS[b][:, :], ACT.Copy), t, fe)
                allb.free(b, t)
                tq_ = t
            ring_free(rn, last)
        fe = fence()
        sk = fl(RING, 16, 128)
        tsk = dma(SP, sk, I["skT"].rearrange("p (a b) -> p a b", a=16), fe)
        sc = fl(RING + 2048, 16, 128)
        cand = fl(RING + 4096, 8, 256)
        st_ = fl(RING + 6144, 16, 16)
        siu = AR_[:, RING + 6400:RING + 6656].bitcast(u32).rearrange("p (a b) -> p a b", a=16)
        sif = fl(RING + 6656, 16, 16)
        best = fl(RING + 6912, 8, 16)
        posu = AR_[:, RING + 7040:RING + 7168].bitcast(u32).rearrange("p (a b) -> p a b", a=8)
        pai = AR_[:, RING + 7168:RING + 7296].bitcast(u32).rearrange("p (a b) -> p a b", a=8)
        paf = fl(RING + 7296, 128)
        pbf = fl(RING + 7424, 128)
        oh = fl(RING + 7552, 128, 16)
        e1 = fl(RING + 9600, 128)
        e2_ = fl(RING + 9728, 128)
        eidx = [AR_[:, D0 + 17408 + 128 * i:D0 + 17408 + 128 * i + 128].bitcast(i32) for i in range(4)]
        gw = at(17920, 4, 128)
        dots = at(18432, 4, 128)
        io16 = cons[:, C_IOTA:C_IOTA + 16].rearrange("p (a b) -> p a b", a=1)
        teidx = []
        for i in range(4):
            for q4 in range(4):
                b = allb.take()
                t = pe([mm(PS[b][:, 128 * q:128 * q + 128], qT[:, 4 * q4 + q, 128 * i:128 * i + 128], sk[:, 4 * q4 + q, :]) for q in range(4)],
                       tq_, tsk, allb.rel[b])
                t = s(act(sc[:, 4 * q4:4 * q4 + 4, :], PS[b][:, :].rearrange("p (a b) -> p a b", a=4), ACT.Copy), t, tok(V))
                allb.free(b, t)
            v(lambda e: e.max(st_[:, 0, 0:8], sc[:, 0, :]), t)
            for q in range(16):
                if q:
                    v(lambda e, q=q: e.max(st_[:, q, 0:8], sc[:, q, :]))
                v(lambda e, q=q: e.max_index(siu[:, q, 0:8], st_[:, q, 0:8], sc[:, q, :]))
                v(lambda e, q=q: e.match_replace(sc[:, q, :], st_[:, q, 0:8], sc[:, q, :], -3.0e38))
                v(lambda e, q=q: e.max(st_[:, q, 8:16], sc[:, q, :]))
                v(lambda e, q=q: e.max_index(siu[:, q, 8:16], st_[:, q, 8:16], sc[:, q, :]))
            v(cp(sif, siu))
            for h in range(8):
                v(tt(cand[:, h, :].rearrange("p (a b) -> p a b", a=16), bc(st_[:, 2 * h, :].rearrange("p (a b) -> p a b", b=1), 16),
                     st_[:, 2 * h + 1, :].rearrange("p (a b) -> p a b", a=1).to_broadcast([128, 16, 16]), ADD))
                v(lambda e, h=h: e.max(best[:, h, 0:8], cand[:, h, :]))
                v(lambda e, h=h: e.max_index(posu[:, h, 0:8], best[:, h, 0:8], cand[:, h, :]))
                v(lambda e, h=h: e.match_replace(cand[:, h, :], best[:, h, 0:8], cand[:, h, :], -3.0e38))
                v(lambda e, h=h: e.max(best[:, h, 8:16], cand[:, h, :]))
                v(lambda e, h=h: e.max_index(posu[:, h, 8:16], best[:, h, 8:16], cand[:, h, :]))
            v(ts(pai, posu, 4, ALU.logical_shift_right))
            v(cp(paf.rearrange("p (a b) -> p a b", a=8), pai))
            v(ts(pai, posu, 15, ALU.bitwise_and))
            v(cp(pbf.rearrange("p (a b) -> p a b", a=8), pai))
            for pf, half_, dst in ((paf, 0, e1), (pbf, 1, e2_)):
                v(tt(oh, bc(pf.rearrange("p (a b) -> p a b", b=1), 16), io16.to_broadcast([128, 128, 16]), ALU.is_equal))
                for h in range(8):
                    v(tt(oh[:, 16 * h:16 * h + 16, :], oh[:, 16 * h:16 * h + 16, :],
                         sif[:, 2 * h + half_, :].rearrange("p (a b) -> p a b", a=1).to_broadcast([128, 16, 16]), MUL))
                v(lambda e, dst=dst: e.tensor_reduce(dst, oh, AX.X, ADD))
            teidx.append(v(stt(eidx[i], e1, 128.0, e2_, MUL, ADD)))
            g3 = gw[:, i, :].rearrange("p (a b) -> p a b", a=8)
            t = v(tt(g3, best, best[:, :, 0:1].to_broadcast([128, 8, 16]), SUB))
            t = s(act(g3, g3, ACT.Exp), t)
            v(lambda e, g3=g3: e.tensor_reduce(small[:, 40:48], g3, AX.X, ADD), t)
            v(lambda e: e.reciprocal(small[:, 40:48], small[:, 40:48]))
            v(tt(g3, g3, bc(small[:, 40:48].rearrange("p (a b) -> p a b", b=1), 16), MUL))
        fe = fence()
        NG = 15
        GB = [fl(RING + 1024 * i, 1024) for i in range(12)] + [at(4096 + 1024 * i, 1024) for i in range(NG - 12)]
        JV = at(8192, 1024)
        gr = {i: fe for i in range(NG)}
        gn = [0]
        plan = []
        for i in range(5):
            if i < 4:
                plan += [("u", i, k) for k in range(128)]
            if i >= 1:
                if i < 4:
                    a_ = plan[-128:]
                    del plan[-128:]
                    for k in range(128):
                        plan += [a_[k], ("v", i - 1, k)]
                else:
                    plan += [("v", i - 1, k) for k in range(128)]
        wtk = {}
        for kind, i, k in plan:
            n = gn[0]
            gn[0] += 1
            sl = n % NG
            buf = GB[sl]
            t = gather(buf, I["peer_u" if kind == "u" else "peer_v"], eidx[i][:, k:k + 1], teidx[i], gr[sl], on=f"gb{sl}")
            if kind == "u":
                t = v(lambda e, buf=buf, i=i, k=k: e.tensor_tensor_reduce(out=JV, in0=buf, in1=XN[:, i, :], scale=1.0, scalar=0.0,
                                                                         op0=MUL, op1=ADD, accum_out=dots[:, i, k:k + 1]), t, txb, fe)
                gr[sl] = t
                if k == 127:
                    t = s(act(dots[:, i, :], dots[:, i, :], ACT.Gelu_apprx_tanh), t)
                    wtk[i] = v(tt(dots[:, i, :], dots[:, i, :], gw[:, i, :], MUL), t)
            else:
                gr[sl] = v(stt(X[:, i, :], buf, dots[:, i, k:k + 1], X[:, i, :], MUL, ADD), t, wtk[i])
        outt = []
        for i in range(4):
            outt.append(dma(SP, O.rearrange("(a p) f -> p a f", p=128)[:, i, :], X[:, i, :], tok(V)))
        finish(nc, ctx, PE, V, S, G, SP, sems)


def finish(nc, ctx, PE, V, S, G, SP, sems):
    block = ctx.enter_context(nc.Block())

    @block.tensor
    def _(e):
        PE.emit(e)

    @block.vector
    def _(e):
        V.emit(e)

    @block.scalar
    def _(e):
        S.emit(e)

    @block.gpsimd
    def _(e):
        G.emit(e)

    @block.sync
    def _(e):
        SP.emit(e)
        for sm, val in sems.values():
            e.wait_ge(sm, val)


def constants():
    c = np.zeros((128, C_END), np.float32)
    p = np.arange(128)
    c[:, 0:128] = np.eye(128)
    same = (p[:, None] // 64) == (p[None, :] // 64)
    c[:, C_ONES:C_ONES + 128] = same
    strict = same & (p[:, None] < p[None, :])
    incl = same & (p[:, None] <= p[None, :])
    for n in range(4):
        c[:, C_M4 + 128 * n:C_M4 + 128 * n + 128] = incl if n % 2 else strict
    for n in range(6):
        b = 2 ** n
        big = (p[:, None] // (2 * b)) == (p[None, :] // (2 * b))
        c[:, C_LVL + 128 * n:C_LVL + 128 * n + 128] = big & ((p[:, None] // b) % 2 == 0) & ((p[None, :] // b) % 2 == 1)
    c[:, C_SCAN:C_SCAN + 512] = (np.arange(512) % 64 != 0)[None, :]
    c[:, C_BD:C_BD + 128] = same
    c[:, C_IOTA:C_IOTA + 512] = np.arange(512)[None, :]
    c[:, C_WM:C_WM + 128] = (p[:, None] // 64) <= (p[None, :] // 64)
    e = np.arange(16)
    c[0:16, C_EM:C_EM + 128] = (e[:, None] % 2) == (p[None, :] // 64)
    c[0:16, C_ES:C_ES + 8] = (e[:, None] // 2) == np.arange(8)[None, :]
    return c


def tiles(w):
    k, n = w.shape
    return w.reshape(k // 128, 128, n // 256, 256).transpose(2, 1, 0, 3).reshape(n // 256, 128, (k // 128) * 256)


def layouts(a):
    f = {k: np.asarray(v) for k, v in a.items()}
    w = f["w_in"][0]
    ch = [w[:, 128 * c:128 * c + 128] for c in range(46)]
    order = list(range(9, 20)) + list(range(0, 9)) + [20, 21]
    gates = []
    br = np.concatenate([f["w_branch_na"][0], f["w_branch_rw"][0], f["w_branch_mem"][0]], 0)
    parts = [tiles(np.concatenate([ch[c] for c in order], 1)), tiles(f["w_mem_kv"][0])]
    for f2 in range(4):
        for b in range(3):
            parts.append(tiles(np.concatenate([ch[22 + 8 * b + 2 * f2], ch[23 + 8 * b + 2 * f2]], 1)))
        parts.append(tiles(br[:, 256 * f2:256 * f2 + 256]))
    parts += [tiles(f["w_out"][0]), tiles(f["w_in_2"][0]), tiles(f["w_out_2"][0]), tiles(f["peer_w_query_2"][0])]
    wt = np.concatenate(parts, 0)

    def col(v, n):
        return v.reshape(n, 128).T
    cols = [col(f["norm_mix_g"][0], 8), col(f["norm_mem_g"][0], 8), col(f["norm_ffn_g"][0], 8), col(f["ln_mix_g_2"][0], 8),
            col(f["ln_ffn_g_2"][0], 8), col(f["rw_mu_rkv"][0].reshape(-1), 18),
            np.concatenate([f["rw_mu_w"][0].T, f["rw_mu_a"][0].T], 0),
            col(f["rw_w0"][0].reshape(-1), 6), col(f["rw_a0"][0].reshape(-1), 6), col(f["rw_k_k"][0], 3), col(f["rw_k_a"][0], 3),
            col(f["rw_r_k"][0].reshape(-1), 3), col(f["rw_ln_g"][0], 3), col(f["rw_ln_b"][0], 3),
            np.concatenate([f["q_norm_g_2"][0]] * 2)[:, None], np.concatenate([f["k_norm_g_2"][0]] * 2)[:, None]]
    cols = np.concatenate(cols, 1)
    low = np.full((1,), -1e30, np.float32)
    c = np.arange(64)
    start = np.clip(c - 8, 0, 48)
    inside = (c[None, :] >= start[:, None]) & (c[None, :] < start[:, None] + 16)
    j = c[None, :] - c[:, None] + 15
    nab = np.zeros((128, 6, 16, 64), np.float32)
    for h in range(6):
        flat_ = np.concatenate([f["na_rpb"][0, h].reshape(-1), low])
        for dr in range(15):
            v = flat_[np.where(inside, dr * 31 + np.clip(j, 0, 30), 15 * 31)]
            nab[0:64, h, dr, :] = v
            nab[64:128, h, dr + 1, :] = v
    p = np.arange(128)[:, None]
    x = np.arange(512)[None, :] - 384
    ok = np.floor_divide(x, 64) <= p // 64
    idx = np.where(ok, np.clip(p - x, -128, 128) + 128, 257)
    abias = np.stack([np.concatenate([f["rel_bias_2"][0, h], low])[idx] for h in range(8)], 1)
    return {
        "x": f["x"][0], "mem": f["mem"][0], "wt": wt, "cols": cols, "consts": constants(),
        "w2a2": np.concatenate([f["rw_w2"][0].transpose(1, 0, 2).reshape(64, 768), f["rw_a2"][0].transpose(1, 0, 2).reshape(64, 768)], 0),
        "g2": f["rw_g2"][0], "nab": nab.reshape(128, 6144), "abias": abias.reshape(128, 4096),
        "rt": f["w_router"][0].reshape(8, 128, 16).transpose(1, 0, 2).reshape(128, 128),
        "eg": f["w_exp_gate"][0], "eu": f["w_exp_up"][0], "ed": f["w_exp_down"][0],
        "rows": np.concatenate([np.broadcast_to(v[None, :], (128, v.shape[0])) for v in
                                (f["norm_final_g"], f["ln_ffn_g_2"][0], f["gmlp_norm_g_2"][0])], 1),
        "wsT": f["gmlp_w_s_2"][0].transpose(2, 0, 1).reshape(128, 1024), "bsT": f["gmlp_b_s_2"][0].T,
        "skT": f["peer_sub_keys_2"][0].reshape(16, 128, 128).transpose(2, 0, 1).reshape(128, 2048),
        "peer_u": f["peer_u_2"][0], "peer_v": f["peer_v_2"][0],
    }


def kernel(**inputs):
    import concourse.bacc as bacc
    from concourse.bass_utils import run_bass_kernel_spmd

    nc = bacc.Bacc("TRN2", target_bir_lowering=False, num_devices=1)
    arrays = {k: np.ascontiguousarray(v) for k, v in layouts(inputs).items()}
    I = {k: nc.dram_tensor("in_" + k, v.shape, mybir.dt.from_np(v.dtype), kind="ExternalInput").ap() for k, v in arrays.items()}
    O = nc.dram_tensor("out_0", (512, 1024), mybir.dt.float32, kind="ExternalOutput").ap()
    block_program(nc, I, O)
    r = run_bass_kernel_spmd(nc, [{"in_" + k: v for k, v in arrays.items()}], core_ids=[0])
    return r.results[0]["out_0"].reshape(1, 512, 1024)
```

```python
import math
from contextlib import ExitStack

import numpy as np

import concourse.bass as bass
from concourse import mybir

NS = 3
PACE, FILL_M = 3.0, 1

C_IDENT, C_ONES, C_M4, C_LVL, C_SCAN, C_BD, C_IOTA, C_WM, C_EM, C_ES, C_END = (
    0, 128, 256, 512, 1280, 1792, 1920, 2432, 2560, 2688, 2696)
(K_MIX, K_MEM, K_FFN, K_MIX2, K_FFN2, K_MU, K_MUWA, K_W0, K_A0, K_KK, K_KA, K_RK, K_LNG, K_LNB, K_QN, K_KN, K_END) = (
    0, 8, 16, 24, 32, 40, 58, 60, 66, 72, 75, 78, 81, 84, 87, 88, 89)


class Queue:

    def __init__(self, sem):
        self.sem, self.n, self.items = sem, 0, []

    def add(self, fns, deps, chain):
        waits = flat(deps)
        if chain and self.n:
            waits.append((self.sem, self.n))
        self.n += 1
        self.items.append((fns, waits, (self.sem, 1)))
        return (self.sem, self.n)

    def emit(self, eng):
        seen = {}
        for fns, waits, (sem, k) in self.items:
            for s, v in waits:
                if seen.get(id(s), 0) < v:
                    eng.wait_ge(s, v)
                    seen[id(s)] = v
            last = None
            for f in fns:
                last = f(eng)
            if last is not None:
                last.then_inc(sem, k)


def flat(deps):
    out = []
    for d in deps:
        if d is None:
            continue
        if len(d) == 2 and isinstance(d[1], int):
            out.append(d)
        else:
            out += flat(d)
    return out


def block_program(nc, I, O, stop=None, dbg=None):
    f32, f32r, i32, u32 = mybir.dt.float32, mybir.dt.float32r, mybir.dt.int32, mybir.dt.uint32
    ACT, ALU, AX = mybir.ActivationFunctionType, mybir.AluOpType, mybir.AxisListType
    ADD, SUB, MUL, MAX = ALU.add, ALU.subtract, ALU.mult, ALU.max
    ctx = ExitStack()
    with ctx:
        def sem(n):
            return ctx.enter_context(nc.semaphore(n))

        TOTAL = 36824
        AR_ = ctx.enter_context(nc.sbuf_tensor("arena", [128, TOTAL], f32))
        tails = []

        def drop(level):
            while len(tails) > level:
                tails.pop().close()
        ctx.callback(drop, 0)

        def tail_is(name, *parts, level=0):
            drop(level)
            tails.append(ExitStack())
            return [tails[-1].enter_context(nc.sbuf_tensor(f"{name}{i}", [128, n], dt)) for i, (n, dt) in enumerate(parts)]

        PS = [ctx.enter_context(nc.psum_tensor(f"ps{i}", [128, 512], f32)) for i in range(8)]
        p_dram = nc.dram_tensor("p_scratch", (128, 35 * 512), f32, kind="Internal").ap()
        h_dram = nc.dram_tensor("h_scratch", (512, 1024), f32, kind="Internal").ap()

        PE, V, S, G, SP = (Queue(sem(f"q_{n}")) for n in ("pe", "dve", "act", "pool", "sp"))

        pace = [0.0, 0.0, None]

        def v(fn, *deps):
            t = V.add([fn], deps, True)
            pace[1] += pace[0]
            while pace[1] >= 1.0 and pace[0]:
                pace[1] -= 1.0
                hold, pace[0] = pace[0], 0.0
                pace[2](1)
                pace[0] = hold
            return t

        def vu(fn, *deps):
            return V.add([fn], deps, False)

        def s(fn, *deps):
            return S.add([fn], deps, True)

        def g(fn, *deps):
            return G.add([fn], deps, True)

        def pe(fns, *deps):
            return PE.add(fns, deps, False)

        nsem = [0]
        sems = {}

        def dma(q, out, in_, *deps, on=None):
            if on is None:
                nsem[0] += 1
                on = f"d{nsem[0]}"
            if on not in sems:
                sems[on] = [sem(on), 0]
            r = sems[on]
            r[1] += 16
            q.items.append(([lambda e: e.dma_start(out, in_)], flat(deps), (r[0], 16)))
            return (r[0], r[1])

        def gather(out, table, idx, *deps, on):
            if on not in sems:
                sems[on] = [sem(on), 0]
            r = sems[on]
            r[1] += 16
            G.items.append(([lambda e: e.indirect_dma_start(out, None, table, bass.IndirectOffsetOnAxis(ap=idx, axis=0))],
                            flat(deps), (r[0], 16)))
            return (r[0], r[1])

        def tok(q):
            return (q.sem, q.n) if q.n else None

        def fence():
            return [tok(PE), tok(V), tok(S), tok(G)]

        def mm(out, l, r, st=True, sp=True):
            return lambda e: e.matmul(out, l, r, start=st, stop=sp, skip_group_check=True)

        def mr(out, l, r, st, sp):
            return lambda e: e.matmul(out, l, r, start=st, stop=sp, skip_group_check=True)

        def tr(out, in_):
            n = in_.shape[0]
            return lambda e: e.transpose(out, in_, ident[0:n, 0:n])

        def tt(o, a, b, op):
            return lambda e: e.tensor_tensor(o, a, b, op)

        def ts(o, a, s1, op, s2=None, op2=None):
            if op2 is None:
                return lambda e: e.tensor_scalar(o, a, s1, None, op)
            return lambda e: e.tensor_scalar(o, a, s1, s2, op, op2)

        def stt(o, a, sc, b, o0, o1):
            return lambda e: e.scalar_tensor_tensor(out=o, in0=a, scalar=sc, in1=b, op0=o0, op1=o1)

        def act(o, a, f, **k):
            return lambda e: e.activation(o, a, f, **k)

        def cp(o, a):
            return lambda e: e.tensor_copy(o, a)

        def bc(ap, n):
            return ap.to_broadcast(list(ap.shape[:-1]) + [n])

        class Banks:
            def __init__(self, ids):
                self.ids, self.at, self.rel = ids, 0, {i: None for i in ids}

            def take(self):
                i = self.ids[self.at % len(self.ids)]
                self.at += 1
                return i

            def free(self, i, *t):
                self.rel[i] = list(t)

        def fl(off, *shape):
            n = int(np.prod(shape))
            assert off + n <= TOTAL, (off, shape)
            a = AR_[:, off:off + n]
            if len(shape) == 1:
                return a
            names = "abcd"[:len(shape)]
            return a.rearrange("p (" + " ".join(names) + ") -> p " + " ".join(names), **dict(zip(names, shape)))

        cons = fl(0, C_END)
        ident = cons[:, 0:128]
        ones = cons[:, C_ONES:C_ONES + 128]
        cols = fl(C_END, K_END)
        o = C_END + 96
        small = fl(o, 192)
        o += 192
        RING = o
        o += NS * 2048
        XO = o
        X = fl(o, 4, 1024)
        o += 4096
        D0 = o
        room = TOTAL - D0

        def at(off, *shape):
            assert off + int(np.prod(shape)) <= room, (off, shape, room)
            return fl(D0 + off, *shape)

        ring_slots = [fl(RING + 2048 * i, 2048) for i in range(NS)]
        ring_rel = [None] * NS
        ring_at = [0]

        def ring_grow(bufs, rel):
            ring_at[0] = ring_at[0] % len(ring_slots)
            ring_slots[ring_at[0]:ring_at[0]] = bufs
            ring_rel[ring_at[0]:ring_at[0]] = [rel] * len(bufs)
            ring_sem[ring_at[0]:ring_at[0]] = [f"ring{NS + i}" for i in range(len(bufs))]

        def ring_shrink():
            for i in reversed(range(len(ring_slots))):
                if int(ring_sem[i][4:]) >= NS:
                    del ring_slots[i], ring_rel[i], ring_sem[i]
            ring_at[0] = 0

        ring_sem = [f"ring{i}" for i in range(NS)]

        def ring_next(parts):
            n = ring_at[0] % len(ring_slots)
            ring_at[0] = n + 1
            buf = ring_slots[n]
            t = None
            for shape, src in parts:
                dst = buf if shape is None else buf.rearrange("p (a b) -> p a b", a=shape)
                t = dma(SP, dst, src, ring_rel[n], on=ring_sem[n])
            return n, buf, t

        def ring_free(n, *t):
            ring_rel[n] = list(t)

        wt_n = [0]

        def wtile():
            t = wt_n[0]
            wt_n[0] += 1
            n, buf, tk = ring_next([(None, I["wt"][t])])
            return n, buf.rearrange("p (k c) -> p k c", k=8), tk

        tc = dma(SP, cons, I["consts"])
        tk = dma(SP, cols, I["cols"])
        tx = dma(SP, X, I["x"].rearrange("(a p) f -> p a f", p=128))

        allb = Banks(list(range(8)))

        def dump(ap, *deps):
            n = int(np.prod(ap.shape[1:]))
            dst = dbg.rearrange("p n -> p n")[:, 0:n]
            if len(ap.shape) == 3:
                dst = dst.rearrange("p (a b) -> p a b", a=ap.shape[1])
            return dma(SP, dst, ap, fence())

        def colmul(out, in_, k0):
            return lambda e: e.tensor_scalar(out, in_, cols[:, k0:k0 + 1], None, MUL)

        def rms_rows(src, dst, nt, width, junk, sc, eps, *deps):
            t = None
            for i in range(nt):
                t = s(act(junk, src[:, i, :], ACT.Square, accum_out=sc[:, i:i + 1]), *deps)
            t = v(ts(sc[:, 0:nt], sc[:, 0:nt], 1.0 / width, MUL, eps, ADD), t)
            t = s(act(sc[:, 0:nt], sc[:, 0:nt], ACT.Sqrt), t)
            t = v(lambda e: e.reciprocal(sc[:, 0:nt], sc[:, 0:nt]), t)
            for i in range(nt):
                t = v(ts(dst[:, i, :], src[:, i, :], sc[:, i:i + 1], MUL), *deps)
            return t

        def to_feature(src, dst, nt, k0, banks, *deps, hl=None):
            last = []
            for c in range(8):
                b = banks.take()
                t = pe([tr(PS[b][:, 128 * i:128 * i + 128], src[:, i, 128 * c:128 * c + 128]) for i in range(nt)],
                       deps, tc, banks.rel[b])
                raw = dst[:, c, :] if hl is None else dst[:, c % 2, :]
                if c % 2 and hl is None:
                    t = v(colmul(raw, PS[b][:, 0:128 * nt], k0 + c), t, tk)
                else:
                    t = s(act(raw, PS[b][:, 0:128 * nt], ACT.Copy, scale=cols[:, k0 + c:k0 + c + 1]), t, tk, last[c - 2] if hl and c > 1 else None)
                banks.free(b, t)
                if hl is not None:
                    t = halve(raw, hl[0][:, c, :], hl[1][:, c, :], t)
                last.append(t)
            return last[-2:]

        def halve(src, hi, lo, *deps, by_act=False):
            t = s(act(hi, src, ACT.Copy), *deps) if by_act else v(cp(hi, src), *deps)
            return v(tt(lo, src, hi.bitcast(f32), SUB), t)

        def product(out, pairs):
            n = len(pairs)
            fs = []
            for k, (l, r) in enumerate(pairs):
                fs += [mr(out, l[0], r[0], k == 0, False), mr(out, l[0], r[1], False, False),
                       mr(out, l[1], r[0], False, k == n - 1)]
            return fs

        class Weights:

            def __init__(self, bufs, width, ntile, rel, by_act=False):
                self.by_act = by_act
                self.bufs, self.width, self.rel = bufs, width, [rel] * len(bufs)
                self.left, self.n, self.tile, self.lo, self.next = ntile, 0, None, 256, None

            def prepare(self):
                if self.lo == 256:
                    if not self.left:
                        self.next = None
                        return
                    self.left -= 1
                    self.tile, self.lo = wtile(), 0
                rn, w, tw = self.tile
                i = self.n % len(self.bufs)
                self.n += 1
                part = w[:, :, self.lo:self.lo + self.width]
                hi, low = self.bufs[i]
                t = halve(part, hi, low, tw, self.rel[i], by_act=self.by_act)
                self.lo += self.width
                self.next = (hi, low, t, i)
                if self.lo == 256:
                    ring_free(rn, t)

            def get(self):
                if self.n == 0:
                    self.prepare()
                r = self.next
                self.prepare()
                return r

            def done(self, r, t):
                self.rel[r[3]] = [t]

        def proj_f(r, rhs, b, *deps):
            hi, lo, tw = r[:3]
            return pe(product(PS[b][:, :], [((hi[:, k, :], lo[:, k, :]), (rhs[0][:, k, :], rhs[1][:, k, :])) for k in range(8)]),
                      tw, deps, allb.rel[b])

        def proj_t(r, lhs, i, b, *deps):
            hi, lo, tw = r[:3]
            q = slice(128 * i, 128 * i + 128)
            return pe(product(PS[b][:, 0:256], [((lhs[0][:, k, q], lhs[1][:, k, q]), (hi[:, k, :], lo[:, k, :])) for k in range(8)]),
                      tw, deps, allb.rel[b])

        def v3(t, a):
            return t[:, :].rearrange("p (a b) -> p a b", a=a)

        F = tail_is("fa", (4096, f32r), (4096, f32r), (4096, f32), *[(1024, f32r)] * 4)
        h2 = (v3(F[0], 8), v3(F[1], 8))
        hT, hL = h2
        EX = F[2]
        HB = [(v3(F[3 + 2 * i], 8), v3(F[4 + 2 * i], 8)) for i in range(2)]
        XN = at(8192, 4, 1024)
        JK = at(12288, 1024)
        FS = at(13312, 2, 512)
        tr1 = rms_rows(X, XN, 4, 1024.0, JK, small[:, 0:4], 1e-6, tx)
        th = to_feature(XN, FS, 4, K_MIX, allb, tr1, hl=h2)

        o = 0
        pr = at(o, 3, 514); o += 1542
        pk = at(o, 3, 514); o += 1542
        pv = at(o, 3, 514); o += 1542
        pw = at(o, 514); o += 514
        lg = at(o, 512); o += 512
        yS = at(o, 3, 512); o += 1536
        bS = at(o, 3, 512); o += 1536
        R = at(o, 3, 512); o += 1536
        K = at(o, 3, 512); o += 1536
        VV = at(o, 3, 512); o += 1536
        T1o = o
        T1 = at(o, 3, 512); o += 1536
        T3 = at(o, 3, 512); o += 1536
        T4 = at(o, 3, 512); o += 1536
        T5 = at(o, 3, 512); o += 1536
        T2 = at(o, 3, 512); o += 1536
        AR = EX[:, 0:3072].rearrange("p (a b c) -> p a b c", a=3, b=4)
        P1, P2 = v3(EX[:, 0:1536], 3), v3(EX[:, 1536:3072], 3)
        W2, G2 = fl(XO, 2, 384), fl(XO, 384)
        m_ = T1o
        M4s = [at(m_, 6, 256), fl(XO, 6, 256)]; m_ += 1536
        Tm = at(m_, 6, 128); m_ += 768
        TT = at(m_, 6, 128); m_ += 768
        X1 = at(m_, 6, 128); m_ += 768
        BT = [at(m_, 6, 128), at(m_ + 768, 6, 128)]; m_ += 1536
        PCM = at(m_, 3, 128); m_ += 384
        PC = at(m_, 3, 8); m_ += 24
        assert m_ <= T1o + 6144
        AToks = [at(o, 4, 384), fl(XO + 1536, 4, 384)]; o += 1536
        SB = [EX[:, 3072:3584], EX[:, 3584:4096]]
        SS = [at(o, 3, 128), at(o + 384, 3, 128)]; o += 768
        Ro = T1o - 4608
        MV, U = at(Ro + 384, 384), at(Ro + 1152, 384)
        Ats = [at(Ro, 3, 128), fl(XO + 3072, 3, 128)]
        U0s = [at(Ro + 768, 384), fl(XO + 3456, 384)]
        te = fence()
        tz = None
        for p in (pr, pk, pv):
            tz = g(lambda e, p=p: e.memset(p[:, :, 0:514:513], 0.0), te)
        tz = g(lambda e: e.memset(pw[:, 0:514:513], 0.0), te)

        dst = [p[:, c, 1:513] for p in (pr, pk, pv) for c in range(3)] + [pw[:, 1:513], lg]
        tp = []
        wa = Weights(HB, 128, 23, te)
        for n in range(11):
            r = wa.get()
            b = allb.take()
            t = proj_f(r, h2, b, th)
            wa.done(r, t)
            t2 = s(act(dst[n], PS[b][:, :], ACT.Copy), t, te)
            allb.free(b, t2)
            tp.append(t2)
        tp = [tp[-1], tp[-2], tz]

        fb = Banks([6, 7])
        for i in fb.ids:
            fb.rel[i] = allb.rel[i]
        spilled = {}

        def spill(slot, src, t, relu):
            spilled[slot] = dma(SP, p_dram[:, 512 * slot:512 * slot + 512], src, t, on=f"sp{relu}")
            return spilled[slot]

        def filler():
            rel = [None, None]
            q = 0
            for n in range(35):
                r = wa.get()
                b = fb.take()
                fs = product(PS[b][:, :], [((r[0][:, k, :], r[1][:, k, :]), (hT[:, k, :], hL[:, k, :])) for k in range(8)])
                for k in range(8):
                    t = pe(fs[3 * k:3 * k + 3], r[2], fb.rel[b] if k == 0 else None)
                    if k < 7:
                        yield
                wa.done(r, t)
                q = 1 - q
                if n >= 11:
                    t = s(act(SB[q], PS[b][:, :], ACT.Sigmoid), t, rel[q])
                else:
                    t = s(act(SB[q], PS[b][:, :], ACT.Copy, scale=0.125 if n < 3 or n >= 9 else 1.0), t, rel[q])
                fb.free(b, t)
                if 6 <= n < 9:
                    yield
                    b = fb.take()
                    t = pe([tr(PS[b][:, 128 * i:128 * i + 128], SB[q][:, 128 * i:128 * i + 128]) for i in range(4)], t, fb.rel[b])
                    rel[q] = [t]
                    q = 1 - q
                    t = s(act(SB[q], PS[b][:, :], ACT.Copy), t, rel[q])
                    fb.free(b, t)
                rel[q] = [spill(n, SB[q], t, q)]
                yield
        fill_g = filler()

        def fill(n):
            for _ in range(n):
                if next(fill_g, 1) == 1:
                    return
        pb = Banks([0, 1, 2, 3, 4, 5])
        pb.rel.update({i: allb.rel[i] for i in range(6)})

        def head_sum(src, nch, use, *deps):
            for c in range(nch):
                b = pb.take()
                t = pe([mm(PS[b][:, :], ones, src(c))], deps, tc, pb.rel[b])
                pb.free(b, use(c, PS[b], t))

        for d in range(2):
            fe = fence()
            tw2 = dma(SP, W2, I["w2a2"].rearrange("p (a b) -> p a b", a=2), fe)
            fw = slice(None, None, None) if d == 0 else slice(None, None, -1)
            lo = 0 if d == 0 else 2
            pace[0], pace[2] = PACE, fill

            def delta(out, p):
                return tt(out, p[:, :, lo:lo + 512], p[:, :, 1:513], SUB)
            v(tt(T5[:, 0, :], pw[:, lo:lo + 512], pw[:, 1:513], SUB), tp, fe)
            tm = v(stt(T5[:, 1, fw], T5[:, 0, :], cols[:, K_MUWA + d:K_MUWA + d + 1], pw[:, 1:513], MUL, ADD), tk)
            t = s(act(T5[0:64, 2, :], T5[0:64, 1, :], ACT.Tanh), tm, fe)
            v(delta(T1, pk), fe)
            for c in range(3):
                k0 = K_MU + (d * 3 + 1) * 3 + c
                tkm = v(stt(K[:, c, fw], T1[:, c, :], cols[:, k0:k0 + 1], pk[:, c, 1:513], MUL, ADD))
            g(delta(P1, pv), tp, fe)
            for c in range(3):
                k0 = K_MU + (d * 3 + 2) * 3 + c
                g(ts(P1[:, c, :], P1[:, c, :], cols[:, k0:k0 + 1], MUL), tk)
            tvm = g(tt(VV[:, :, fw], P1, pv[:, :, 1:513], ADD))
            tsc = []
            for c in range(3):
                b = pb.take()
                t1 = pe([mm(PS[b][:, :], W2[0:64, d, 128 * c:128 * c + 128], T5[0:64, 2, :])], t, tw2, pb.rel[b], fe)
                t2 = s(act(T3[:, c, :], PS[b][:, :], ACT.Sigmoid, bias=cols[:, K_W0 + 3 * d + c:K_W0 + 3 * d + c + 1]), t1)
                pb.free(b, t2)
                b = pb.take()
                t1 = pe([mm(PS[b][:, :], W2[64:128, d, 128 * c:128 * c + 128], T5[64:128, 1, :])], tm, tw2, pb.rel[b])
                t2 = s(act(T2[:, c, :], PS[b][:, :], ACT.Sigmoid, bias=cols[:, K_A0 + 3 * d + c:K_A0 + 3 * d + c + 1]), t1)
                pb.free(b, t2)
                tsc = t2
            for c in range(3):
                tk1 = v(ts(T1[:, c, :], K[:, c, :], cols[:, K_KK + c:K_KK + c + 1], MUL))
            t = v(tt(T5[:, :, :], T1[:, :, :], T1[:, :, :], MUL), tok(PE))
            nr = []

            def use_norm(c, P, t):
                t = s(act(T5[:, c, :], P[:, :], ACT.Sqrt), t)
                nr.append(t)
                return t
            for c in range(3):
                g(ts(P1[:, c, :], T2[:, c, :], 1.0, SUB, cols[:, K_KA + c:K_KA + c + 1], MUL), tsc)
            g(ts(P1, P1, 1.0, ADD))
            tkp = g(tt(K, K, P1, MUL), tk1)
            head_sum(lambda c: T5[:, c, :], 3, use_norm, t)
            v(delta(P2, pr), fe)
            for c in range(3):
                k0 = K_MU + d * 9 + c
                trm = v(stt(R[:, c, fw], P2[:, c, :], cols[:, k0:k0 + 1], pr[:, c, 1:513], MUL, ADD))
            g(tt(P1, R, K, MUL), trm)
            for c in range(3):
                tbp = g(ts(P1[:, c, :], P1[:, c, :], cols[:, K_RK + c:K_RK + c + 1], MUL))
            v(ts(T3[:, :, :], T3[:, :, :], -math.exp(-0.5), MUL), tsc)
            for c in range(3):
                v(lambda e, c=c: e.tensor_tensor_scan(T4[:, c, :], cons[:, C_SCAN:C_SCAN + 512], T3[:, c, :], 0.0, MUL, ADD), tc)
            v(ts(T5[:, :, :], T5[:, :, :], 1e-12, MAX), nr)
            v(lambda e: e.reciprocal(T5[:, :, :], T5[:, :, :]))
            tkn = v(tt(T1[:, :, :], T1[:, :, :], T5[:, :, :], MUL))
            tbh = g(tt(T2, T2, T1, MUL), tkn)
            t = v(tt(T5[:, :, :], T4[:, :, :], T3[:, :, :], SUB))
            te0 = s(act(T5[:, :, :], T5[:, :, :], ACT.Exp), t)
            te1 = s(act(T3[:, :, :], T4[:, :, :], ACT.Exp, scale=-1.0), t)
            te2 = s(act(T4[:, :, :], T4[:, :, :], ACT.Exp), t)

            def use_bonus(c, P, t):
                if d == 0:
                    return v(tt(bS[:, c, :], P[:, :], VV[:, c, :], MUL), t, tvm, fe)
                v(tt(P2[:, c, :], P[:, :], VV[:, c, :], MUL), t, tvm)
                return v(tt(bS[:, c, ::-1], P2[:, c, :], bS[:, c, ::-1], ADD))
            head_sum(lambda c: P1[:, c, :], 3, use_bonus, tbp)
            for c in range(3):
                v(stt(AR[:, c, :, 0:128], T1[:, c, :].rearrange("p (j t) -> p j t", j=4), -1.0,
                      T5[:, c, :].rearrange("p (j t) -> p j t", j=4), MUL, MUL), te0, tok(PE), tkp)
            v(tt(T2[:, :, :], T2[:, :, :], T3[:, :, :], MUL), te1, tbh)
            v(tt(K[:, :, :], K[:, :, :], T3[:, :, :], MUL), tbp)
            for c in range(3):
                v(tt(AR[:, c, :, 128:256], R[:, c, :].rearrange("p (j t) -> p j t", j=4),
                     T4[:, c, :].rearrange("p (j t) -> p j t", j=4), MUL), te2)
            pace[0] = 0.0
            tel = v(cp(PC, T4[:, :, 63:512:64]))
            ts0 = g(lambda e: e.memset(SS[0], 0.0), fe)
            state = {"t": ts0, "cur": 0}
            done = [fe, fe]
            MX = [None]

            def spread(put, out, q, n, *deps):
                k_ = q.stop - q.start
                return put(tt(out[:, q, :].rearrange("p h (x c) -> p h x c", x=2),
                              MX[0][:, q, 0:64].rearrange("p h (x c) -> p h x c", x=1).to_broadcast([128, k_, 2, 64]),
                              cons[:, C_LVL + 128 * n:C_LVL + 128 * n + 128].rearrange("p (h x c) -> p h x c", h=1, x=2)
                              .to_broadcast([128, k_, 2, 64]), MUL), *deps)

            def pair(ap):
                return ap.rearrange("p (a b) -> p a b", a=2)

            def matrix(j):
                jt = slice(128 * j, 128 * j + 128)
                M4, ATok, At, U0 = M4s[j % 2], AToks[j % 2], Ats[j % 2], U0s[j % 2]
                MX[0] = M4
                free = done[j % 2]
                f0 = [tok(V), tok(S), tok(PE)]
                tm4 = []
                for hs in ((0, 2), (1, 3), (4,), (5,)):
                    b = pb.take()
                    fs = []
                    for n, h in enumerate(hs):
                        c, r = h // 2, slice(64 * (h % 2), 64 * (h % 2) + 64)
                        for m, src in enumerate((T2, K)):
                            for q in range(2):
                                lo_ = 256 * n + 128 * m
                                fs.append(mm(PS[b][64 * q:64 * q + 64, lo_:lo_ + 128], src[r, c, 128 * j + 64 * q:128 * j + 64 * q + 64],
                                             AR[r, c, j, :].rearrange("p (a b) -> p a b", a=2)[:, :, 64 * q:64 * q + 64]))
                    t = pe(fs, tel, pb.rel[b])
                    w_ = 256 * len(hs)
                    t = v(tt(M4[:, hs[0]:hs[-1] + 1:2, :], PS[b][:, 0:w_].rearrange("p (a b) -> p a b", b=256),
                             cons[:, C_M4:C_M4 + 256].rearrange("p (a b) -> p a b", a=1).to_broadcast([128, len(hs), 256]), MUL),
                          t, free, f0)
                    tm4.append(t)
                    pb.free(b, t)
                    yield
                for n, src in enumerate((None, T2, K, VV)):
                    b = pb.take()
                    t = pe([tr(PS[b][:, 128 * c:128 * c + 128], AR[:, c, j, 0:128] if src is None else src[:, c, jt])
                            for c in range(3)], tel, pb.rel[b])
                    t = s(act(ATok[:, n, :], PS[b][:, 0:384], ACT.Copy), t, free, f0)
                    pb.free(b, t)
                ttk = t
                yield
                G3 = [slice(2 * k, 2 * k + 2) for k in range(3)]
                tTT, tT = [None] * 3, [None] * 3
                for k, q in enumerate(G3):
                    spread(v, TT, q, 0, f0)
                    tTT[k] = v(tt(TT[:, q, :], TT[:, q, :], ident.rearrange("p (a b) -> p a b", a=1).to_broadcast([128, 2, 128]), ADD))
                for k, q in enumerate(G3):
                    b = pb.take()
                    t = pe([tr(PS[b][:, 128 * a:128 * a + 128], TT[:, 2 * k + a, :]) for a in range(2)], tTT[k], pb.rel[b])
                    tT[k] = s(act(Tm[:, q, :], pair(PS[b][:, 0:256]), ACT.Copy), t)
                    pb.free(b, tT[k])
                    yield
                tread = [f0, f0]
                tb = [None, None]

                def masked(n):
                    tb[n % 2] = spread(g, BT[n % 2], slice(0, 6), n, tm4, tread[n % 2])
                masked(1)
                masked(2)
                for n in range(1, 6):
                    tx1 = []
                    for k, q in enumerate(G3):
                        b = pb.take()
                        t = pe([mm(PS[b][:, 128 * a:128 * a + 128], BT[n % 2][:, 2 * k + a, :], Tm[:, 2 * k + a, :])
                                for a in range(2)], tb[n % 2], tT[k], tTT[k], pb.rel[b])
                        t1 = s(act(X1[:, q, :], pair(PS[b][:, 0:256]), ACT.Copy), t)
                        pb.free(b, t1)
                        tx1.append(t1)
                        yield
                    tread[n % 2] = [t]
                    if n + 2 < 6:
                        masked(n + 2)
                    for k, q in enumerate(G3):
                        b = pb.take()
                        t = pe([mm(PS[b][:, 128 * a:128 * a + 128], X1[:, 2 * k + a, :], TT[:, 2 * k + a, :]) for a in range(2)],
                               tx1[k], pb.rel[b])
                        tTT[k] = v(tt(TT[:, q, :], TT[:, q, :], pair(PS[b][:, 0:256]), ADD), t)
                        pb.free(b, tTT[k])
                        yield
                    if n < 5:
                        for k, q in enumerate(G3):
                            b = pb.take()
                            t = pe([tr(PS[b][:, 128 * a:128 * a + 128], TT[:, 2 * k + a, :]) for a in range(2)], tTT[k], pb.rel[b])
                            tT[k] = s(act(Tm[:, q, :], pair(PS[b][:, 0:256]), ACT.Copy), t)
                            pb.free(b, tT[k])
                            yield
                for q in range(2):
                    r = slice(64 * q, 64 * q + 64)
                    b = pb.take()
                    t = pe([mm(PS[b][r, 64 * h:64 * h + 64], M4[r, h, 128:192], ATok[r, 3, 64 * h:64 * h + 64]) for h in range(6)],
                           tm4, ttk, pb.rel[b])
                    t = s(act(MV[r, :], PS[b][r, 0:384], ACT.Copy), t, f0)
                    pb.free(b, t)
                yield
                b = pb.take()
                t = pe([mm(PS[b][64 * (h % 2):64 * (h % 2) + 64, 128 * (h // 2):128 * (h // 2) + 128],
                           ATok[:, 0, 64 * h:64 * h + 64], TT[:, h, :]) for h in range(6)], tTT, pb.rel[b])
                tat = s(act(At, PS[b][:, 0:384].rearrange("p (a b) -> p a b", a=3), ACT.Copy), t, free)
                pb.free(b, tat)
                yield
                b = pb.take()
                t = pe([mm(PS[b][:, 64 * h:64 * h + 64], TT[:, h, :], MV[:, 64 * h:64 * h + 64]) for h in range(6)],
                       tok(S), pb.rel[b])
                tu0 = s(act(U0, PS[b][:, 0:384], ACT.Copy), t, free)
                pb.free(b, tu0)
                state[j] = (tat, tu0)
                yield

            def chunks(j):
                M4, ATok, At, U0 = M4s[j % 2], AToks[j % 2], Ats[j % 2], U0s[j % 2]
                tat, tu0 = state[j]
                for q in range(2):
                    n = 2 * j + q
                    r = slice(64 * q, 64 * q + 64)
                    S0, S1 = SS[state["cur"]], SS[1 - state["cur"]]
                    tpc = g(tt(PCM, cons[:, C_BD:C_BD + 128].rearrange("p (a b) -> p a b", a=1).to_broadcast([128, 3, 128]),
                               PC[:, :, n:n + 1].to_broadcast([128, 3, 128]), MUL), tel, tok(V))
                    b = pb.take()
                    t = pe([mm(PS[b][r, 128 * p:128 * p + 128], At[:, p, r], S0[:, p, :]) for p in range(3)],
                           tat, state["t"], pb.rel[b])
                    tu = v(tt(U[r, :], PS[b][r, 0:384], U0[r, :], ADD), t, tu0)
                    pb.free(b, tu)
                    yield
                    b = pb.take()
                    fs = []
                    for p in range(3):
                        pc = slice(128 * p, 128 * p + 128)
                        fs += [mm(PS[b][:, pc], ATok[r, 1, pc], U[r, pc], True, False),
                               mm(PS[b][:, pc], ATok[r, 2, pc], ATok[r, 3, pc], False, True)]
                    t = pe(fs, tu, pb.rel[b])
                    v(tt(S1, PS[b][:, 0:384].rearrange("p (a b) -> p a b", a=3), S0, ADD), t)
                    state["t"] = v(tt(S1, S1, PCM, MUL), tpc)
                    pb.free(b, state["t"])
                    yield
                    b = pb.take()
                    fs = []
                    for p in range(3):
                        oc = slice(64 * p, 64 * p + 64)
                        fs.append(mm(PS[b][:, oc], S0[:, p, :], AR[:, p, j, 128 + 64 * q:192 + 64 * q], True, False))
                        for e2 in range(2):
                            h = 2 * p + e2
                            orow = slice(64 * e2, 64 * e2 + 64)
                            fs.append(mm(PS[b][orow, oc], U[r, 64 * h:64 * h + 64], M4[r, h, 64:128], False, False))
                            fs.append(mm(PS[b][orow, oc], ATok[r, 3, 64 * h:64 * h + 64], M4[r, h, 192:256], False, True))
                    t = pe(fs, pb.rel[b])
                    done[j % 2] = [t]
                    src = PS[b][:, 0:192].rearrange("p (a b) -> p a b", a=3)
                    if d == 0:
                        t = s(act(yS[:, :, 64 * n:64 * n + 64], src, ACT.Copy), t, fe)
                    else:
                        o_ = yS[:, :, 448 - 64 * n:512 - 64 * n]
                        t = v(tt(o_[:, :, ::-1], src, o_[:, :, ::-1], ADD), t)
                    pb.free(b, t)
                    state["cur"] = 1 - state["cur"]
                    yield

            before = iter(())
            for j in range(4):
                for n, _ in enumerate(matrix(j)):
                    if n % 5 == 4:
                        next(before, None)
                    if n % 3 == 2:
                        fill(FILL_M)
                for _ in before:
                    fill(1)
                before = chunks(j)
            for _ in before:
                fill(2)

        for _ in fill_g:
            pass
        fe = fence()
        tg2 = dma(SP, G2, I["g2"], fe)

        def use_mean(c, P, t):
            t = v(stt(T1[:, c, :], P[:, :], -1.0 / 64, yS[:, c, :], MUL, ADD), t, fe)
            return v(tt(T3[:, c, :], T1[:, c, :], T1[:, c, :], MUL))
        head_sum(lambda c: yS[:, c, :], 3, use_mean, fe)
        rs = []

        def use_var(c, P, t):
            t = v(ts(T4[:, c, :], P[:, :], 1.0 / 64, MUL, 64e-5, ADD), t)
            t2 = s(act(T4[:, c, :], T4[:, c, :], ACT.Sqrt), t)
            rs.append(t2)
            return t
        head_sum(lambda c: T3[:, c, :], 3, use_var, tok(V))
        v(lambda e: e.reciprocal(T4[:, :, :], T4[:, :, :]), rs)
        v(tt(T1[:, :, :], T1[:, :, :], T4[:, :, :], MUL))
        for c in range(3):
            v(ts(T1[:, c, :], T1[:, c, :], cols[:, K_LNG + c:K_LNG + c + 1], MUL, cols[:, K_LNB + c:K_LNB + c + 1], ADD))
        ty = v(tt(T1[:, :, :], T1[:, :, :], bS[:, :, :], ADD))
        tg = s(act(T5[:, 0, :], lg, ACT.Sigmoid), fe)
        for c in range(3):
            b = pb.take()
            t = pe([mm(PS[b][:, :], G2[:, 128 * c:128 * c + 128], T5[:, 0, :])], tg, tg2, pb.rel[b])
            t = v(tt(yS[:, c, :], T1[:, c, :], PS[b][:, :], MUL), t)
            pb.free(b, t)
        allb.rel.update(pb.rel)
        allb.rel.update(fb.rel)
        if stop == "rw":
            dump(yS)
            return finish(nc, ctx, PE, V, S, G, SP, sems)

        YO = room - 4096 - 1536
        yR = at(YO, 3, 512)
        yN = at(YO + 1536, 3, 512)
        yM = at(YO + 3072, 2, 512)
        fe = fence()
        tyr = g(cp(yR, yS), fe)
        fe = fence()
        o = 0
        qT = at(o, 3, 512); o += 1536
        kT = at(o, 3, 512); o += 1536
        vt = at(o, 4, 384); o += 1536
        nb = at(o, 6, 1024); o += 6144
        Pb = [at(o + 512 * i, 512) for i in range(4)]; o += 2048
        PT = [at(o + 2048 * i, 4, 512) for i in range(2)]; o += 4096
        mq = at(o, 2, 512); o += 1024
        assert o <= YO
        tnb = dma(SP, nb, I["nab"].rearrange("p (a b) -> p a b", a=6), fe)
        tqk = [dma(SP, qT, p_dram[:, 0:1536].rearrange("p (a b) -> p a b", a=3), fe, [spilled[i] for i in range(3)]),
               dma(SP, kT, p_dram[:, 1536:3072].rearrange("p (a b) -> p a b", a=3), fe, [spilled[i] for i in range(3, 6)]),
               dma(SP, mq, p_dram[:, 4608:5632].rearrange("p (a b) -> p a b", a=2), fe, [spilled[i] for i in (9, 10)])]
        for c in range(3):
            tqk.append(dma(SP, vt[:, :, 128 * c:128 * c + 128],
                           p_dram[:, 3072 + 512 * c:3584 + 512 * c].rearrange("p (a b) -> p a b", a=4), fe, spilled[6 + c]))

        def attention(nh, ntile, q_, k_, nk, bias, v_, out, Pb, PT, sm, deps, causal=False):
            sb_ = Banks([0, 1, 2])
            tb_ = Banks([3, 4, 5])
            ob_ = Banks([6, 7])
            for x_ in (sb_, tb_, ob_):
                for i in x_.ids:
                    x_.rel[i] = allb.rel[i]
            units = [(h, i) for h in range(nh) for i in range(ntile)]
            prel = [None] * 4
            ptrel = [None] * 2
            info = {}
            ptt = {}

            def scores(u):
                h, i = units[u]
                r = slice(64 * (h % 2), 64 * (h % 2) + 64)
                b = sb_.take()
                n = nk(i)
                t = pe([mm(PS[b][:, 0:n], q_[r, h // 2, 128 * i:128 * i + 128], k_[r, h // 2, 0:n])], deps, sb_.rel[b])
                P = Pb[u % 4][:, 0:n]
                m = sm[:, u % 8:u % 8 + 1]
                l = sm[:, 8 + u % 8:9 + u % 8]
                if bias is not None:
                    t = v(lambda e: e.tensor_tensor_reduce(out=P, in0=PS[b][:, 0:n], in1=bias(h, i), scale=-1.0, scalar=3.0e38,
                                                           op0=ADD, op1=ALU.min, accum_out=m), t, prel[u % 4])
                    sb_.free(b, t)
                    t = s(act(P, P, ACT.Exp, bias=m, scale=-1.0, accum_out=l), t)
                else:
                    t = v(lambda e: e.tensor_reduce(m, PS[b][:, 0:n], AX.X, MAX, negate=True), t)
                    t = s(act(P, PS[b][:, 0:n], ACT.Exp, bias=m, accum_out=l), t, prel[u % 4])
                    sb_.free(b, t)
                info[u] = (P, l, t)

            def norm(u):
                P, l, t = info[u]
                v(lambda e: e.reciprocal(l, l), t)
                info[u] = v(ts(P, P, l, MUL))

            def turn(u):
                h, i = units[u]
                P = Pb[u % 4]
                n = nk(i) // 128
                b = tb_.take()
                t = pe([tr(PS[b][:, 128 * k:128 * k + 128], P[:, 128 * k:128 * k + 128]) for k in range(n)], info[u], tb_.rel[b])
                prel[u % 4] = t
                t = s(act(PT[h % 2][:, 0:n, 128 * i:128 * i + 128], PS[b][:, 0:128 * n].rearrange("p (a b) -> p a b", a=n), ACT.Copy),
                      t, ptrel[h % 2])
                tb_.free(b, t)
                if i == ntile - 1:
                    nkc = nk(ntile - 1) // 128
                    if h % 2 == 0:
                        info["o"] = ob_.take()
                    b = info["o"]
                    orow = slice(64 * (h % 2), 64 * (h % 2) + 64)
                    lo = (lambda k: 128 * k) if causal else (lambda k: 0)
                    t = pe([mm(PS[b][orow, lo(k):512], v_[:, k, 64 * h:64 * h + 64], PT[h % 2][:, k, lo(k):512], k == 0, k == nkc - 1)
                            for k in range(nkc)], t, ob_.rel[b])
                    ptrel[h % 2] = t
                    if h % 2:
                        t = v(cp(out[:, h // 2, :], PS[b][:, :]), t)
                        ob_.free(b, t)
                        info["y"] = t
            for u in range(len(units) + 3):
                if u < len(units):
                    scores(u)
                if 1 <= u <= len(units):
                    norm(u - 1)
                if u >= 3:
                    turn(u - 3)
            for x_ in (sb_, tb_, ob_):
                allb.rel.update(x_.rel)
            return info["y"]

        ty1 = attention(6, 4, qT, kT, lambda i: 512, lambda h, i: nb[:, h, 64 * (7 - 2 * i):64 * (7 - 2 * i) + 512] , vt, yN,
                        Pb, PT, small[:, 16:32], [tqk, tnb])
        if stop == "na":
            dump(yN)
            return finish(nc, ctx, PE, V, S, G, SP, sems)

        fe = fence()
        o = 0
        mx = at(o, 2, 1024); o += 2048
        mT = at(o, 8, 256); o += 2048
        mj = at(o, 1024); o += 1024
        mk = at(o, 2, 256); o += 512
        mv = at(o, 2, 256); o += 512
        assert o <= 3 * 1536 + 6144
        tmx = dma(SP, mx, I["mem"].rearrange("(a p) f -> p a f", p=128), fe)
        t = rms_rows(mx, mx, 2, 1024.0, mj, small[:, 4:8], 1e-6, tmx)
        tmt = to_feature(mx, mT, 2, K_MEM, allb, t)
        tkv = []
        rn, w, tw = wtile()
        for a in range(2):
            b = allb.take()
            last = t = pe([mm(PS[b][:, 0:256], w[:, k, 128 * a:128 * a + 128], mT[:, k, :], k == 0, k == 7) for k in range(8)],
                          tmt, tw, allb.rel[b])
            t = v(cp(mk[:, a, :], PS[b][:, 0:256]), t, fe)
            allb.free(b, t)
            tkv.append(t)
        ring_free(rn, last)
        rn, w, tw = wtile()
        for a in range(2):
            b = allb.take()
            last = t = pe([mm(PS[b][:, 0:256], mT[:, k, 128 * a:128 * a + 128], w[:, k, :], k == 0, k == 7) for k in range(8)],
                          tmt, tw, allb.rel[b])
            t = v(cp(mv[:, a, :], PS[b][:, 0:256]), t, fe)
            allb.free(b, t)
            tkv.append(t)
        ring_free(rn, last)
        ty2 = attention(4, 4, mq, mk, lambda i: 256, None, mv, yM, Pb, PT, small[:, 16:32], [tqk, tkv])
        if stop == "mem":
            dump(yM)
            return finish(nc, ctx, PE, V, S, G, SP, sems)

        fe = fence()
        mg = at(0, 8, 512)
        sgs = at(4096, 24, 512)
        tsg = [dma(SP, sgs[:, 6 * f2:6 * f2 + 6, :], p_dram[:, 512 * (11 + 6 * f2):512 * (17 + 6 * f2)].rearrange("p (a b) -> p a b", a=6),
                   fe, [spilled[11 + 6 * f2 + i] for i in range(6)]) for f2 in range(4)]
        txx = dma(SP, X, I["x"].rearrange("(a p) f -> p a f", p=128), fe)
        F = tail_is("fb", (4096, f32r), (4096, f32r), *[(2048, f32r)] * 4)
        YH, YL = v3(F[0], 8), v3(F[1], 8)
        HB2 = [(v3(F[2 + 2 * i], 8), v3(F[3 + 2 * i], 8)) for i in range(2)]
        ty = []
        for n, (src, k0, kn) in enumerate(((yN, 0, 3), (yR, 3, 3), (yM, 6, 2))):
            ty.append(halve(src, YH[:, k0:k0 + kn, :], YL[:, k0:k0 + kn, :], fe))
        kc0 = (0, 3, 6)
        kcn = (3, 3, 2)
        wb = Weights(HB2, 256, 8, fe)
        tmg = []
        for f2 in range(4):
            sg = [sgs[:, 6 * f2 + i, :] for i in range(6)]
            r = wb.get()
            for a in range(2):
                f = 2 * f2 + a
                for br in range(3):
                    b = allb.take()
                    q = slice(128 * a, 128 * a + 128)
                    last = t = pe(product(PS[b][:, :], [((r[0][:, k, q], r[1][:, k, q]), (YH[:, k, :], YL[:, k, :]))
                                                        for k in range(kc0[br], kc0[br] + kcn[br])]), r[2], ty, allb.rel[b])
                    if br == 0:
                        t = v(tt(mg[:, f, :], sg[a], PS[b][:, :], MUL), t, tsg[f2], fe)
                    else:
                        t = v(tt(sg[2 * br + a], sg[2 * br + a], PS[b][:, :], MUL), t, tsg[f2])
                    allb.free(b, t)
                v(tt(mg[:, f, :], mg[:, f, :], sg[2 + a], ADD))
                t = v(tt(mg[:, f, :], mg[:, f, :], sg[4 + a], ADD))
            wb.done(r, last)
        tmg = halve(mg, YH, YL, fence())

        def out_proj(wb, src, *deps):
            t = None
            for n in range(4):
                r = wb.get()
                for i in range(4):
                    b = allb.take()
                    last = t = proj_t(r, src, i, b, deps)
                    t = v(tt(X[:, i, 256 * n:256 * n + 256], X[:, i, 256 * n:256 * n + 256], PS[b][:, 0:256], ADD), t)
                    allb.free(b, t)
                wb.done(r, last)
            return t
        tX = out_proj(wb, (YH, YL), tmg, txx)
        if stop == "mix1":
            dump(X)
            return finish(nc, ctx, PE, V, S, G, SP, sems)

        fe = fence()
        XN = at(0, 4, 1024)
        hT = at(4096, 8, 512)
        JK = at(8192, 1024)
        rt = at(9216, 8, 16)
        lgt = at(9344, 4, 16)
        aff = at(9408, 512)
        top = at(9920, 64)
        idxu = AR_[:, D0 + 9984:D0 + 10048].bitcast(u32)
        idxf = at(10048, 64)
        tv8 = at(10112, 8)
        ti8 = at(10120, 8)
        ii8 = AR_[:, D0 + 10128:D0 + 10136].bitcast(i32)
        two = at(10144, 2, 128)
        trt = dma(SP, rt, I["rt"].rearrange("p (a b) -> p a b", a=8), fe)
        t = rms_rows(X, XN, 4, 1024.0, JK, small[:, 0:4], 1e-6, fe)
        thd = dma(G, h_dram.rearrange("(a p) f -> p a f", p=128), XN, t)
        th = to_feature(XN, hT, 4, K_FFN, allb, t)
        b = allb.take()
        t = pe([mm(PS[b][:, 16 * i:16 * i + 16], hT[:, k, 128 * i:128 * i + 128], rt[:, k, :], k == 0, k == 7)
                for i in range(4) for k in range(8)], th, trt, allb.rel[b])
        l3 = PS[b][:, 0:64].rearrange("p (a b) -> p a b", a=4)
        mxs = small[:, 32:36]
        v(lambda e: e.tensor_reduce(mxs, l3, AX.X, MAX), t)
        t = v(tt(lgt, l3, bc(mxs.rearrange("p (a b) -> p a b", b=1), 16), SUB))
        allb.free(b, t)
        t = s(act(lgt, lgt, ACT.Exp), t)
        v(lambda e: e.tensor_reduce(mxs, lgt, AX.X, ADD), t)
        v(lambda e: e.reciprocal(mxs, mxs))
        t = v(tt(lgt, lgt, bc(mxs.rearrange("p (a b) -> p a b", b=1), 16), MUL))
        b = allb.take()
        t = pe([tr(PS[b][0:16, 128 * i:128 * i + 128], lgt[:, i, :]) for i in range(4)], t, allb.rel[b])
        t = v(cp(aff[0:16, :], PS[b][0:16, :]), t)
        allb.free(b, t)
        for n in range(8):
            q = slice(8 * n, 8 * n + 8)
            v(lambda e, q=q: e.max(top[0:16, q], aff[0:16, :]))
            v(lambda e, q=q: e.max_index(idxu[0:16, q], top[0:16, q], aff[0:16, :]))
            v(lambda e, q=q: e.match_replace(aff[0:16, :], top[0:16, q], aff[0:16, :], -1.0))
        t = v(cp(idxf[0:16, :], idxu[0:16, :]))
        b = allb.take()
        t0 = allb.rel[b]
        for n, (src, dst) in enumerate(((top, tv8), (idxf, ti8))):
            for hh in range(2):
                em = cons[0:16, C_EM + 64 * hh:C_EM + 64 * hh + 64]
                t = v(tt(two[0:16, n, 64 * hh:64 * hh + 64], src[0:16, :], em, MUL))
            t = pe([mm(PS[b][:, 8 * n:8 * n + 8], two[0:16, n, :], cons[0:16, C_ES:C_ES + 8])], t, t0)
            tr1 = tr2 = v(cp(dst, PS[b][:, 8 * n:8 * n + 8]), t)
            t0 = tr1
        allb.free(b, tr1)
        t = v(cp(ii8, ti8), tr2)
        fe = fence()
        XE = [at(10496 + 1024 * i, 1024) for i in range(2)]
        XT = [at(12544 + 1024 * i, 8, 128) for i in range(2)]
        AC = at(14592, 2048)
        AT = at(16640, 16, 128)
        YE = [at(18688 + 1024 * i, 1024) for i in range(2)]
        PM = [at(20736 + 512 * i, 512) for i in range(2)]
        gb, ub, db, xb_ = Banks([0, 1]), Banks([2, 3]), Banks([4, 5]), Banks([6, 7])
        for x_ in (gb, ub, db, xb_):
            for i in x_.ids:
                x_.rel[i] = allb.rel[i]
        gath = {}
        xerel = [fe, fe]

        def fetch(c):
            gath[c] = gather(XE[c % 2], h_dram, ii8[:, c:c + 1], t, thd, xerel[c % 2], on=f"xe{c % 2}")

        def half_w(name, e, k2, f0):
            return I[name][e, 256 * k2:256 * k2 + 256, f0:f0 + 1024].rearrange("(a p) f -> p a f", p=128)

        def etile(src):
            n, buf, tk_ = ring_next([(2, src)])
            return n, buf.rearrange("p (k c) -> p k c", k=2), tk_

        F = tail_is("ga", (16384, f32))
        ring_grow([F[0][:, 2048 * i:2048 * i + 2048] for i in range(8)], fe)
        xtrel = [fe, fe]
        yerel = [fe, fe]
        acrel = atrel = fe
        xtt = {}

        def turn_x(c):
            XEc, XTc = XE[c % 2], XT[c % 2]
            ts_ = []
            for k4 in range(2):
                b = xb_.take()
                t = pe([tr(PS[b][:, 128 * q:128 * q + 128], XEc[:, 512 * k4 + 128 * q:512 * k4 + 128 * q + 128]) for q in range(4)],
                       gath[c], xb_.rel[b])
                xerel[c % 2] = [t]
                for q in range(4):
                    k = 4 * k4 + q
                    t2 = v(colmul(XTc[:, k, :], PS[b][:, 128 * q:128 * q + 128], K_FFN + k), t, xtrel[c % 2])
                xb_.free(b, t2)
                ts_.append(t2)
            xtt[c] = ts_

        fetch(0)
        turn_x(0)
        for c in range(8):
            if c + 1 < 8:
                fetch(c + 1)
            XTc = XT[c % 2]
            tpm = v(ts(PM[c % 2], cons[:, C_IOTA:C_IOTA + 512], ti8[:, c:c + 1], ALU.is_equal, tv8[:, c:c + 1], MUL),
                    tr1, tr2, yerel[c % 2])
            for fh in range(2):
                for nm, bk in (("eg", gb), ("eu", ub)):
                    for k2 in range(4):
                        for e2 in range(2):
                            rn, w, tw = etile(half_w(nm, 2 * c + e2, k2, 1024 * fh))
                            orow = slice(64 * e2, 64 * e2 + 64)
                            fs = []
                            for kk in range(2):
                                k = 2 * k2 + kk
                                for n in range(2):
                                    fs.append(mm(PS[bk.ids[n]][orow, :], XTc[:, k, orow], w[:, kk, 512 * n:512 * n + 512], k == 0, k == 7))
                            t = pe(fs, tw, xtt[c], [bk.rel[i] for i in bk.ids] if k2 == 0 else None)
                            ring_free(rn, t)
                    if nm == "eg":
                        tg_ = t
                        for n in range(2):
                            t = s(act(AC[:, 1024 * fh + 512 * n:1024 * fh + 512 * n + 512], PS[gb.ids[n]][:, :], ACT.Silu), tg_, acrel)
                            gb.free(gb.ids[n], t)
                        tsl = t
                tu_ = t_last = tok(PE)
                for n in range(2):
                    a_ = AC[:, 1024 * fh + 512 * n:1024 * fh + 512 * n + 512]
                    t = v(tt(a_, a_, PS[ub.ids[n]][:, :], MUL), tu_, tsl)
                    ub.free(ub.ids[n], t)
                tac = t
                for f4 in range(2):
                    b = xb_.take()
                    f0 = 8 * fh + 4 * f4
                    t = pe([tr(PS[b][:, 128 * q:128 * q + 128], AC[:, 128 * (f0 + q):128 * (f0 + q) + 128]) for q in range(4)],
                           tac, xb_.rel[b])
                    acrel = [t]
                    t = s(act(AT[:, f0:f0 + 4, :], PS[b][:, :].rearrange("p (a b) -> p a b", a=4), ACT.Copy), t, atrel)
                    xb_.free(b, t)
                tat = t
            xtrel[c % 2] = [tu_]
            if c + 1 < 8:
                turn_x(c + 1)
            for f2 in range(8):
                for e2 in range(2):
                    rn, w, tw = etile(I["ed"][2 * c + e2, 256 * f2:256 * f2 + 256, :].rearrange("(a p) f -> p a f", p=128))
                    orow = slice(64 * e2, 64 * e2 + 64)
                    fs = [mm(PS[db.ids[n]][orow, :], AT[:, 2 * f2 + kk, orow], w[:, kk, 512 * n:512 * n + 512],
                             f2 + kk == 0, f2 == 7 and kk == 1) for kk in range(2) for n in range(2)]
                    t = pe(fs, tw, tat, [db.rel[i] for i in db.ids] if f2 == 0 else None)
                    ring_free(rn, t)
            atrel = [t]
            for n in range(2):
                t2 = s(act(YE[c % 2][:, 512 * n:512 * n + 512], PS[db.ids[n]][:, :], ACT.Copy), t, yerel[c % 2])
                db.free(db.ids[n], t2)
            for i in range(4):
                for n in range(2):
                    b = xb_.take()
                    t = pe([mm(PS[b][:, :], PM[c % 2][:, 128 * i:128 * i + 128], YE[c % 2][:, 512 * n:512 * n + 512])],
                           t2, tpm, xb_.rel[b])
                    yerel[c % 2] = [t]
                    t3 = v(tt(X[:, i, 512 * n:512 * n + 512], X[:, i, 512 * n:512 * n + 512], PS[b][:, :], ADD), t)
                    xb_.free(b, t3)
        for x_ in (gb, ub, db, xb_):
            allb.rel.update(x_.rel)
        ring_shrink()
        if stop == "moe":
            dump(X)
            return finish(nc, ctx, PE, V, S, G, SP, sems)

        fe = fence()
        XN = at(0, 4, 1024)
        F = tail_is("fc", (4096, f32r), (4096, f32r), *[(2048, f32r)] * 4)
        h2 = (v3(F[0], 8), v3(F[1], 8))
        HB2 = [(v3(F[2 + 2 * i], 8), v3(F[3 + 2 * i], 8)) for i in range(2)]
        aT = at(4096, 8, 512)
        sq = at(4096, 4, 512)
        JK = at(6144, 1024)
        FS = at(7168, 2, 512)
        rows = at(20480, 2560)
        gu = at(8192, 4, 512)
        gv = at(10240, 4, 512)
        qT = at(12288, 4, 512)
        kT = at(14336, 4, 512)
        vt = at(16384, 4, 512)
        ws = at(18432, 8, 128)
        bs_ = at(19456, 8)
        JK2 = at(19584, 512)
        trw = dma(SP, rows, I["rows"], fe)
        tws = dma(SP, ws, I["wsT"].rearrange("p (a b) -> p a b", a=8), fe)
        tbs = dma(SP, bs_, I["bsT"], fe)
        t = rms_rows(X, XN, 4, 1024.0, JK, small[:, 0:4], 1e-6, fe)
        for i in range(4):
            t = v(tt(X[:, i, :], XN[:, i, :], rows[:, 0:1024], MUL), trw)
        t = rms_rows(X, XN, 4, 1024.0, JK, small[:, 4:8], 1e-6, t)
        wb = Weights(HB2, 256, 14, fence())
        th = to_feature(XN, FS, 4, K_MIX2, allb, t, hl=h2)
        twm = g(tt(ws, ws, cons[:, C_WM:C_WM + 128].rearrange("p (a b) -> p a b", a=1).to_broadcast([128, 8, 128]), MUL), tws)

        def rows_of(dst, n, func):
            r = wb.get()
            for i in range(4):
                b = allb.take()
                t = proj_t(r, h2, i, b, th)
                t2 = s(act(dst[:, i, 256 * n:256 * n + 256], PS[b][:, 0:256], func), t, fe)
                allb.free(b, t2)
            wb.done(r, t)
            return t2

        def features_of(dst, n):
            r = wb.get()
            for a in range(2):
                b = allb.take()
                q = slice(128 * a, 128 * a + 128)
                t = proj_f((r[0][:, :, q], r[1][:, :, q], r[2]), h2, b, th)
                t2 = s(act(dst[:, 2 * n + a, :], PS[b][:, :], ACT.Copy), t, fe)
                allb.free(b, t2)
            wb.done(r, t)
            return t2

        def head_norm(arr, kcol, scale, tin):
            t = v(tt(sq, arr, arr, MUL), tin, tok(PE))
            t9 = []
            for c in range(4):
                b = allb.take()
                t2 = pe([mm(PS[b][:, :], ones, sq[:, c, :])], t, allb.rel[b])
                t3 = v(ts(sq[:, c, :], PS[b][:, :], 1.0 / 64, MUL, 1e-6, ADD), t2)
                allb.free(b, t3)
                t9.append(s(act(sq[:, c, :], sq[:, c, :], ACT.Sqrt), t3))
            v(lambda e: e.reciprocal(sq, sq), t9)
            v(tt(arr, arr, sq, MUL))
            return v(ts(arr, arr, cols[:, kcol:kcol + 1], MUL, scale, MUL))

        for n in range(2):
            tgv = rows_of(gv, n, ACT.Gelu_apprx_tanh)
        for n in range(2):
            tgu_ = rows_of(gu, n, ACT.Gelu_apprx_tanh)
        ab = at(0, 8, 512)
        tab = dma(SP, ab, I["abias"].rearrange("p (a b) -> p a b", a=8), th)
        tq_ = [features_of(qT, n) for n in range(2)]
        t = rms_rows(gv, gv, 4, 512.0, JK2, small[:, 0:4], 1e-6, tgv)
        for i in range(4):
            tgn = v(tt(gv[:, i, :], gv[:, i, :], rows[:, 2048:2560], MUL), trw)
        tk_ = [features_of(kT, n) for n in range(2)]
        tnq = head_norm(qT, K_QN, 0.125, tq_)
        tvv = [rows_of(vt, 0, ACT.Copy)]
        for i in range(4):
            b = allb.take()
            t = pe([mm(PS[b][:, 64 * q:64 * q + 64], ws[:, q, :], gv[:, i, 64 * q:64 * q + 64]) for q in range(8)],
                   tgn, twm, allb.rel[b])
            t = v(tt(JK2.rearrange("p (a b) -> p a b", a=8), PS[b][:, :].rearrange("p (a b) -> p a b", a=8),
                     bc(bs_.rearrange("p (a b) -> p a b", b=1), 64), ADD), t, tbs)
            allb.free(b, t)
            tgu = v(tt(gu[:, i, :], gu[:, i, :], JK2, MUL), tgu_)
        tnk = head_norm(kT, K_KN, 1.0, tk_)
        tvv.append(rows_of(vt, 1, ACT.Copy))
        for c in range(4):
            b = allb.take()
            t = pe([tr(PS[b][:, 128 * i:128 * i + 128], gu[:, i, 128 * c:128 * c + 128]) for i in range(4)], tgu, allb.rel[b])
            t = s(act(aT[:, c, :], PS[b][:, :], ACT.Copy), t, fe, tnk)
            allb.free(b, t)
        taT = t
        PT = [at(8192 + 2048 * i, 4, 512) for i in range(2)]
        Pb = [at(18432 + 512 * i, 512) for i in range(4)]
        ta2 = attention(8, 4, qT, kT, lambda i: 128 * (i + 1), lambda h, i: ab[:, h, 384 - 128 * i:512], vt, aT[:, 4:8, :],
                        Pb, PT, small[:, 16:32], [tab, tnq, tnk, tvv, taT], causal=True)
        ta2 = halve(aT, h2[0], h2[1], taT, ta2)
        tX = out_proj(wb, h2, ta2)
        if stop == "mix2":
            dump(X)
            return finish(nc, ctx, PE, V, S, G, SP, sems)

        fe = fence()
        XN = at(0, 4, 1024)
        qT = at(8192, 16, 512)
        JK = at(16384, 1024)
        FS = at(4096, 2, 512)
        EX, = tail_is("ex", (4096, f32))
        F = tail_is("fd", (4096, f32r), (4096, f32r), *[(1024, f32r)] * 4, level=1)
        h2 = (v3(F[0], 8), v3(F[1], 8))
        sk = v3(EX[:, 0:2048], 16)
        tsk = dma(SP, sk, I["skT"].rearrange("p (a b) -> p a b", a=16), fe)
        wb = Weights([(v3(F[2 + 2 * i], 8), v3(F[3 + 2 * i], 8)) for i in range(2)], 128, 8, fe, True)
        t = rms_rows(X, XN, 4, 1024.0, JK, small[:, 0:4], 1e-6, fe)
        th = to_feature(XN, FS, 4, K_FFN2, allb, t, hl=h2)
        for i in range(4):
            txb = v(tt(XN[:, i, :], XN[:, i, :], rows[:, 1024:2048], MUL), th, tok(PE))
        o = D0 + 20480
        sc = fl(o, 2, 2, 128)
        cand = fl(o + 512, 256)
        o = D0 + 22528
        oh = fl(o + 336, 2, 16, 16)
        best = fl(o, 8, 16)
        st_ = fl(o + 128, 2, 16)
        siu = AR_[:, o + 160:o + 192].bitcast(u32).rearrange("p (a b) -> p a b", a=2)
        sif = fl(o + 192, 2, 16)
        posu = AR_[:, o + 224:o + 240].bitcast(u32)
        pai = AR_[:, o + 240:o + 272].bitcast(u32).rearrange("p (a b) -> p a b", a=2)
        pf = fl(o + 272, 2, 16)
        e12 = fl(o + 304, 2, 16)
        eidx = [AR_[:, D0 + 17408 + 128 * i:D0 + 17408 + 128 * i + 128].bitcast(i32) for i in range(4)]
        gw = at(17920, 4, 128)
        dots = at(18432, 4, 128)
        io16 = cons[:, C_IOTA:C_IOTA + 16].rearrange("p (a b) -> p a b", a=1)
        teidx, wtk = {}, {}
        JV = [at(16384, 1024), at(18944, 1024)]
        scfree = [fe, fe]
        tqh = {}

        last_c = [fe]

        def vc(fn, *deps):
            last_c[0] = V.add([fn], [deps, last_c[0]], False)
            return last_c[0]

        def choose(i, h):
            b = allb.take()
            t = pe([mm(PS[b][:, 128 * q:128 * q + 128], qT[:, 2 * h + q, 128 * i:128 * i + 128], sk[:, 2 * h + q, :]) for q in range(2)],
                   tqh[h], tsk, allb.rel[b])
            S_ = sc[:, h % 2, :, :]
            t = s(act(S_, PS[b][:, 0:256].rearrange("p (a b) -> p a b", a=2), ACT.Copy), t, scfree[h % 2])
            allb.free(b, t)
            for q in range(2):
                vc(lambda e, q=q: e.max(st_[:, q, 0:8], S_[:, q, :]), t)
                yield
                vc(lambda e, q=q: e.max_index(siu[:, q, 0:8], st_[:, q, 0:8], S_[:, q, :]))
                yield
                vc(lambda e, q=q: e.match_replace(S_[:, q, :], st_[:, q, 0:8], S_[:, q, :], -3.0e38))
                yield
                vc(lambda e, q=q: e.max(st_[:, q, 8:16], S_[:, q, :]))
                yield
                scfree[h % 2] = vc(lambda e, q=q: e.max_index(siu[:, q, 8:16], st_[:, q, 8:16], S_[:, q, :]))
                yield
            vc(cp(sif, siu))
            yield
            vc(tt(cand.rearrange("p (a b) -> p a b", a=16), bc(st_[:, 0, :].rearrange("p (a b) -> p a b", b=1), 16),
                 st_[:, 1, :].rearrange("p (a b) -> p a b", a=1).to_broadcast([128, 16, 16]), ADD))
            yield
            vc(lambda e: e.max(best[:, h, 0:8], cand))
            yield
            vc(lambda e: e.max_index(posu[:, 0:8], best[:, h, 0:8], cand))
            yield
            vc(lambda e: e.match_replace(cand, best[:, h, 0:8], cand, -3.0e38))
            yield
            vc(lambda e: e.max(best[:, h, 8:16], cand))
            yield
            vc(lambda e: e.max_index(posu[:, 8:16], best[:, h, 8:16], cand))
            yield
            vc(ts(pai[:, 0, :], posu, 4, ALU.logical_shift_right))
            yield
            vc(ts(pai[:, 1, :], posu, 15, ALU.bitwise_and))
            yield
            vc(cp(pf, pai))
            yield
            vc(tt(oh, pf.rearrange("p a (b c) -> p a b c", c=1).to_broadcast([128, 2, 16, 16]),
                 io16.rearrange("p (c a) b -> p c a b", c=1).to_broadcast([128, 2, 16, 16]), ALU.is_equal))
            yield
            vc(tt(oh, oh, sif.rearrange("p a (c b) -> p a c b", c=1).to_broadcast([128, 2, 16, 16]), MUL))
            yield
            vc(lambda e: e.tensor_reduce(e12, oh, AX.X, ADD))
            yield
            teidx[i, h] = vc(stt(eidx[i][:, 16 * h:16 * h + 16], e12[:, 0, :], 128.0, e12[:, 1, :], MUL, ADD))
            yield
            if h == 7:
                g3 = gw[:, i, :].rearrange("p (a b) -> p a b", a=8)
                t = vc(tt(g3, best, best[:, :, 0:1].to_broadcast([128, 8, 16]), SUB))
                yield
                t = s(act(g3, g3, ACT.Exp), t)
                vc(lambda e: e.tensor_reduce(small[:, 40:48], g3, AX.X, ADD), t)
                yield
                vc(lambda e: e.reciprocal(small[:, 40:48], small[:, 40:48]))
                yield
                vc(tt(g3, g3, bc(small[:, 40:48].rearrange("p (a b) -> p a b", b=1), 16), MUL))
                yield

        def choose_all(i):
            for h in range(8):
                yield from choose(i, h)

        GB = [at(4096 + 1024 * i, 1024) for i in range(4)] + [EX[:, 2048 + 1024 * i:3072 + 1024 * i] for i in range(2)]
        gr = [[txb, th]] * 6
        last_c[0] = txb
        names = [f"gb{i}" for i in range(6)]
        gn = [0]
        outt = []
        last_u, last_v = [tok(V), tok(V)], [tok(V), tok(V)]

        def expert(kind, i, k):
            sl = gn[0] % len(GB)
            gn[0] += 1
            buf = GB[sl]
            t = gather(buf, I["peer_u" if kind == "u" else "peer_v"], eidx[i][:, k:k + 1], teidx[i, k // 16], gr[sl], on=names[sl])
            if kind == "u":
                t = vu(lambda e: e.tensor_tensor_reduce(out=JV[k % 2], in0=buf, in1=XN[:, i, :], scale=1.0, scalar=0.0,
                                                        op0=MUL, op1=ADD, accum_out=dots[:, i, k:k + 1]), t, txb, fe, last_u[0])
                last_u[:] = [last_u[1], t]
                gr[sl] = t
                if k == 127:
                    t = s(act(dots[:, i, :], dots[:, i, :], ACT.Gelu_apprx_tanh), t)
                    wtk[i] = t
            else:
                if k == 0:
                    wtk[i] = v(tt(dots[:, i, :], dots[:, i, :], gw[:, i, :], MUL), wtk[i])
                    last_v[:] = [wtk[i]] * 2
                acc = X[:, i, :] if k % 2 == 0 else XN[:, i, :]
                if k == 1:
                    f_ = ts(acc, buf, dots[:, i, k:k + 1], MUL)
                else:
                    f_ = stt(acc, buf, dots[:, i, k:k + 1], acc, MUL, ADD)
                gr[sl] = last_v[k % 2] = vu(f_, t, wtk[i], last_v[k % 2])
                if k == 127:
                    last_v[0] = vu(tt(X[:, i, :], X[:, i, :], XN[:, i, :], ADD), last_v)

        for n in range(9):
            if n < 8:
                for a in range(2):
                    r = wb.get()
                    b = allb.take()
                    t = proj_f(r, h2, b, th)
                    wb.done(r, t)
                    tqh[n] = s(act(qT[:, 2 * n + a, :], PS[b][:, :], ACT.Copy), t, fe)
                    allb.free(b, tqh[n])
                c_ = choose(0, n)
            else:
                c_ = iter(())
            for k in range(16):
                if n:
                    expert("u", 0, 16 * (n - 1) + k)
                next(c_, None)
                next(c_, None)
            for _ in c_:
                pass
            if n == 7:
                last_proj = [tok(PE), tok(V)]
        F, = tail_is("gb", (12288, f32), level=1)
        at_ = gn[0] % 6
        more = [F[:, 1024 * i:1024 * i + 1024] for i in range(12)]
        GB = GB[at_:] + more + GB[:at_]
        gr = gr[at_:] + [last_proj] * 12 + gr[:at_]
        names = [f"gb{(at_ + i) % 6}" for i in range(6)]
        names = names[:6 - at_] + [f"gb{6 + i}" for i in range(12)] + names[6 - at_:]
        gn[0] = 0
        nxt, due = choose_all(1), [0.0]

        def step(rate):
            due[0] += rate
            while due[0] >= 1.0:
                due[0] -= 1.0
                next(nxt, None)
        for i in range(4):
            if i:
                for k in range(128):
                    expert("u", i, k)
                    step(0.75)
            for k in range(128):
                expert("v", i, k)
                step(0.75 if i else 1.5)
            for _ in nxt:
                pass
            if i < 2:
                nxt = choose_all(i + 2)
            outt.append(dma(SP, O.rearrange("(a p) f -> p a f", p=128)[:, i, :], X[:, i, :], last_v[0]))
        finish(nc, ctx, PE, V, S, G, SP, sems)


def finish(nc, ctx, PE, V, S, G, SP, sems):
    block = ctx.enter_context(nc.Block())

    @block.tensor
    def _(e):
        PE.emit(e)

    @block.vector
    def _(e):
        V.emit(e)

    @block.scalar
    def _(e):
        S.emit(e)

    @block.gpsimd
    def _(e):
        G.emit(e)

    @block.sync
    def _(e):
        SP.emit(e)
        for sm, val in sems.values():
            e.wait_ge(sm, val)


def constants():
    c = np.zeros((128, C_END), np.float32)
    p = np.arange(128)
    c[:, 0:128] = np.eye(128)
    same = (p[:, None] // 64) == (p[None, :] // 64)
    c[:, C_ONES:C_ONES + 128] = same
    t = np.arange(64)
    for n in range(4):
        c[:, C_M4 + 64 * n:C_M4 + 64 * n + 64] = ((p % 64)[:, None] <= t) if n % 2 else ((p % 64)[:, None] < t)
    for n in range(6):
        b = 2 ** n
        big = (p[:, None] // (2 * b)) == (p[None, :] // (2 * b))
        c[:, C_LVL + 128 * n:C_LVL + 128 * n + 128] = big & ((p[:, None] // b) % 2 == 0) & ((p[None, :] // b) % 2 == 1)
    c[:, C_SCAN:C_SCAN + 512] = (np.arange(512) % 64 != 0)[None, :]
    c[:, C_BD:C_BD + 128] = same
    c[:, C_IOTA:C_IOTA + 512] = np.arange(512)[None, :]
    c[:, C_WM:C_WM + 128] = (p[:, None] // 64) <= (p[None, :] // 64)
    e = np.arange(16)
    c[0:16, C_EM:C_EM + 128] = (e[:, None] % 2) == (p[None, :] // 64)
    c[0:16, C_ES:C_ES + 8] = (e[:, None] // 2) == np.arange(8)[None, :]
    return c


def tiles(w):
    k, n = w.shape
    return w.reshape(k // 128, 128, n // 256, 256).transpose(2, 1, 0, 3).reshape(n // 256, 128, (k // 128) * 256)


def layouts(a):
    f = {k: np.asarray(v) for k, v in a.items()}
    w = f["w_in"][0]
    ch = [w[:, 128 * c:128 * c + 128] for c in range(46)]
    order = list(range(9, 20)) + list(range(0, 9)) + [20, 21]
    gates = []
    br = np.concatenate([f["w_branch_na"][0], f["w_branch_rw"][0], f["w_branch_mem"][0]], 0)
    order += [22 + 8 * b + 2 * f2 + a for f2 in range(4) for b in range(3) for a in range(2)]
    parts = [tiles(np.concatenate([ch[c] for c in order], 1)), tiles(f["w_mem_kv"][0]), tiles(br)]
    parts += [tiles(f["w_out"][0]), tiles(np.concatenate([f["w_in_2"][0][:, 512:1024], f["w_in_2"][0][:, 0:512], f["w_in_2"][0][:, 1024:]], 1)), tiles(f["w_out_2"][0]), tiles(f["peer_w_query_2"][0])]
    wt = np.concatenate(parts, 0)

    def col(v, n):
        return v.reshape(n, 128).T
    cols = [col(f["norm_mix_g"][0], 8), col(f["norm_mem_g"][0], 8), col(f["norm_ffn_g"][0], 8), col(f["ln_mix_g_2"][0], 8),
            col(f["ln_ffn_g_2"][0], 8), col(f["rw_mu_rkv"][0].reshape(-1), 18),
            np.concatenate([f["rw_mu_w"][0].T, f["rw_mu_a"][0].T], 0),
            col(f["rw_w0"][0].reshape(-1), 6), col(f["rw_a0"][0].reshape(-1), 6), col(f["rw_k_k"][0], 3), col(f["rw_k_a"][0], 3),
            col(f["rw_r_k"][0].reshape(-1), 3), col(f["rw_ln_g"][0], 3), col(f["rw_ln_b"][0], 3),
            np.concatenate([f["q_norm_g_2"][0]] * 2)[:, None], np.concatenate([f["k_norm_g_2"][0]] * 2)[:, None]]
    cols = np.concatenate(cols, 1)
    low = np.full((1,), -1e30, np.float32)
    c = np.arange(64)
    start = np.clip(c - 8, 0, 48)
    inside = (c[None, :] >= start[:, None]) & (c[None, :] < start[:, None] + 16)
    j = c[None, :] - c[:, None] + 15
    nab = np.zeros((128, 6, 16, 64), np.float32)
    for h in range(6):
        flat_ = np.concatenate([f["na_rpb"][0, h].reshape(-1), low])
        for dr in range(15):
            v = flat_[np.where(inside, dr * 31 + np.clip(j, 0, 30), 15 * 31)]
            nab[0:64, h, dr, :] = v
            nab[64:128, h, dr + 1, :] = v
    p = np.arange(128)[:, None]
    x = np.arange(512)[None, :] - 384
    ok = np.floor_divide(x, 64) <= p // 64
    idx = np.where(ok, np.clip(p - x, -128, 128) + 128, 257)
    abias = np.stack([np.concatenate([f["rel_bias_2"][0, h], low])[idx] for h in range(8)], 1)
    return {
        "x": f["x"][0], "mem": f["mem"][0], "wt": wt, "cols": cols, "consts": constants(),
        "w2a2": np.concatenate([f["rw_w2"][0].transpose(1, 0, 2).reshape(64, 768), f["rw_a2"][0].transpose(1, 0, 2).reshape(64, 768)], 0),
        "g2": f["rw_g2"][0], "nab": nab.reshape(128, 6144), "abias": abias.reshape(128, 4096),
        "rt": f["w_router"][0].reshape(8, 128, 16).transpose(1, 0, 2).reshape(128, 128),
        "eg": f["w_exp_gate"][0], "eu": f["w_exp_up"][0], "ed": f["w_exp_down"][0],
        "rows": np.concatenate([np.broadcast_to(v[None, :], (128, v.shape[0])) for v in
                                (f["norm_final_g"], f["ln_ffn_g_2"][0], f["gmlp_norm_g_2"][0])], 1),
        "wsT": f["gmlp_w_s_2"][0].transpose(2, 0, 1).reshape(128, 1024), "bsT": f["gmlp_b_s_2"][0].T,
        "skT": f["peer_sub_keys_2"][0].reshape(16, 128, 128).transpose(2, 0, 1).reshape(128, 2048),
        "peer_u": f["peer_u_2"][0], "peer_v": f["peer_v_2"][0],
    }


def kernel(**inputs):
    import concourse.bacc as bacc
    from concourse.bass_utils import run_bass_kernel_spmd

    nc = bacc.Bacc("TRN2", target_bir_lowering=False, num_devices=1)
    arrays = {k: np.ascontiguousarray(v) for k, v in layouts(inputs).items()}
    I = {k: nc.dram_tensor("in_" + k, v.shape, mybir.dt.from_np(v.dtype), kind="ExternalInput").ap() for k, v in arrays.items()}
    O = nc.dram_tensor("out_0", (512, 1024), mybir.dt.float32, kind="ExternalOutput").ap()
    block_program(nc, I, O)
    r = run_bass_kernel_spmd(nc, [{"in_" + k: v for k, v in arrays.items()}], core_ids=[0])
    return r.results[0]["out_0"].reshape(1, 512, 1024)
```

```python
import math
from contextlib import ExitStack

import numpy as np

import concourse.bass as bass
from concourse import mybir

NS = 3
PACE, FILL_M = 3.0, 1

C_IDENT, C_ONES, C_M4, C_LVL, C_SCAN, C_BD, C_IOTA, C_WM, C_EM, C_ES, C_END = (
    0, 128, 256, 512, 1280, 1792, 1920, 2432, 2560, 2688, 2696)
(K_MIX, K_MEM, K_FFN, K_MIX2, K_FFN2, K_MU, K_MUWA, K_W0, K_A0, K_KK, K_KA, K_RK, K_LNG, K_LNB, K_QN, K_KN, K_END) = (
    0, 8, 16, 24, 32, 40, 58, 60, 66, 72, 75, 78, 81, 84, 87, 88, 89)


class Queue:

    def __init__(self, sem):
        self.sem, self.n, self.items = sem, 0, []

    def add(self, fns, deps, chain):
        waits = flat(deps)
        if chain and self.n:
            waits.append((self.sem, self.n))
        self.n += 1
        self.items.append((fns, waits, (self.sem, 1)))
        return (self.sem, self.n)

    def emit(self, eng):
        seen = {}
        for fns, waits, (sem, k) in self.items:
            for s, v in waits:
                if seen.get(id(s), 0) < v:
                    eng.wait_ge(s, v)
                    seen[id(s)] = v
            last = None
            for f in fns:
                last = f(eng)
            if last is not None:
                last.then_inc(sem, k)


def flat(deps):
    out = []
    for d in deps:
        if d is None:
            continue
        if len(d) == 2 and isinstance(d[1], int):
            out.append(d)
        else:
            out += flat(d)
    return out


def block_program(nc, I, O, stop=None, dbg=None):
    f32, f32r, i32, u32 = mybir.dt.float32, mybir.dt.float32r, mybir.dt.int32, mybir.dt.uint32
    ACT, ALU, AX = mybir.ActivationFunctionType, mybir.AluOpType, mybir.AxisListType
    ADD, SUB, MUL, MAX = ALU.add, ALU.subtract, ALU.mult, ALU.max
    ctx = ExitStack()
    with ctx:
        def sem(n):
            return ctx.enter_context(nc.semaphore(n))

        TOTAL = 36824
        AR_ = ctx.enter_context(nc.sbuf_tensor("arena", [128, TOTAL], f32))
        tails = []

        def drop(level):
            while len(tails) > level:
                tails.pop().close()
        ctx.callback(drop, 0)

        def tail_is(name, *parts, level=0):
            drop(level)
            tails.append(ExitStack())
            return [tails[-1].enter_context(nc.sbuf_tensor(f"{name}{i}", [128, n], dt)) for i, (n, dt) in enumerate(parts)]

        PS = [ctx.enter_context(nc.psum_tensor(f"ps{i}", [128, 512], f32)) for i in range(8)]
        p_dram = nc.dram_tensor("p_scratch", (128, 35 * 512), f32, kind="Internal").ap()
        h_dram = nc.dram_tensor("h_scratch", (512, 1024), f32, kind="Internal").ap()

        PE, V, S, G, SP = (Queue(sem(f"q_{n}")) for n in ("pe", "dve", "act", "pool", "sp"))

        pace = [0.0, 0.0, None]

        def v(fn, *deps):
            t = V.add([fn], deps, True)
            pace[1] += pace[0]
            while pace[1] >= 1.0 and pace[0]:
                pace[1] -= 1.0
                hold, pace[0] = pace[0], 0.0
                pace[2](1)
                pace[0] = hold
            return t

        def vu(fn, *deps):
            return V.add([fn], deps, False)

        def s(fn, *deps):
            return S.add([fn], deps, True)

        def g(fn, *deps):
            return G.add([fn], deps, True)

        def pe(fns, *deps):
            return PE.add(fns, deps, False)

        nsem = [0]
        sems = {}

        def dma(q, out, in_, *deps, on=None):
            if on is None:
                nsem[0] += 1
                on = f"d{nsem[0]}"
            if on not in sems:
                sems[on] = [sem(on), 0]
            r = sems[on]
            r[1] += 16
            q.items.append(([lambda e: e.dma_start(out, in_)], flat(deps), (r[0], 16)))
            return (r[0], r[1])

        def gather(out, table, idx, *deps, on):
            if on not in sems:
                sems[on] = [sem(on), 0]
            r = sems[on]
            r[1] += 16
            G.items.append(([lambda e: e.indirect_dma_start(out, None, table, bass.IndirectOffsetOnAxis(ap=idx, axis=0))],
                            flat(deps), (r[0], 16)))
            return (r[0], r[1])

        def tok(q):
            return (q.sem, q.n) if q.n else None

        def fence():
            return [tok(PE), tok(V), tok(S), tok(G)]

        def mm(out, l, r, st=True, sp=True):
            return lambda e: e.matmul(out, l, r, start=st, stop=sp, skip_group_check=True)

        def mr(out, l, r, st, sp):
            return lambda e: e.matmul(out, l, r, start=st, stop=sp, skip_group_check=True)

        def tr(out, in_):
            n = in_.shape[0]
            return lambda e: e.transpose(out, in_, ident[0:n, 0:n])

        def tt(o, a, b, op):
            return lambda e: e.tensor_tensor(o, a, b, op)

        def ts(o, a, s1, op, s2=None, op2=None):
            if op2 is None:
                return lambda e: e.tensor_scalar(o, a, s1, None, op)
            return lambda e: e.tensor_scalar(o, a, s1, s2, op, op2)

        def stt(o, a, sc, b, o0, o1):
            return lambda e: e.scalar_tensor_tensor(out=o, in0=a, scalar=sc, in1=b, op0=o0, op1=o1)

        def act(o, a, f, **k):
            return lambda e: e.activation(o, a, f, **k)

        def cp(o, a):
            return lambda e: e.tensor_copy(o, a)

        def bc(ap, n):
            return ap.to_broadcast(list(ap.shape[:-1]) + [n])

        class Banks:
            def __init__(self, ids):
                self.ids, self.at, self.rel = ids, 0, {i: None for i in ids}

            def take(self):
                i = self.ids[self.at % len(self.ids)]
                self.at += 1
                return i

            def free(self, i, *t):
                self.rel[i] = list(t)

        def fl(off, *shape):
            n = int(np.prod(shape))
            assert off + n <= TOTAL, (off, shape)
            a = AR_[:, off:off + n]
            if len(shape) == 1:
                return a
            names = "abcd"[:len(shape)]
            return a.rearrange("p (" + " ".join(names) + ") -> p " + " ".join(names), **dict(zip(names, shape)))

        cons = fl(0, C_END)
        ident = cons[:, 0:128]
        ones = cons[:, C_ONES:C_ONES + 128]
        cols = fl(C_END, K_END)
        o = C_END + 96
        small = fl(o, 192)
        o += 192
        RING = o
        o += NS * 2048
        XO = o
        X = fl(o, 4, 1024)
        o += 4096
        D0 = o
        room = TOTAL - D0

        def at(off, *shape):
            assert off + int(np.prod(shape)) <= room, (off, shape, room)
            return fl(D0 + off, *shape)

        ring_slots = [fl(RING + 2048 * i, 2048) for i in range(NS)]
        ring_rel = [None] * NS
        ring_at = [0]

        def ring_grow(bufs, rel, last=False):
            at_, have = ring_at[0] % len(ring_slots), len(ring_slots)
            ring_slots[at_:at_] = bufs
            ring_rel[at_:at_] = [rel] * len(bufs)
            ring_sem[at_:at_] = [f"ring{have + i}" for i in range(len(bufs))]
            ring_at[0] = at_ + (len(bufs) if last else 0)

        def ring_shrink():
            for i in reversed(range(len(ring_slots))):
                if int(ring_sem[i][4:]) >= NS:
                    del ring_slots[i], ring_rel[i], ring_sem[i]
            ring_at[0] = 0

        ring_sem = [f"ring{i}" for i in range(NS)]

        def ring_next(parts):
            n = ring_at[0] % len(ring_slots)
            ring_at[0] = n + 1
            buf = ring_slots[n]
            t = None
            for shape, src in parts:
                dst = buf if shape is None else buf.rearrange("p (a b) -> p a b", a=shape)
                t = dma(SP, dst, src, ring_rel[n], on=ring_sem[n])
            return n, buf, t

        def ring_free(n, *t):
            ring_rel[n] = list(t)

        wt_n = [0]

        def wtile():
            t = wt_n[0]
            wt_n[0] += 1
            n, buf, tk = ring_next([(None, I["wt"][t])])
            return n, buf.rearrange("p (k c) -> p k c", k=8), tk

        tc = dma(SP, cons, I["consts"])
        tk = dma(SP, cols, I["cols"])
        tx = dma(SP, X, I["x"].rearrange("(a p) f -> p a f", p=128))

        allb = Banks(list(range(8)))

        def dump(ap, *deps):
            n = int(np.prod(ap.shape[1:]))
            dst = dbg.rearrange("p n -> p n")[:, 0:n]
            if len(ap.shape) == 3:
                dst = dst.rearrange("p (a b) -> p a b", a=ap.shape[1])
            return dma(SP, dst, ap, fence())

        def colmul(out, in_, k0):
            return lambda e: e.tensor_scalar(out, in_, cols[:, k0:k0 + 1], None, MUL)

        def rms_rows(src, dst, nt, width, junk, sc, eps, *deps):
            t = None
            for i in range(nt):
                t = s(act(junk, src[:, i, :], ACT.Square, accum_out=sc[:, i:i + 1]), *deps)
            t = v(ts(sc[:, 0:nt], sc[:, 0:nt], 1.0 / width, MUL, eps, ADD), t)
            t = s(act(sc[:, 0:nt], sc[:, 0:nt], ACT.Sqrt), t)
            t = v(lambda e: e.reciprocal(sc[:, 0:nt], sc[:, 0:nt]), t)
            for i in range(nt):
                t = v(ts(dst[:, i, :], src[:, i, :], sc[:, i:i + 1], MUL), *deps)
            return t

        def rms_tile(i, src, dst, junk, sc, eps, *deps):
            q = sc[:, i:i + 1]
            t = s(act(junk, src[:, i, :], ACT.Square, accum_out=q), *deps)
            t = v(ts(q, q, 1.0 / 1024, MUL, eps, ADD), t)
            t = s(act(q, q, ACT.Sqrt), t)
            v(lambda e: e.reciprocal(q, q), t)
            return v(ts(dst[:, i, :], src[:, i, :], q, MUL), *deps)

        def tile_to_feature(i, src, dst, k0, banks, *deps):
            for k4 in range(2):
                b = banks.take()
                t = pe([tr(PS[b][:, 128 * q:128 * q + 128], src[:, i, 512 * k4 + 128 * q:512 * k4 + 128 * q + 128]) for q in range(4)],
                       deps, tc, banks.rel[b])
                k_ = k0 + 4 * k4
                t = v(tt(dst[:, 4 * k4:4 * k4 + 4, 128 * i:128 * i + 128], PS[b][:, :].rearrange("p (a b) -> p a b", a=4),
                         bc(cols[:, k_:k_ + 4].rearrange("p (a b) -> p a b", b=1), 128), MUL), t, tk)
                banks.free(b, t)
            return t

        def to_feature(src, dst, nt, k0, banks, *deps, hl=None):
            last = []
            for c in range(8):
                b = banks.take()
                t = pe([tr(PS[b][:, 128 * i:128 * i + 128], src[:, i, 128 * c:128 * c + 128]) for i in range(nt)],
                       deps, tc, banks.rel[b])
                col = cols[:, k0 + c:k0 + c + 1]
                if hl is not None:
                    hi, lo = hl[0][:, c, :], hl[1][:, c, :]
                    t = s(act(hi, PS[b][:, 0:128 * nt], ACT.Copy, scale=col), t, tk)
                    t = v(stt(lo, PS[b][:, 0:128 * nt], col, hi.bitcast(f32), MUL, SUB), t)
                elif c % 2:
                    t = v(colmul(dst[:, c, :], PS[b][:, 0:128 * nt], k0 + c), t, tk)
                else:
                    t = s(act(dst[:, c, :], PS[b][:, 0:128 * nt], ACT.Copy, scale=col), t, tk)
                banks.free(b, t)
                last.append(t)
            return last[-2:]

        def halve(src, hi, lo, *deps, by_act=False):
            t = s(act(hi, src, ACT.Copy), *deps) if by_act else v(cp(hi, src), *deps)
            return v(tt(lo, src, hi.bitcast(f32), SUB), t)

        def product(out, pairs):
            n = len(pairs)
            fs = []
            for k, (l, r) in enumerate(pairs):
                fs += [mr(out, l[0], r[0], k == 0, False), mr(out, l[0], r[1], False, False),
                       mr(out, l[1], r[0], False, k == n - 1)]
            return fs

        class Weights:

            def __init__(self, bufs, width, ntile, rel, by_act=False):
                self.by_act = by_act
                self.bufs, self.width, self.rel = bufs, width, [rel] * len(bufs)
                self.left, self.n, self.tile, self.lo, self.next = ntile, 0, None, 256, None

            def prepare(self):
                if self.lo == 256:
                    if not self.left:
                        self.next = None
                        return
                    self.left -= 1
                    self.tile, self.lo = wtile(), 0
                rn, w, tw = self.tile
                i = self.n % len(self.bufs)
                self.n += 1
                part = w[:, :, self.lo:self.lo + self.width]
                hi, low = self.bufs[i]
                t = halve(part, hi, low, tw, self.rel[i], by_act=self.by_act)
                self.lo += self.width
                self.next = (hi, low, t, i)
                if self.lo == 256:
                    ring_free(rn, t)

            def get(self):
                if self.n == 0:
                    self.prepare()
                r = self.next
                self.prepare()
                return r

            def done(self, r, t):
                self.rel[r[3]] = [t]

        def proj_f(r, rhs, b, *deps):
            hi, lo, tw = r[:3]
            return pe(product(PS[b][:, :], [((hi[:, k, :], lo[:, k, :]), (rhs[0][:, k, :], rhs[1][:, k, :])) for k in range(8)]),
                      tw, deps, allb.rel[b])

        def proj_t(r, lhs, i, b, *deps):
            hi, lo, tw = r[:3]
            q = slice(128 * i, 128 * i + 128)
            return pe(product(PS[b][:, 0:256], [((lhs[0][:, k, q], lhs[1][:, k, q]), (hi[:, k, :], lo[:, k, :])) for k in range(8)]),
                      tw, deps, allb.rel[b])

        def v3(t, a):
            return t[:, :].rearrange("p (a b) -> p a b", a=a)

        F = tail_is("fa", (4096, f32r), (4096, f32r), (4096, f32), *[(1024, f32r)] * 4)
        h2 = (v3(F[0], 8), v3(F[1], 8))
        hT, hL = h2
        EX = F[2]
        HB = [(v3(F[3 + 2 * i], 8), v3(F[4 + 2 * i], 8)) for i in range(2)]
        XN = at(8192, 4, 1024)
        JK = at(12288, 1024)
        wa = Weights(HB, 128, 23, None)
        tr1 = rms_rows(X, XN, 4, 1024.0, JK, small[:, 0:4], 1e-6, tx)
        wa.prepare()
        th = to_feature(XN, None, 4, K_MIX, allb, tr1, hl=h2)

        o = 0
        pr = at(o, 3, 514); o += 1542
        pk = at(o, 3, 514); o += 1542
        pv = at(o, 3, 514); o += 1542
        pw = at(o, 514); o += 514
        lg = at(o, 512); o += 512
        yS = at(o, 3, 512); o += 1536
        bS = at(o, 3, 512); o += 1536
        R = at(o, 3, 512); o += 1536
        K = at(o, 3, 512); o += 1536
        VV = at(o, 3, 512); o += 1536
        T1o = o
        T1 = at(o, 3, 512); o += 1536
        T3 = at(o, 3, 512); o += 1536
        T4 = at(o, 3, 512); o += 1536
        T5 = at(o, 3, 512); o += 1536
        T2 = at(o, 3, 512); o += 1536
        AR = EX[:, 0:3072].rearrange("p (a b c) -> p a b c", a=3, b=4)
        P1, P2 = v3(EX[:, 0:1536], 3), v3(EX[:, 1536:3072], 3)
        W2, G2 = fl(XO, 2, 384), fl(XO, 384)
        m_ = T1o
        M4s = [at(m_, 6, 256), fl(XO, 6, 256)]; m_ += 1536
        Tm = at(m_, 6, 128); m_ += 768
        TT = at(m_, 6, 128); m_ += 768
        X1 = at(m_, 6, 128); m_ += 768
        BT = [at(m_, 6, 128), at(m_ + 768, 6, 128)]; m_ += 1536
        PCM = at(m_, 3, 128); m_ += 384
        PC = at(m_, 3, 8); m_ += 24
        assert m_ <= T1o + 6144
        AToks = [at(o, 4, 384), fl(XO + 1536, 4, 384)]; o += 1536
        SB = [EX[:, 3072:3584], EX[:, 3584:4096]]
        SS = [at(o, 3, 128), at(o + 384, 3, 128)]; o += 768
        Ro = T1o - 4608
        MV, U = at(Ro + 384, 384), at(Ro + 1152, 384)
        Ats = [at(Ro, 3, 128), fl(XO + 3072, 3, 128)]
        U0s = [at(Ro + 768, 384), fl(XO + 3456, 384)]
        te = fence()
        tz = None
        for p in (pr, pk, pv):
            tz = g(lambda e, p=p: e.memset(p[:, :, 0:514:513], 0.0), te)
        tz = g(lambda e: e.memset(pw[:, 0:514:513], 0.0), te)

        dst = [p[:, c, 1:513] for p in (pr, pk, pv) for c in range(3)] + [pw[:, 1:513], lg]
        tp = []
        for n in range(11):
            r = wa.get()
            b = allb.take()
            t = proj_f(r, h2, b, th)
            wa.done(r, t)
            t2 = s(act(dst[n], PS[b][:, :], ACT.Copy), t, te)
            allb.free(b, t2)
            tp.append(t2)
        tp = [tp[-1], tp[-2], tz]

        fb = Banks([6, 7])
        for i in fb.ids:
            fb.rel[i] = allb.rel[i]
        spilled = {}

        def spill(slot, src, t, relu):
            spilled[slot] = dma(SP, p_dram[:, 512 * slot:512 * slot + 512], src, t, on=f"sp{relu}")
            return spilled[slot]

        def filler():
            rel = [None, None]
            q = 0
            for n in range(35):
                r = wa.next
                b = fb.take()
                fs = product(PS[b][:, :], [((r[0][:, k, :], r[1][:, k, :]), (hT[:, k, :], hL[:, k, :])) for k in range(8)])
                for k in range(8):
                    t = pe(fs[3 * k:3 * k + 3], r[2], fb.rel[b] if k == 0 else None)
                    if k == 3:
                        wa.prepare()
                    if k < 7:
                        yield
                wa.done(r, t)
                q = 1 - q
                if n >= 11:
                    t = s(act(SB[q], PS[b][:, :], ACT.Sigmoid), t, rel[q])
                else:
                    t = s(act(SB[q], PS[b][:, :], ACT.Copy, scale=0.125 if n < 3 or n >= 9 else 1.0), t, rel[q])
                fb.free(b, t)
                if 6 <= n < 9:
                    yield
                    b = fb.take()
                    t = pe([tr(PS[b][:, 128 * i:128 * i + 128], SB[q][:, 128 * i:128 * i + 128]) for i in range(4)], t, fb.rel[b])
                    rel[q] = [t]
                    q = 1 - q
                    t = s(act(SB[q], PS[b][:, :], ACT.Copy), t, rel[q])
                    fb.free(b, t)
                rel[q] = [spill(n, SB[q], t, q)]
                yield
        fill_g = filler()

        def fill(n):
            for _ in range(n):
                if next(fill_g, 1) == 1:
                    return
        pb = Banks([0, 1, 2, 3, 4, 5])
        pb.rel.update({i: allb.rel[i] for i in range(6)})

        def head_sum(src, nch, use, *deps):
            for c in range(nch):
                b = pb.take()
                t = pe([mm(PS[b][:, :], ones, src(c))], deps, tc, pb.rel[b])
                pb.free(b, use(c, PS[b], t))

        for d in range(2):
            fe = fence()
            tw2 = dma(SP, W2, I["w2a2"].rearrange("p (a b) -> p a b", a=2), fe)
            fw = slice(None, None, None) if d == 0 else slice(None, None, -1)
            lo = 0 if d == 0 else 2
            pace[0], pace[2] = PACE, fill

            def delta(out, p):
                return tt(out, p[:, :, lo:lo + 512], p[:, :, 1:513], SUB)
            v(tt(T5[:, 0, :], pw[:, lo:lo + 512], pw[:, 1:513], SUB), tp, fe)
            tm = v(stt(T5[:, 1, fw], T5[:, 0, :], cols[:, K_MUWA + d:K_MUWA + d + 1], pw[:, 1:513], MUL, ADD), tk)
            t = s(act(T5[0:64, 2, :], T5[0:64, 1, :], ACT.Tanh), tm, fe)
            v(delta(T1, pk), fe)
            for c in range(3):
                k0 = K_MU + (d * 3 + 1) * 3 + c
                tkm = v(stt(K[:, c, fw], T1[:, c, :], cols[:, k0:k0 + 1], pk[:, c, 1:513], MUL, ADD))
            g(delta(P1, pv), tp, fe)
            for c in range(3):
                k0 = K_MU + (d * 3 + 2) * 3 + c
                g(ts(P1[:, c, :], P1[:, c, :], cols[:, k0:k0 + 1], MUL), tk)
            tvm = g(tt(VV[:, :, fw], P1, pv[:, :, 1:513], ADD))
            tsc = []
            for c in range(3):
                b = pb.take()
                t1 = pe([mm(PS[b][:, :], W2[0:64, d, 128 * c:128 * c + 128], T5[0:64, 2, :])], t, tw2, pb.rel[b], fe)
                t2 = s(act(T3[:, c, :], PS[b][:, :], ACT.Sigmoid, bias=cols[:, K_W0 + 3 * d + c:K_W0 + 3 * d + c + 1]), t1)
                pb.free(b, t2)
                b = pb.take()
                t1 = pe([mm(PS[b][:, :], W2[64:128, d, 128 * c:128 * c + 128], T5[64:128, 1, :])], tm, tw2, pb.rel[b])
                t2 = s(act(T2[:, c, :], PS[b][:, :], ACT.Sigmoid, bias=cols[:, K_A0 + 3 * d + c:K_A0 + 3 * d + c + 1]), t1)
                pb.free(b, t2)
                tsc = t2
            for c in range(3):
                tk1 = v(ts(T1[:, c, :], K[:, c, :], cols[:, K_KK + c:K_KK + c + 1], MUL))
            t = v(tt(T5[:, :, :], T1[:, :, :], T1[:, :, :], MUL), tok(PE))
            nr = []

            def use_norm(c, P, t):
                t = s(act(T5[:, c, :], P[:, :], ACT.Sqrt), t)
                nr.append(t)
                return t
            for c in range(3):
                g(ts(P1[:, c, :], T2[:, c, :], 1.0, SUB, cols[:, K_KA + c:K_KA + c + 1], MUL), tsc)
            g(ts(P1, P1, 1.0, ADD))
            tkp = g(tt(K, K, P1, MUL), tk1)
            head_sum(lambda c: T5[:, c, :], 3, use_norm, t)
            v(delta(P2, pr), fe)
            for c in range(3):
                k0 = K_MU + d * 9 + c
                trm = v(stt(R[:, c, fw], P2[:, c, :], cols[:, k0:k0 + 1], pr[:, c, 1:513], MUL, ADD))
            g(tt(P1, R, K, MUL), trm)
            for c in range(3):
                tbp = g(ts(P1[:, c, :], P1[:, c, :], cols[:, K_RK + c:K_RK + c + 1], MUL))
            v(ts(T3[:, :, :], T3[:, :, :], -math.exp(-0.5), MUL), tsc)
            for c in range(3):
                v(lambda e, c=c: e.tensor_tensor_scan(T4[:, c, :], cons[:, C_SCAN:C_SCAN + 512], T3[:, c, :], 0.0, MUL, ADD), tc)
            v(ts(T5[:, :, :], T5[:, :, :], 1e-12, MAX), nr)
            v(lambda e: e.reciprocal(T5[:, :, :], T5[:, :, :]))
            tkn = v(tt(T1[:, :, :], T1[:, :, :], T5[:, :, :], MUL))
            tbh = g(tt(T2, T2, T1, MUL), tkn)
            t = v(tt(T5[:, :, :], T4[:, :, :], T3[:, :, :], SUB))
            te0 = s(act(T5[:, :, :], T5[:, :, :], ACT.Exp), t)
            te1 = s(act(T3[:, :, :], T4[:, :, :], ACT.Exp, scale=-1.0), t)
            te2 = s(act(T4[:, :, :], T4[:, :, :], ACT.Exp), t)

            def use_bonus(c, P, t):
                if d == 0:
                    return v(tt(bS[:, c, :], P[:, :], VV[:, c, :], MUL), t, tvm, fe)
                v(tt(P2[:, c, :], P[:, :], VV[:, c, :], MUL), t, tvm)
                return v(tt(bS[:, c, ::-1], P2[:, c, :], bS[:, c, ::-1], ADD))
            head_sum(lambda c: P1[:, c, :], 3, use_bonus, tbp)
            for c in range(3):
                v(stt(AR[:, c, :, 0:128], T1[:, c, :].rearrange("p (j t) -> p j t", j=4), -1.0,
                      T5[:, c, :].rearrange("p (j t) -> p j t", j=4), MUL, MUL), te0, tok(PE), tkp)
            v(tt(T2[:, :, :], T2[:, :, :], T3[:, :, :], MUL), te1, tbh)
            v(tt(K[:, :, :], K[:, :, :], T3[:, :, :], MUL), tbp)
            for c in range(3):
                v(tt(AR[:, c, :, 128:256], R[:, c, :].rearrange("p (j t) -> p j t", j=4),
                     T4[:, c, :].rearrange("p (j t) -> p j t", j=4), MUL), te2)
            pace[0] = 0.0
            tel = v(cp(PC, T4[:, :, 63:512:64]))
            ts0 = g(lambda e: e.memset(SS[0], 0.0), fe)
            state = {"t": ts0, "cur": 0}
            done = [fe, fe]
            MX = [None]

            def spread(put, out, q, n, *deps):
                k_ = q.stop - q.start
                return put(tt(out[:, q, :].rearrange("p h (x c) -> p h x c", x=2),
                              MX[0][:, q, 0:64].rearrange("p h (x c) -> p h x c", x=1).to_broadcast([128, k_, 2, 64]),
                              cons[:, C_LVL + 128 * n:C_LVL + 128 * n + 128].rearrange("p (h x c) -> p h x c", h=1, x=2)
                              .to_broadcast([128, k_, 2, 64]), MUL), *deps)

            def pair(ap):
                return ap.rearrange("p (a b) -> p a b", a=2)

            def matrix(j):
                jt = slice(128 * j, 128 * j + 128)
                M4, ATok, At, U0 = M4s[j % 2], AToks[j % 2], Ats[j % 2], U0s[j % 2]
                MX[0] = M4
                free = done[j % 2]
                f0 = [tok(V), tok(S), tok(PE)]
                tm4 = []
                for hs in ((0, 2), (1, 3), (4,), (5,)):
                    b = pb.take()
                    fs = []
                    for n, h in enumerate(hs):
                        c, r = h // 2, slice(64 * (h % 2), 64 * (h % 2) + 64)
                        for m, src in enumerate((T2, K)):
                            for q in range(2):
                                lo_ = 256 * n + 128 * m
                                fs.append(mm(PS[b][64 * q:64 * q + 64, lo_:lo_ + 128], src[r, c, 128 * j + 64 * q:128 * j + 64 * q + 64],
                                             AR[r, c, j, :].rearrange("p (a b) -> p a b", a=2)[:, :, 64 * q:64 * q + 64]))
                    t = pe(fs, tel, pb.rel[b])
                    w_ = 256 * len(hs)
                    t = v(tt(M4[:, hs[0]:hs[-1] + 1:2, :], PS[b][:, 0:w_].rearrange("p (a b) -> p a b", b=256),
                             cons[:, C_M4:C_M4 + 256].rearrange("p (a b) -> p a b", a=1).to_broadcast([128, len(hs), 256]), MUL),
                          t, free, f0)
                    tm4.append(t)
                    pb.free(b, t)
                    yield
                for n, src in enumerate((None, T2, K, VV)):
                    b = pb.take()
                    t = pe([tr(PS[b][:, 128 * c:128 * c + 128], AR[:, c, j, 0:128] if src is None else src[:, c, jt])
                            for c in range(3)], tel, pb.rel[b])
                    t = s(act(ATok[:, n, :], PS[b][:, 0:384], ACT.Copy), t, free, f0)
                    pb.free(b, t)
                ttk = t
                yield
                G3 = [slice(2 * k, 2 * k + 2) for k in range(3)]
                tTT, tT = [None] * 3, [None] * 3
                for k, q in enumerate(G3):
                    spread(v, TT, q, 0, f0)
                    tTT[k] = v(tt(TT[:, q, :], TT[:, q, :], ident.rearrange("p (a b) -> p a b", a=1).to_broadcast([128, 2, 128]), ADD))
                for k, q in enumerate(G3):
                    b = pb.take()
                    t = pe([tr(PS[b][:, 128 * a:128 * a + 128], TT[:, 2 * k + a, :]) for a in range(2)], tTT[k], pb.rel[b])
                    tT[k] = s(act(Tm[:, q, :], pair(PS[b][:, 0:256]), ACT.Copy), t)
                    pb.free(b, tT[k])
                    yield
                tread = [f0, f0]
                tb = [None, None]

                def masked(n):
                    tb[n % 2] = spread(g, BT[n % 2], slice(0, 6), n, tm4, tread[n % 2])
                masked(1)
                masked(2)
                for n in range(1, 6):
                    tx1 = []
                    for k, q in enumerate(G3):
                        b = pb.take()
                        t = pe([mm(PS[b][:, 128 * a:128 * a + 128], BT[n % 2][:, 2 * k + a, :], Tm[:, 2 * k + a, :])
                                for a in range(2)], tb[n % 2], tT[k], tTT[k], pb.rel[b])
                        t1 = s(act(X1[:, q, :], pair(PS[b][:, 0:256]), ACT.Copy), t)
                        pb.free(b, t1)
                        tx1.append(t1)
                        yield
                    tread[n % 2] = [t]
                    if n + 2 < 6:
                        masked(n + 2)
                    for k, q in enumerate(G3):
                        b = pb.take()
                        t = pe([mm(PS[b][:, 128 * a:128 * a + 128], X1[:, 2 * k + a, :], TT[:, 2 * k + a, :]) for a in range(2)],
                               tx1[k], pb.rel[b])
                        tTT[k] = v(tt(TT[:, q, :], TT[:, q, :], pair(PS[b][:, 0:256]), ADD), t)
                        pb.free(b, tTT[k])
                        yield
                    if n < 5:
                        for k, q in enumerate(G3):
                            b = pb.take()
                            t = pe([tr(PS[b][:, 128 * a:128 * a + 128], TT[:, 2 * k + a, :]) for a in range(2)], tTT[k], pb.rel[b])
                            tT[k] = s(act(Tm[:, q, :], pair(PS[b][:, 0:256]), ACT.Copy), t)
                            pb.free(b, tT[k])
                            yield
                for q in range(2):
                    r = slice(64 * q, 64 * q + 64)
                    b = pb.take()
                    t = pe([mm(PS[b][r, 64 * h:64 * h + 64], M4[r, h, 128:192], ATok[r, 3, 64 * h:64 * h + 64]) for h in range(6)],
                           tm4, ttk, pb.rel[b])
                    t = s(act(MV[r, :], PS[b][r, 0:384], ACT.Copy), t, f0)
                    pb.free(b, t)
                yield
                b = pb.take()
                t = pe([mm(PS[b][64 * (h % 2):64 * (h % 2) + 64, 128 * (h // 2):128 * (h // 2) + 128],
                           ATok[:, 0, 64 * h:64 * h + 64], TT[:, h, :]) for h in range(6)], tTT, pb.rel[b])
                tat = s(act(At, PS[b][:, 0:384].rearrange("p (a b) -> p a b", a=3), ACT.Copy), t, free)
                pb.free(b, tat)
                yield
                b = pb.take()
                t = pe([mm(PS[b][:, 64 * h:64 * h + 64], TT[:, h, :], MV[:, 64 * h:64 * h + 64]) for h in range(6)],
                       tok(S), pb.rel[b])
                tu0 = s(act(U0, PS[b][:, 0:384], ACT.Copy), t, free)
                pb.free(b, tu0)
                state[j] = (tat, tu0)
                yield

            def chunks(j):
                M4, ATok, At, U0 = M4s[j % 2], AToks[j % 2], Ats[j % 2], U0s[j % 2]
                tat, tu0 = state[j]
                for q in range(2):
                    n = 2 * j + q
                    r = slice(64 * q, 64 * q + 64)
                    S0, S1 = SS[state["cur"]], SS[1 - state["cur"]]
                    tpc = g(tt(PCM, cons[:, C_BD:C_BD + 128].rearrange("p (a b) -> p a b", a=1).to_broadcast([128, 3, 128]),
                               PC[:, :, n:n + 1].to_broadcast([128, 3, 128]), MUL), tel, tok(V))
                    b = pb.take()
                    t = pe([mm(PS[b][r, 128 * p:128 * p + 128], At[:, p, r], S0[:, p, :]) for p in range(3)],
                           tat, state["t"], pb.rel[b])
                    tu = v(tt(U[r, :], PS[b][r, 0:384], U0[r, :], ADD), t, tu0)
                    pb.free(b, tu)
                    yield
                    b = pb.take()
                    fs = []
                    for p in range(3):
                        pc = slice(128 * p, 128 * p + 128)
                        fs += [mm(PS[b][:, pc], ATok[r, 1, pc], U[r, pc], True, False),
                               mm(PS[b][:, pc], ATok[r, 2, pc], ATok[r, 3, pc], False, True)]
                    t = pe(fs, tu, pb.rel[b])
                    v(tt(S1, PS[b][:, 0:384].rearrange("p (a b) -> p a b", a=3), S0, ADD), t)
                    state["t"] = v(tt(S1, S1, PCM, MUL), tpc)
                    pb.free(b, state["t"])
                    yield
                    b = pb.take()
                    fs = []
                    for p in range(3):
                        oc = slice(64 * p, 64 * p + 64)
                        fs.append(mm(PS[b][:, oc], S0[:, p, :], AR[:, p, j, 128 + 64 * q:192 + 64 * q], True, False))
                        for e2 in range(2):
                            h = 2 * p + e2
                            orow = slice(64 * e2, 64 * e2 + 64)
                            fs.append(mm(PS[b][orow, oc], U[r, 64 * h:64 * h + 64], M4[r, h, 64:128], False, False))
                            fs.append(mm(PS[b][orow, oc], ATok[r, 3, 64 * h:64 * h + 64], M4[r, h, 192:256], False, True))
                    t = pe(fs, pb.rel[b])
                    done[j % 2] = [t]
                    src = PS[b][:, 0:192].rearrange("p (a b) -> p a b", a=3)
                    if d == 0:
                        t = s(act(yS[:, :, 64 * n:64 * n + 64], src, ACT.Copy), t, fe)
                    else:
                        o_ = yS[:, :, 448 - 64 * n:512 - 64 * n]
                        t = v(tt(o_[:, :, ::-1], src, o_[:, :, ::-1], ADD), t)
                    pb.free(b, t)
                    state["cur"] = 1 - state["cur"]
                    yield

            if d == 1:
                mx, mT = at(0, 2, 1024), at(2048, 8, 256)
                fm = fence()
                tmx = dma(SP, mx, I["mem"].rearrange("(a p) f -> p a f", p=128), fm)
            before = iter(())
            for j in range(4):
                for n, _ in enumerate(matrix(j)):
                    if n % 4 == 2:
                        next(before, None)
                    if n % 3 == 2:
                        fill(FILL_M)
                for _ in before:
                    fill(1)
                before = chunks(j)
            for _ in before:
                fill(2)

        for _ in fill_g:
            pass
        t = rms_rows(mx, mx, 2, 1024.0, at(2048, 1024), small[:, 4:8], 1e-6, tmx, fm)
        tmt = to_feature(mx, mT, 2, K_MEM, fb, t)
        fe = fence()
        fsp = [fe, spilled[33], spilled[34]]
        o = YO = room - 4096 - 1536
        yR = at(o, 3, 512); o += 1536
        yN = at(o, 3, 512); o += 1536
        yM = at(o, 2, 512); o += 1024
        mk = at(o, 2, 256); o += 512
        mv = at(o, 2, 256); o += 512
        N1, N3, N4, N5 = at(8724, 3, 512), at(10260, 3, 512), at(11796, 3, 512), at(13332, 512)
        mq = at(16896, 2, 512)
        tg2 = dma(SP, G2, I["g2"], fe)
        tmq = dma(SP, mq, p_dram[:, 4608:5632].rearrange("p (a b) -> p a b", a=2), fe, [spilled[i] for i in (9, 10)])
        F = tail_is("fb", (4096, f32r), (4096, f32r), *[(2048, f32r)] * 4)
        YH, YL = v3(F[0], 8), v3(F[1], 8)
        HB2 = [(v3(F[2 + 2 * i], 8), v3(F[3 + 2 * i], 8)) for i in range(2)]
        tkv = []

        def mem_kv():
            for half in range(2):
                rn, w, tw = wtile()
                for a in range(2):
                    q = slice(128 * a, 128 * a + 128)
                    b = fb.take()
                    for k in range(8):
                        l_, r_ = (w[:, k, q], mT[:, k, :]) if half == 0 else (mT[:, k, q], w[:, k, :])
                        last = pe([mm(PS[b][:, 0:256], l_, r_, k == 0, k == 7)], tmt, tw, fb.rel[b])
                        if k % 2:
                            yield
                    tkv.append(s(act((mk, mv)[half][:, a, :], PS[b][:, 0:256], ACT.Copy), last, fe))
                    fb.free(b, tkv[-1])
                ring_free(rn, last)
        kv = mem_kv()

        def beside(n):
            for _ in range(n):
                next(kv, None)

        def use_mean(c, P, t):
            t = v(stt(N1[:, c, :], P[:, :], -1.0 / 64, yS[:, c, :], MUL, ADD), t, fe)
            return v(tt(N3[:, c, :], N1[:, c, :], N1[:, c, :], MUL))
        tg = s(act(N5, lg, ACT.Sigmoid), fe)
        head_sum(lambda c: yS[:, c, :], 3, use_mean, fe)
        tsq = tok(V)
        beside(2)
        gt = []
        for c in range(3):
            b = pb.take()
            gt.append((b, pe([mm(PS[b][:, :], G2[:, 128 * c:128 * c + 128], N5)], tg, tg2, pb.rel[b])))
        rs = []

        def use_var(c, P, t):
            t = v(ts(N4[:, c, :], P[:, :], 1.0 / 64, MUL, 64e-5, ADD), t)
            t2 = s(act(N4[:, c, :], N4[:, c, :], ACT.Sqrt), t)
            rs.append(t2)
            return t
        head_sum(lambda c: N3[:, c, :], 3, use_var, tsq)
        beside(100)
        v(lambda e: e.reciprocal(N4[:, :, :], N4[:, :, :]), rs)
        v(tt(N1[:, :, :], N1[:, :, :], N4[:, :, :], MUL))
        for c in range(3):
            v(ts(N1[:, c, :], N1[:, c, :], cols[:, K_LNG + c:K_LNG + c + 1], MUL, cols[:, K_LNB + c:K_LNB + c + 1], ADD))
        v(tt(N1[:, :, :], N1[:, :, :], bS[:, :, :], ADD))
        for c, (b, t) in enumerate(gt):
            tyr = v(tt(yR[:, c, :], N1[:, c, :], PS[b][:, :], MUL), t)
            pb.free(b, tyr)
        allb.rel.update(pb.rel)
        allb.rel.update(fb.rel)
        if stop == "rw":
            dump(yR)
            return finish(nc, ctx, PE, V, S, G, SP, sems)

        fg = [tok(PE), tyr]
        o = 0
        qT = at(o, 3, 512); o += 1536
        kT = at(o, 3, 512); o += 1536
        vt = at(o, 4, 384); o += 1536
        nb = at(o, 6, 1024); o += 6144
        Pb = [at(o + 512 * i, 512) for i in range(4)]; o += 2048
        PT = [at(o + 2048 * i, 4, 512) for i in range(2)]; o += 4096
        assert o <= 16896 and 16896 + 1024 <= YO
        tqk = [dma(SP, qT, p_dram[:, 0:1536].rearrange("p (a b) -> p a b", a=3), fg, [spilled[i] for i in range(3)]),
               dma(SP, kT, p_dram[:, 1536:3072].rearrange("p (a b) -> p a b", a=3), fg, [spilled[i] for i in range(3, 6)])]
        for c in range(3):
            tqk.append(dma(SP, vt[:, :, 128 * c:128 * c + 128],
                           p_dram[:, 3072 + 512 * c:3584 + 512 * c].rearrange("p (a b) -> p a b", a=4), fg, spilled[6 + c]))
        tnb = dma(SP, nb, I["nab"].rearrange("p (a b) -> p a b", a=6), fg)
        txx = dma(SP, X, I["x"].rearrange("(a p) f -> p a f", p=128), fg)
        prel, ptrel = [fg] * 4, [fg] * 2

        def attention(nh, ntile, q_, k_, nk, bias, v_, out, Pb, PT, prel, ptrel, sm, deps, causal=False, each=None):
            sb_ = Banks([0, 1, 2])
            tb_ = Banks([3, 4, 5])
            ob_ = Banks([6, 7])
            for x_ in (sb_, tb_, ob_):
                for i in x_.ids:
                    x_.rel[i] = allb.rel[i]
            units = [(h, i) for h in range(nh) for i in range(ntile)]
            info = {}
            ptt = {}

            def scores(u):
                h, i = units[u]
                r = slice(64 * (h % 2), 64 * (h % 2) + 64)
                b = sb_.take()
                n = nk(i)
                t = pe([mm(PS[b][:, 0:n], q_[r, h // 2, 128 * i:128 * i + 128], k_[r, h // 2, 0:n])], deps, sb_.rel[b])
                P = Pb[u % 4][:, 0:n]
                m = sm[:, u % 8:u % 8 + 1]
                l = sm[:, 8 + u % 8:9 + u % 8]
                if bias is not None:
                    t = v(lambda e: e.tensor_tensor_reduce(out=P, in0=PS[b][:, 0:n], in1=bias(h, i), scale=-1.0, scalar=3.0e38,
                                                           op0=ADD, op1=ALU.min, accum_out=m), t, prel[u % 4])
                    sb_.free(b, t)
                    t = s(act(P, P, ACT.Exp, bias=m, scale=-1.0, accum_out=l), t)
                else:
                    t = v(lambda e: e.tensor_reduce(m, PS[b][:, 0:n], AX.X, MAX, negate=True), t)
                    t = s(act(P, PS[b][:, 0:n], ACT.Exp, bias=m, accum_out=l), t, prel[u % 4])
                    sb_.free(b, t)
                info[u] = (P, l, t)

            def norm(u):
                P, l, t = info[u]
                v(lambda e: e.reciprocal(l, l), t)
                info[u] = v(ts(P, P, l, MUL))

            def turn(u):
                h, i = units[u]
                P = Pb[u % 4]
                n = nk(i) // 128
                b = tb_.take()
                t = pe([tr(PS[b][:, 128 * k:128 * k + 128], P[:, 128 * k:128 * k + 128]) for k in range(n)], info[u], tb_.rel[b])
                prel[u % 4] = t
                t = s(act(PT[h % 2][:, 0:n, 128 * i:128 * i + 128], PS[b][:, 0:128 * n].rearrange("p (a b) -> p a b", a=n), ACT.Copy),
                      t, ptrel[h % 2])
                tb_.free(b, t)
                if i == ntile - 1:
                    nkc = nk(ntile - 1) // 128
                    if h % 2 == 0:
                        info["o"] = ob_.take()
                    b = info["o"]
                    orow = slice(64 * (h % 2), 64 * (h % 2) + 64)
                    lo = (lambda k: 128 * k) if causal else (lambda k: 0)
                    t = pe([mm(PS[b][orow, lo(k):512], v_[:, k, 64 * h:64 * h + 64], PT[h % 2][:, k, lo(k):512], k == 0, k == nkc - 1)
                            for k in range(nkc)], t, ob_.rel[b])
                    ptrel[h % 2] = t
                    if h % 2:
                        t = v(cp(out[:, h // 2, :], PS[b][:, :]), t)
                        ob_.free(b, t)
                        info["y"] = t
                        if each is not None:
                            info["y"] = each(h // 2, t)
            for u in range(len(units) + 3):
                if u < len(units):
                    scores(u)
                if 1 <= u <= len(units):
                    norm(u - 1)
                if u == len(units) - 1:
                    info["s"] = [tok(PE), tok(V)]
                if u >= 3:
                    turn(u - 3)
            for x_ in (sb_, tb_, ob_):
                allb.rel.update(x_.rel)
            return info["y"], info["s"]

        def part(src, k0):
            return lambda c, t: halve(src[:, c, :], YH[:, k0 + c, :], YL[:, k0 + c, :], t, fsp)

        wb = Weights(HB2, 256, 8, fsp, True)
        attention(4, 4, mq, mk, lambda i: 256, None, mv, yM, Pb, PT, prel, ptrel, small[:, 16:32], [tmq, tkv],
                  each=part(yM, 6))
        for c in range(3):
            part(yR, 3)(c, tyr)
        wb.prepare()
        if stop == "mem":
            dump(yM)
            return finish(nc, ctx, PE, V, S, G, SP, sems)
        ty, tsc_ = attention(6, 4, qT, kT, lambda i: 512, lambda h, i: nb[:, h, 64 * (7 - 2 * i):64 * (7 - 2 * i) + 512], vt, yN,
                             Pb, PT, prel, ptrel, small[:, 16:32], [tqk, tnb], each=part(yN, 0))
        if stop == "na":
            dump(yN)
            return finish(nc, ctx, PE, V, S, G, SP, sems)

        fe = fence()
        mg = at(13824, 8, 512)
        sgs, tsg = [], []
        for f2, (o, rel) in enumerate(((4608, tsc_), (7680, tsc_), (0, tsc_), (10752, fe))):
            sgs.append(at(o, 6, 512))
            tsg.append(dma(SP, sgs[f2], p_dram[:, 512 * (11 + 6 * f2):512 * (17 + 6 * f2)].rearrange("p (a b) -> p a b", a=6),
                           rel, [spilled[11 + 6 * f2 + i] for i in range(6)]))
        kc0 = (0, 3, 6)
        kcn = (3, 3, 2)
        tmg = []
        for f2 in range(4):
            sg = [sgs[f2][:, i, :] for i in range(6)]
            r = wb.get()
            for a in range(2):
                f = 2 * f2 + a
                for br in range(3):
                    b = allb.take()
                    q = slice(128 * a, 128 * a + 128)
                    last = t = pe(product(PS[b][:, :], [((r[0][:, k, q], r[1][:, k, q]), (YH[:, k, :], YL[:, k, :]))
                                                        for k in range(kc0[br], kc0[br] + kcn[br])]), r[2], ty, allb.rel[b])
                    if br == 0:
                        t = v(tt(mg[:, f, :], sg[a], PS[b][:, :], MUL), t, tsg[f2], fe)
                    else:
                        t = v(tt(sg[2 * br + a], sg[2 * br + a], PS[b][:, :], MUL), t, tsg[f2])
                    allb.free(b, t)
                v(tt(mg[:, f, :], mg[:, f, :], sg[2 + a], ADD))
                t = v(tt(mg[:, f, :], mg[:, f, :], sg[4 + a], ADD))
            wb.done(r, last)
        fm = fence()
        for c in range(2):
            q = slice(4 * c, 4 * c + 4)
            t = s(act(YH[:, q, :], mg[:, q, :], ACT.Copy), fm) if c else v(cp(YH[:, q, :], mg[:, q, :]), fm)
            tmg = v(tt(YL[:, q, :], mg[:, q, :], YH[:, q, :].bitcast(f32), SUB), t)

        def out_proj(wb, src, each, *deps):
            t = None
            for n in range(4):
                r = wb.get()
                for i in range(4):
                    b = allb.take()
                    last = t = proj_t(r, src, i, b, deps)
                    t = v(tt(X[:, i, 256 * n:256 * n + 256], X[:, i, 256 * n:256 * n + 256], PS[b][:, 0:256], ADD), t)
                    allb.free(b, t)
                    if n == 3:
                        each(i, t)
                wb.done(r, last)
            return t
        XN = at(0, 4, 1024)
        hT = at(4096, 8, 512)
        JK = at(8192, 1024)
        txn, th = {}, {}
        rt = at(9216, 8, 16)
        trt = dma(SP, rt, I["rt"].rearrange("p (a b) -> p a b", a=8), fm)
        rb = allb.ids.pop()

        def feature(i):
            th[i] = tile_to_feature(i, XN, hT, K_FFN, allb, txn[i])

        def route(i):
            return pe([mm(PS[rb][:, 16 * i:16 * i + 16], hT[:, k, 128 * i:128 * i + 128], rt[:, k, :], k == 0, k == 7)
                       for k in range(8)], th[i], trt, allb.rel[rb])

        def normed(i, t):
            txn[i] = rms_tile(i, X, XN, JK, small[:, 0:4], 1e-6, t, fm)
            if i:
                feature(i - 1)
            if i > 1:
                route(i - 2)
        tX = out_proj(wb, (YH, YL), normed, tmg, txx)
        if stop == "mix1":
            dump(X)
            return finish(nc, ctx, PE, V, S, G, SP, sems)

        fe = fence()
        F = tail_is("ga", (16384, f32))
        ring_grow([F[0][:, 2048 * i:2048 * i + 2048] for i in range(8)], fe)
        lgt = at(9344, 4, 16)
        aff = at(9408, 512)
        top = at(9920, 64)
        idxu = AR_[:, D0 + 9984:D0 + 10048].bitcast(u32)
        idxf = at(10048, 64)
        tv8 = at(10112, 8)
        ti8 = at(10120, 8)
        ii8 = AR_[:, D0 + 10128:D0 + 10136].bitcast(i32)
        two = at(10144, 2, 128)
        thd = dma(G, h_dram.rearrange("(a p) f -> p a f", p=128), XN, txn[3])
        feature(3)
        route(2)
        t = route(3)
        b = rb
        allb.ids.append(rb)
        l3 = PS[b][:, 0:64].rearrange("p (a b) -> p a b", a=4)
        mxs = small[:, 32:36]
        v(lambda e: e.tensor_reduce(mxs, l3, AX.X, MAX), t)
        t = v(tt(lgt, l3, bc(mxs.rearrange("p (a b) -> p a b", b=1), 16), SUB))
        allb.free(b, t)
        t = s(act(lgt, lgt, ACT.Exp), t)
        v(lambda e: e.tensor_reduce(mxs, lgt, AX.X, ADD), t)
        v(lambda e: e.reciprocal(mxs, mxs))
        t = v(tt(lgt, lgt, bc(mxs.rearrange("p (a b) -> p a b", b=1), 16), MUL))
        b = allb.take()
        t = pe([tr(PS[b][0:16, 128 * i:128 * i + 128], lgt[:, i, :]) for i in range(4)], t, allb.rel[b])
        t = v(cp(aff[0:16, :], PS[b][0:16, :]), t)
        allb.free(b, t)
        for n in range(8):
            q = slice(8 * n, 8 * n + 8)
            v(lambda e, q=q: e.max(top[0:16, q], aff[0:16, :]))
            v(lambda e, q=q: e.max_index(idxu[0:16, q], top[0:16, q], aff[0:16, :]))
            v(lambda e, q=q: e.match_replace(aff[0:16, :], top[0:16, q], aff[0:16, :], -1.0))
        t = v(cp(idxf[0:16, :], idxu[0:16, :]))
        b = allb.take()
        t0 = allb.rel[b]
        for n, (src, dst) in enumerate(((top, tv8), (idxf, ti8))):
            for hh in range(2):
                em = cons[0:16, C_EM + 64 * hh:C_EM + 64 * hh + 64]
                t = v(tt(two[0:16, n, 64 * hh:64 * hh + 64], src[0:16, :], em, MUL))
            t = pe([mm(PS[b][:, 8 * n:8 * n + 8], two[0:16, n, :], cons[0:16, C_ES:C_ES + 8])], t, t0)
            tr1 = tr2 = v(cp(dst, PS[b][:, 8 * n:8 * n + 8]), t)
            t0 = tr1
        allb.free(b, tr1)
        t = v(cp(ii8, ti8), tr2)
        fe = fence()
        XE = [at(10496 + 1024 * i, 1024) for i in range(2)]
        XT = [at(12544 + 1024 * i, 8, 128) for i in range(2)]
        AC = at(14592, 2048)
        AT = at(16640, 16, 128)
        YE = [at(18688 + 1024 * i, 1024) for i in range(2)]
        PM = [at(20736 + 512 * i, 512) for i in range(2)]
        gb, ub, db, xb_ = Banks([0, 1]), Banks([2, 3]), Banks([4, 5]), Banks([6, 7])
        for x_ in (gb, ub, db, xb_):
            for i in x_.ids:
                x_.rel[i] = allb.rel[i]
        gath = {}
        xerel = [fe, fe]

        def fetch(c):
            gath[c] = gather(XE[c % 2], h_dram, ii8[:, c:c + 1], t, thd, xerel[c % 2], on=f"xe{c % 2}")

        def half_w(name, e, k2, f0):
            return I[name][e, 256 * k2:256 * k2 + 256, f0:f0 + 1024].rearrange("(a p) f -> p a f", p=128)

        def etile(src):
            n, buf, tk_ = ring_next([(2, src)])
            return n, buf.rearrange("p (k c) -> p k c", k=2), tk_

        xtrel = [fe, fe]
        yerel = [fe, fe]
        acrel = atrel = fe
        xtt = {}

        def turn_x(c):
            XEc, XTc = XE[c % 2], XT[c % 2]
            ts_ = []
            for k4 in range(2):
                b = xb_.take()
                t = pe([tr(PS[b][:, 128 * q:128 * q + 128], XEc[:, 512 * k4 + 128 * q:512 * k4 + 128 * q + 128]) for q in range(4)],
                       gath[c], xb_.rel[b])
                xerel[c % 2] = [t]
                for q in range(4):
                    k = 4 * k4 + q
                    t2 = v(colmul(XTc[:, k, :], PS[b][:, 128 * q:128 * q + 128], K_FFN + k), t, xtrel[c % 2])
                xb_.free(b, t2)
                ts_.append(t2)
            xtt[c] = ts_

        fetch(0)
        ring_grow([at(2048 * i, 2048) for i in range(4)], [fe, thd, gath[0]], last=True)
        turn_x(0)
        for c in range(8):
            if c + 1 < 8:
                fetch(c + 1)
            XTc = XT[c % 2]
            tpm = v(ts(PM[c % 2], cons[:, C_IOTA:C_IOTA + 512], ti8[:, c:c + 1], ALU.is_equal, tv8[:, c:c + 1], MUL),
                    tr1, tr2, yerel[c % 2])
            for fh in range(2):
                for nm, bk in (("eg", gb), ("eu", ub)):
                    for k2 in range(4):
                        for e2 in range(2):
                            rn, w, tw = etile(half_w(nm, 2 * c + e2, k2, 1024 * fh))
                            orow = slice(64 * e2, 64 * e2 + 64)
                            fs = []
                            for kk in range(2):
                                k = 2 * k2 + kk
                                for n in range(2):
                                    fs.append(mm(PS[bk.ids[n]][orow, :], XTc[:, k, orow], w[:, kk, 512 * n:512 * n + 512], k == 0, k == 7))
                            t = pe(fs, tw, xtt[c], [bk.rel[i] for i in bk.ids] if k2 == 0 else None)
                            ring_free(rn, t)
                    if nm == "eg":
                        tg_ = t
                        for n in range(2):
                            t = s(act(AC[:, 1024 * fh + 512 * n:1024 * fh + 512 * n + 512], PS[gb.ids[n]][:, :], ACT.Silu), tg_, acrel)
                            gb.free(gb.ids[n], t)
                        tsl = t
                tu_ = t_last = tok(PE)
                for n in range(2):
                    a_ = AC[:, 1024 * fh + 512 * n:1024 * fh + 512 * n + 512]
                    t = v(tt(a_, a_, PS[ub.ids[n]][:, :], MUL), tu_, tsl)
                    ub.free(ub.ids[n], t)
                tac = t
                for f4 in range(2):
                    b = xb_.take()
                    f0 = 8 * fh + 4 * f4
                    t = pe([tr(PS[b][:, 128 * q:128 * q + 128], AC[:, 128 * (f0 + q):128 * (f0 + q) + 128]) for q in range(4)],
                           tac, xb_.rel[b])
                    acrel = [t]
                    t = s(act(AT[:, f0:f0 + 4, :], PS[b][:, :].rearrange("p (a b) -> p a b", a=4), ACT.Copy), t, atrel)
                    xb_.free(b, t)
                tat = t
            xtrel[c % 2] = [tu_]
            if c + 1 < 8:
                turn_x(c + 1)
            for f2 in range(8):
                for e2 in range(2):
                    rn, w, tw = etile(I["ed"][2 * c + e2, 256 * f2:256 * f2 + 256, :].rearrange("(a p) f -> p a f", p=128))
                    orow = slice(64 * e2, 64 * e2 + 64)
                    fs = [mm(PS[db.ids[n]][orow, :], AT[:, 2 * f2 + kk, orow], w[:, kk, 512 * n:512 * n + 512],
                             f2 + kk == 0, f2 == 7 and kk == 1) for kk in range(2) for n in range(2)]
                    t = pe(fs, tw, tat, [db.rel[i] for i in db.ids] if f2 == 0 else None)
                    ring_free(rn, t)
            atrel = [t]
            for n in range(2):
                t2 = s(act(YE[c % 2][:, 512 * n:512 * n + 512], PS[db.ids[n]][:, :], ACT.Copy), t, yerel[c % 2])
                db.free(db.ids[n], t2)
            for i in range(4):
                for n in range(2):
                    b = xb_.take()
                    t = pe([mm(PS[b][:, :], PM[c % 2][:, 128 * i:128 * i + 128], YE[c % 2][:, 512 * n:512 * n + 512])],
                           t2, tpm, xb_.rel[b])
                    yerel[c % 2] = [t]
                    t3 = v(tt(X[:, i, 512 * n:512 * n + 512], X[:, i, 512 * n:512 * n + 512], PS[b][:, :], ADD), t)
                    xb_.free(b, t3)
        for x_ in (gb, ub, db, xb_):
            allb.rel.update(x_.rel)
        ring_shrink()
        first = wtile()
        if stop == "moe":
            dump(X)
            return finish(nc, ctx, PE, V, S, G, SP, sems)

        fe = fence()
        XN = at(0, 4, 1024)
        F = tail_is("fc", (4096, f32r), (4096, f32r), *[(2048, f32r)] * 4)
        h2 = (v3(F[0], 8), v3(F[1], 8))
        HB2 = [(v3(F[2 + 2 * i], 8), v3(F[3 + 2 * i], 8)) for i in range(2)]
        aT = at(4096, 8, 512)
        sq = at(4096, 4, 512)
        JK = at(6144, 1024)
        rows = at(20480, 2560)
        gu = at(8192, 4, 512)
        gv = at(10240, 4, 512)
        qT = at(12288, 4, 512)
        kT = at(14336, 4, 512)
        vt = at(16384, 4, 512)
        ws = at(18432, 8, 128)
        bs_ = at(19456, 8)
        JK2 = at(19584, 512)
        trw = dma(SP, rows, I["rows"], fe)
        tws = dma(SP, ws, I["wsT"].rearrange("p (a b) -> p a b", a=8), fe)
        tbs = dma(SP, bs_, I["bsT"], fe)
        wb = Weights(HB2, 256, 14, fe, True)
        wb.tile, wb.lo, wb.left = first, 0, wb.left - 1
        for i in range(4):
            rms_tile(i, X, XN, JK, small[:, 0:4], 1e-6, fe)
            if i:
                t = v(tt(X[:, i - 1, :], XN[:, i - 1, :], rows[:, 0:1024], MUL), trw)
                rms_tile(i - 1, X, XN, JK, small[:, 4:8], 1e-6, t)
        t = v(tt(X[:, 3, :], XN[:, 3, :], rows[:, 0:1024], MUL), trw)
        wb.prepare()
        t = rms_tile(3, X, XN, JK, small[:, 4:8], 1e-6, t)
        th = to_feature(XN, None, 4, K_MIX2, allb, t, hl=h2)
        twm = g(tt(ws, ws, cons[:, C_WM:C_WM + 128].rearrange("p (a b) -> p a b", a=1).to_broadcast([128, 8, 128]), MUL), tws)

        def rows_of(dst, n, func):
            r = wb.get()
            for i in range(4):
                b = allb.take()
                t = proj_t(r, h2, i, b, th)
                t2 = s(act(dst[:, i, 256 * n:256 * n + 256], PS[b][:, 0:256], func), t, fe)
                allb.free(b, t2)
            wb.done(r, t)
            return t2

        def features_of(dst, n):
            r = wb.get()
            for a in range(2):
                b = allb.take()
                q = slice(128 * a, 128 * a + 128)
                t = proj_f((r[0][:, :, q], r[1][:, :, q], r[2]), h2, b, th)
                t2 = s(act(dst[:, 2 * n + a, :], PS[b][:, :], ACT.Copy), t, fe)
                allb.free(b, t2)
            wb.done(r, t)
            return t2

        def head_norm(arr, kcol, scale, tin):
            t = v(tt(sq, arr, arr, MUL), tin, tok(PE))
            t9 = []
            for c in range(4):
                b = allb.take()
                t2 = pe([mm(PS[b][:, :], ones, sq[:, c, :])], t, allb.rel[b])
                t3 = v(ts(sq[:, c, :], PS[b][:, :], 1.0 / 64, MUL, 1e-6, ADD), t2)
                allb.free(b, t3)
                t9.append(s(act(sq[:, c, :], sq[:, c, :], ACT.Sqrt), t3))
            v(lambda e: e.reciprocal(sq, sq), t9)
            v(tt(arr, arr, sq, MUL))
            return v(ts(arr, arr, cols[:, kcol:kcol + 1], MUL, scale, MUL))

        for n in range(2):
            tgv = rows_of(gv, n, ACT.Gelu_apprx_tanh)
        for n in range(2):
            tgu_ = rows_of(gu, n, ACT.Gelu_apprx_tanh)
        ab = at(0, 8, 512)
        tab = dma(SP, ab, I["abias"].rearrange("p (a b) -> p a b", a=8), th)
        tq_ = [features_of(qT, n) for n in range(2)]
        t = rms_rows(gv, gv, 4, 512.0, JK2, small[:, 0:4], 1e-6, tgv)
        for i in range(4):
            tgn = v(tt(gv[:, i, :], gv[:, i, :], rows[:, 2048:2560], MUL), trw)
        tk_ = [features_of(kT, n) for n in range(2)]
        tnq = head_norm(qT, K_QN, 0.125, tq_)
        tvv = [rows_of(vt, 0, ACT.Copy)]
        for i in range(4):
            b = allb.take()
            t = pe([mm(PS[b][:, 64 * q:64 * q + 64], ws[:, q, :], gv[:, i, 64 * q:64 * q + 64]) for q in range(8)],
                   tgn, twm, allb.rel[b])
            t = v(tt(JK2.rearrange("p (a b) -> p a b", a=8), PS[b][:, :].rearrange("p (a b) -> p a b", a=8),
                     bc(bs_.rearrange("p (a b) -> p a b", b=1), 64), ADD), t, tbs)
            allb.free(b, t)
            tgu = v(tt(gu[:, i, :], gu[:, i, :], JK2, MUL), tgu_)
        tnk = head_norm(kT, K_KN, 1.0, tk_)
        tvv.append(rows_of(vt, 1, ACT.Copy))
        for c in range(4):
            b = allb.take()
            t = pe([tr(PS[b][:, 128 * i:128 * i + 128], gu[:, i, 128 * c:128 * c + 128]) for i in range(4)], tgu, allb.rel[b])
            t = s(act(aT[:, c, :], PS[b][:, :], ACT.Copy), t, fe, tnk)
            allb.free(b, t)
        taT = t
        PT = [at(8192 + 2048 * i, 4, 512) for i in range(2)]
        Pb = [at(18432 + 512 * i, 512) for i in range(4)]
        fh_ = [tok(PE), tok(V)]
        ta2, _ = attention(8, 4, qT, kT, lambda i: 128 * (i + 1), lambda h, i: ab[:, h, 384 - 128 * i:512], vt, aT[:, 4:8, :],
                        Pb, PT, [fh_] * 4, [fh_] * 2, small[:, 16:32], [tab, tnq, tnk, tvv, taT], causal=True)
        fm2 = fence()
        ta2 = halve(aT, h2[0], h2[1], taT, ta2)
        XN = at(0, 4, 1024)
        JK = at(16384, 1024)

        def normed_2(i, t):
            txn[i] = rms_tile(i, X, XN, JK, small[:, 0:4], 1e-6, t, fm2)
        tX = out_proj(wb, h2, normed_2, ta2)
        first = wtile()
        if stop == "mix2":
            dump(X)
            return finish(nc, ctx, PE, V, S, G, SP, sems)

        fe = fence()
        qT = at(8192, 16, 512)
        EX, = tail_is("ex", (4096, f32))
        F = tail_is("fd", (4096, f32r), (4096, f32r), *[(1024, f32r)] * 4, level=1)
        h2 = (v3(F[0], 8), v3(F[1], 8))
        sk = v3(EX[:, 0:2048], 16)
        wb = Weights([(v3(F[2 + 2 * i], 8), v3(F[3 + 2 * i], 8)) for i in range(2)], 128, 8, fe, True)
        wb.tile, wb.lo, wb.left = first, 0, wb.left - 1
        tsk = dma(SP, sk, I["skT"].rearrange("p (a b) -> p a b", a=16), fe)
        t = txn[3]
        wb.prepare()
        th = to_feature(XN, None, 4, K_FFN2, allb, t, hl=h2)
        for i in range(4):
            txb = v(tt(XN[:, i, :], XN[:, i, :], rows[:, 1024:2048], MUL), th, tok(PE))
        o = D0 + 20480
        sc = fl(o, 2, 2, 128)
        cand = fl(o + 512, 256)
        o = D0 + 22528
        oh = fl(o + 336, 2, 16, 16)
        best = fl(o, 8, 16)
        st_ = fl(o + 128, 2, 16)
        siu = AR_[:, o + 160:o + 192].bitcast(u32).rearrange("p (a b) -> p a b", a=2)
        sif = fl(o + 192, 2, 16)
        posu = AR_[:, o + 224:o + 240].bitcast(u32)
        pai = AR_[:, o + 240:o + 272].bitcast(u32).rearrange("p (a b) -> p a b", a=2)
        pf = fl(o + 272, 2, 16)
        e12 = fl(o + 304, 2, 16)
        eidx = [AR_[:, D0 + 17408 + 128 * i:D0 + 17408 + 128 * i + 128].bitcast(i32) for i in range(4)]
        gw = at(17920, 4, 128)
        dots = at(18432, 4, 128)
        io16 = cons[:, C_IOTA:C_IOTA + 16].rearrange("p (a b) -> p a b", a=1)
        teidx, wtk, weighed = {}, {}, set()
        JV = [at(16384, 1024), at(18944, 1024)]
        scfree = [fe, fe]
        tqh = {}

        last_c = [fe]

        def vc(fn, *deps):
            last_c[0] = V.add([fn], [deps, last_c[0]], False)
            return last_c[0]

        def choose(i, h):
            b = allb.take()
            t = pe([mm(PS[b][:, 128 * q:128 * q + 128], qT[:, 2 * h + q, 128 * i:128 * i + 128], sk[:, 2 * h + q, :]) for q in range(2)],
                   tqh[h], tsk, allb.rel[b])
            S_ = sc[:, h % 2, :, :]
            t = s(act(S_, PS[b][:, 0:256].rearrange("p (a b) -> p a b", a=2), ACT.Copy), t, scfree[h % 2])
            allb.free(b, t)
            for q in range(2):
                vc(lambda e, q=q: e.max(st_[:, q, 0:8], S_[:, q, :]), t)
                yield
                vc(lambda e, q=q: e.max_index(siu[:, q, 0:8], st_[:, q, 0:8], S_[:, q, :]))
                yield
                vc(lambda e, q=q: e.match_replace(S_[:, q, :], st_[:, q, 0:8], S_[:, q, :], -3.0e38))
                yield
                vc(lambda e, q=q: e.max(st_[:, q, 8:16], S_[:, q, :]))
                yield
                scfree[h % 2] = vc(lambda e, q=q: e.max_index(siu[:, q, 8:16], st_[:, q, 8:16], S_[:, q, :]))
                yield
            vc(cp(sif, siu))
            yield
            vc(tt(cand.rearrange("p (a b) -> p a b", a=16), bc(st_[:, 0, :].rearrange("p (a b) -> p a b", b=1), 16),
                 st_[:, 1, :].rearrange("p (a b) -> p a b", a=1).to_broadcast([128, 16, 16]), ADD))
            yield
            vc(lambda e: e.max(best[:, h, 0:8], cand))
            yield
            vc(lambda e: e.max_index(posu[:, 0:8], best[:, h, 0:8], cand))
            yield
            vc(lambda e: e.match_replace(cand, best[:, h, 0:8], cand, -3.0e38))
            yield
            vc(lambda e: e.max(best[:, h, 8:16], cand))
            yield
            vc(lambda e: e.max_index(posu[:, 8:16], best[:, h, 8:16], cand))
            yield
            vc(ts(pai[:, 0, :], posu, 4, ALU.logical_shift_right))
            yield
            vc(ts(pai[:, 1, :], posu, 15, ALU.bitwise_and))
            yield
            vc(cp(pf, pai))
            yield
            vc(tt(oh, pf.rearrange("p a (b c) -> p a b c", c=1).to_broadcast([128, 2, 16, 16]),
                 io16.rearrange("p (c a) b -> p c a b", c=1).to_broadcast([128, 2, 16, 16]), ALU.is_equal))
            yield
            vc(tt(oh, oh, sif.rearrange("p a (c b) -> p a c b", c=1).to_broadcast([128, 2, 16, 16]), MUL))
            yield
            vc(lambda e: e.tensor_reduce(e12, oh, AX.X, ADD))
            yield
            teidx[i, h] = vc(stt(eidx[i][:, 16 * h:16 * h + 16], e12[:, 0, :], 128.0, e12[:, 1, :], MUL, ADD))
            yield
            if h == 7:
                g3 = gw[:, i, :].rearrange("p (a b) -> p a b", a=8)
                t = vc(tt(g3, best, best[:, :, 0:1].to_broadcast([128, 8, 16]), SUB))
                yield
                t = s(act(g3, g3, ACT.Exp), t)
                vc(lambda e: e.tensor_reduce(small[:, 40:48], g3, AX.X, ADD), t)
                yield
                vc(lambda e: e.reciprocal(small[:, 40:48], small[:, 40:48]))
                yield
                vc(tt(g3, g3, bc(small[:, 40:48].rearrange("p (a b) -> p a b", b=1), 16), MUL))
                weighed.add(i)
                yield

        def choose_all(i):
            for h in range(8):
                yield from choose(i, h)

        GB = [at(4096 + 1024 * i, 1024) for i in range(4)] + [EX[:, 2048 + 1024 * i:3072 + 1024 * i] for i in range(2)]
        gr = [[txb, th]] * 6
        last_c[0] = txb
        names = [f"gb{i}" for i in range(6)]
        gn = [0]
        outt = []
        last_u, last_v = [tok(V), tok(V)], [tok(V), tok(V)]

        def expert(kind, i, k):
            sl = gn[0] % len(GB)
            gn[0] += 1
            buf = GB[sl]
            t = gather(buf, I["peer_u" if kind == "u" else "peer_v"], eidx[i][:, k:k + 1], teidx[i, k // 16], gr[sl], on=names[sl])
            if kind == "u":
                t = vu(lambda e: e.tensor_tensor_reduce(out=JV[k % 2], in0=buf, in1=XN[:, i, :], scale=1.0, scalar=0.0,
                                                        op0=MUL, op1=ADD, accum_out=dots[:, i, k:k + 1]), t, txb, fe, last_u[0])
                last_u[:] = [last_u[1], t]
                gr[sl] = t
                if k == 127:
                    t = s(act(dots[:, i, :], dots[:, i, :], ACT.Gelu_apprx_tanh), t)
                    wtk[i] = t
            else:
                if k == 0:
                    wtk[i] = v(tt(dots[:, i, :], dots[:, i, :], gw[:, i, :], MUL), wtk[i])
                    last_v[:] = [wtk[i]] * 2
                acc = X[:, i, :] if k % 2 == 0 else XN[:, i, :]
                if k == 1:
                    f_ = ts(acc, buf, dots[:, i, k:k + 1], MUL)
                else:
                    f_ = stt(acc, buf, dots[:, i, k:k + 1], acc, MUL, ADD)
                gr[sl] = last_v[k % 2] = vu(f_, t, wtk[i], last_v[k % 2])
                if k == 127:
                    last_v[0] = vu(tt(X[:, i, :], X[:, i, :], XN[:, i, :], ADD), last_v)

        def project(n, a):
            r = wb.get()
            b = allb.take()
            t = proj_f(r, h2, b, th)
            wb.done(r, t)
            tqh[n] = s(act(qT[:, 2 * n + a, :], PS[b][:, :], ACT.Copy), t, fe)
            allb.free(b, tqh[n])

        project(0, 0)
        project(0, 1)
        for n in range(9):
            c_ = choose(0, n) if n < 8 else iter(())
            for k in range(16):
                if n < 7 and k in (2, 8):
                    project(n + 1, k // 8)
                if n:
                    expert("u", 0, 16 * (n - 1) + k)
                next(c_, None)
                next(c_, None)
            for _ in c_:
                pass
            if n == 7:
                last_proj = [tok(PE), tok(V)]
        F, = tail_is("gb", (12288, f32), level=1)
        at_ = gn[0] % 6
        more = [F[:, 1024 * i:1024 * i + 1024] for i in range(12)]
        GB = GB[at_:] + more + GB[:at_]
        gr = gr[at_:] + [last_proj] * 12 + gr[:at_]
        names = [f"gb{(at_ + i) % 6}" for i in range(6)]
        names = names[:6 - at_] + [f"gb{6 + i}" for i in range(12)] + names[6 - at_:]
        gn[0] = 0
        nxt, due = (x_ for i in range(1, 4) for x_ in choose_all(i)), [0.0]

        def step():
            due[0] += 0.95
            while due[0] >= 1.0:
                due[0] -= 1.0
                next(nxt, None)
        for i in range(4):
            if i:
                for k in range(128):
                    while (i, k // 16) not in teidx:
                        next(nxt)
                    expert("u", i, k)
                    step()
            while i not in weighed:
                next(nxt)
            for k in range(128):
                expert("v", i, k)
                step()
            outt.append(dma(SP, O.rearrange("(a p) f -> p a f", p=128)[:, i, :], X[:, i, :], last_v[0]))
        finish(nc, ctx, PE, V, S, G, SP, sems)


def finish(nc, ctx, PE, V, S, G, SP, sems):
    block = ctx.enter_context(nc.Block())

    @block.tensor
    def _(e):
        PE.emit(e)

    @block.vector
    def _(e):
        V.emit(e)

    @block.scalar
    def _(e):
        S.emit(e)

    @block.gpsimd
    def _(e):
        G.emit(e)

    @block.sync
    def _(e):
        SP.emit(e)
        for sm, val in sems.values():
            e.wait_ge(sm, val)


def constants():
    c = np.zeros((128, C_END), np.float32)
    p = np.arange(128)
    c[:, 0:128] = np.eye(128)
    same = (p[:, None] // 64) == (p[None, :] // 64)
    c[:, C_ONES:C_ONES + 128] = same
    t = np.arange(64)
    for n in range(4):
        c[:, C_M4 + 64 * n:C_M4 + 64 * n + 64] = ((p % 64)[:, None] <= t) if n % 2 else ((p % 64)[:, None] < t)
    for n in range(6):
        b = 2 ** n
        big = (p[:, None] // (2 * b)) == (p[None, :] // (2 * b))
        c[:, C_LVL + 128 * n:C_LVL + 128 * n + 128] = big & ((p[:, None] // b) % 2 == 0) & ((p[None, :] // b) % 2 == 1)
    c[:, C_SCAN:C_SCAN + 512] = (np.arange(512) % 64 != 0)[None, :]
    c[:, C_BD:C_BD + 128] = same
    c[:, C_IOTA:C_IOTA + 512] = np.arange(512)[None, :]
    c[:, C_WM:C_WM + 128] = (p[:, None] // 64) <= (p[None, :] // 64)
    e = np.arange(16)
    c[0:16, C_EM:C_EM + 128] = (e[:, None] % 2) == (p[None, :] // 64)
    c[0:16, C_ES:C_ES + 8] = (e[:, None] // 2) == np.arange(8)[None, :]
    return c


def tiles(w):
    k, n = w.shape
    return w.reshape(k // 128, 128, n // 256, 256).transpose(2, 1, 0, 3).reshape(n // 256, 128, (k // 128) * 256)


def layouts(a):
    f = {k: np.asarray(v) for k, v in a.items()}
    w = f["w_in"][0]
    ch = [w[:, 128 * c:128 * c + 128] for c in range(46)]
    order = list(range(9, 20)) + list(range(0, 9)) + [20, 21]
    gates = []
    br = np.concatenate([f["w_branch_na"][0], f["w_branch_rw"][0], f["w_branch_mem"][0]], 0)
    order += [22 + 8 * b + 2 * f2 + a for f2 in range(4) for b in range(3) for a in range(2)]
    parts = [tiles(np.concatenate([ch[c] for c in order], 1)), tiles(f["w_mem_kv"][0]), tiles(br)]
    parts += [tiles(f["w_out"][0]), tiles(np.concatenate([f["w_in_2"][0][:, 512:1024], f["w_in_2"][0][:, 0:512], f["w_in_2"][0][:, 1024:]], 1)), tiles(f["w_out_2"][0]), tiles(f["peer_w_query_2"][0])]
    wt = np.concatenate(parts, 0)

    def col(v, n):
        return v.reshape(n, 128).T
    cols = [col(f["norm_mix_g"][0], 8), col(f["norm_mem_g"][0], 8), col(f["norm_ffn_g"][0], 8), col(f["ln_mix_g_2"][0], 8),
            col(f["ln_ffn_g_2"][0], 8), col(f["rw_mu_rkv"][0].reshape(-1), 18),
            np.concatenate([f["rw_mu_w"][0].T, f["rw_mu_a"][0].T], 0),
            col(f["rw_w0"][0].reshape(-1), 6), col(f["rw_a0"][0].reshape(-1), 6), col(f["rw_k_k"][0], 3), col(f["rw_k_a"][0], 3),
            col(f["rw_r_k"][0].reshape(-1), 3), col(f["rw_ln_g"][0], 3), col(f["rw_ln_b"][0], 3),
            np.concatenate([f["q_norm_g_2"][0]] * 2)[:, None], np.concatenate([f["k_norm_g_2"][0]] * 2)[:, None]]
    cols = np.concatenate(cols, 1)
    low = np.full((1,), -1e30, np.float32)
    c = np.arange(64)
    start = np.clip(c - 8, 0, 48)
    inside = (c[None, :] >= start[:, None]) & (c[None, :] < start[:, None] + 16)
    j = c[None, :] - c[:, None] + 15
    nab = np.zeros((128, 6, 16, 64), np.float32)
    for h in range(6):
        flat_ = np.concatenate([f["na_rpb"][0, h].reshape(-1), low])
        for dr in range(15):
            v = flat_[np.where(inside, dr * 31 + np.clip(j, 0, 30), 15 * 31)]
            nab[0:64, h, dr, :] = v
            nab[64:128, h, dr + 1, :] = v
    p = np.arange(128)[:, None]
    x = np.arange(512)[None, :] - 384
    ok = np.floor_divide(x, 64) <= p // 64
    idx = np.where(ok, np.clip(p - x, -128, 128) + 128, 257)
    abias = np.stack([np.concatenate([f["rel_bias_2"][0, h], low])[idx] for h in range(8)], 1)
    return {
        "x": f["x"][0], "mem": f["mem"][0], "wt": wt, "cols": cols, "consts": constants(),
        "w2a2": np.concatenate([f["rw_w2"][0].transpose(1, 0, 2).reshape(64, 768), f["rw_a2"][0].transpose(1, 0, 2).reshape(64, 768)], 0),
        "g2": f["rw_g2"][0], "nab": nab.reshape(128, 6144), "abias": abias.reshape(128, 4096),
        "rt": f["w_router"][0].reshape(8, 128, 16).transpose(1, 0, 2).reshape(128, 128),
        "eg": f["w_exp_gate"][0], "eu": f["w_exp_up"][0], "ed": f["w_exp_down"][0],
        "rows": np.concatenate([np.broadcast_to(v[None, :], (128, v.shape[0])) for v in
                                (f["norm_final_g"], f["ln_ffn_g_2"][0], f["gmlp_norm_g_2"][0])], 1),
        "wsT": f["gmlp_w_s_2"][0].transpose(2, 0, 1).reshape(128, 1024), "bsT": f["gmlp_b_s_2"][0].T,
        "skT": f["peer_sub_keys_2"][0].reshape(16, 128, 128).transpose(2, 0, 1).reshape(128, 2048),
        "peer_u": f["peer_u_2"][0], "peer_v": f["peer_v_2"][0],
    }


def kernel(**inputs):
    import concourse.bacc as bacc
    from concourse.bass_utils import run_bass_kernel_spmd

    nc = bacc.Bacc("TRN2", target_bir_lowering=False, num_devices=1)
    arrays = {k: np.ascontiguousarray(v) for k, v in layouts(inputs).items()}
    I = {k: nc.dram_tensor("in_" + k, v.shape, mybir.dt.from_np(v.dtype), kind="ExternalInput").ap() for k, v in arrays.items()}
    O = nc.dram_tensor("out_0", (512, 1024), mybir.dt.float32, kind="ExternalOutput").ap()
    block_program(nc, I, O)
    r = run_bass_kernel_spmd(nc, [{"in_" + k: v for k, v in arrays.items()}], core_ids=[0])
    return r.results[0]["out_0"].reshape(1, 512, 1024)
```
